# Optimizing a Trainium2 kernel written in Bass

```python
import math
import jax, jax.numpy as jnp
from jax import lax
import numpy as np

D_MODEL = 1024
BATCH = 1
SEQ = 512
DEPTH = 1

QBLOCK = 128
NEG_INF = -1e30
FORCE_SCORE = 1e9
RMS_EPS = 1e-6

A_HEADS = 4
A_HEAD_DIM = 64
A_WIDTH = A_HEADS * A_HEAD_DIM
A_KV_LATENT = 128
IDX_HEADS = 8
IDX_DIM = 64
TOPK_MAX = 256

B_HEADS = 4
B_HEAD_DIM = 128
B_WIDTH = B_HEADS * B_HEAD_DIM
CONV_WIDTH = 4
GDN_CHUNK = 64

C_HEADS = 4
C_HEAD_DIM = 64
C_WIDTH = C_HEADS * C_HEAD_DIM
CMP_BLOCK = 32
CMP_STRIDE = 16
SEL_BLOCK = 64
N_SEL = 16
WINDOW = 512
PHI_HIDDEN = 256

N_BUCKETS = 32
BUCKET_MAX_EXACT = 16
BUCKET_MAX_DIST = 128

N_BRANCH = 3
W_MIX = A_WIDTH + B_WIDTH + C_WIDTH

A_COLS = (A_WIDTH, A_KV_LATENT, IDX_HEADS * IDX_DIM, IDX_DIM, IDX_HEADS, A_WIDTH)
B_COLS = (3 * B_WIDTH, B_HEADS, B_HEADS, B_WIDTH)
C_COLS = (C_WIDTH, 6 * C_HEAD_DIM, 3 * C_HEADS, C_WIDTH)
G_COLS = (N_BRANCH * D_MODEL,)
N_IN = sum(A_COLS) + sum(B_COLS) + sum(C_COLS) + sum(G_COLS)

kernel_name = 'hybrid_dsa_gdn_nsa_trunk'

def split_cols(a, sizes):
    idx = np.cumsum(sizes)[:-1].tolist()
    return jnp.split(a, idx, axis=-1)

def split_heads(t, n, d):
    return t.reshape(*t.shape[:-1], n, d)

def rms_norm(x, g):
    x32 = x.astype(jnp.float32)
    y = x32 * lax.rsqrt(jnp.mean(x32 * x32, axis=-1, keepdims=True) + RMS_EPS)
    return (y * g.astype(jnp.float32)).astype(x.dtype)

def l2norm(x):
    x32 = x.astype(jnp.float32)
    return x32 * lax.rsqrt(jnp.sum(x32 * x32, axis=-1, keepdims=True) + RMS_EPS)

def masked_softmax(logits, mask):
    logits = jnp.where(mask, logits.astype(jnp.float32), NEG_INF)
    return jnp.where(mask, jax.nn.softmax(logits, axis=-1), 0.0)

def t5_bucket(dist):
    dist = jnp.maximum(dist, 0)
    log_ratio = jnp.log(jnp.maximum(dist, 1).astype(jnp.float32) / BUCKET_MAX_EXACT) / math.log(BUCKET_MAX_DIST / BUCKET_MAX_EXACT)
    large = BUCKET_MAX_EXACT + (log_ratio * (N_BUCKETS - BUCKET_MAX_EXACT)).astype(jnp.int32)
    large = jnp.minimum(large, N_BUCKETS - 1)
    return jnp.where(dist < BUCKET_MAX_EXACT, dist, large)

def to_qblocks(a):
    b, s = a.shape[:2]
    return jnp.moveaxis(a.reshape(b, s // QBLOCK, QBLOCK, *a.shape[2:]), 1, 0)

def from_qblocks(a):
    nb, b = a.shape[:2]
    return jnp.moveaxis(a, 0, 1).reshape(b, nb * QBLOCK, *a.shape[3:])

def dsa_mixer(q, k, v, q_idx, k_idx, w_idx, bias_tab):
    b, s = q.shape[:2]
    topk = min(TOPK_MAX, s // 4)
    bidx = jnp.arange(b)[:, None, None]
    key_pos = jnp.arange(s)
    scale = A_HEAD_DIM ** -0.5

    def block(args):
        qb, qib, wb, start = args
        t = start + jnp.arange(QBLOCK)
        idx_logits = jnp.einsum('bqhd,bsd->bqhs', qib, k_idx) * (IDX_DIM ** -0.5)
        score = jnp.einsum('bqh,bqhs->bqs', wb * (IDX_HEADS ** -0.5), jax.nn.relu(idx_logits))
        score = jnp.where(key_pos[None, None, :] <= t[None, :, None], score.astype(jnp.float32), NEG_INF)
        _, sel = lax.top_k(score, topk)
        kg = k[bidx, sel]
        vg = v[bidx, sel]
        dist = t[None, :, None] - sel
        bias = jnp.transpose(bias_tab[t5_bucket(dist)], (0, 3, 1, 2))
        logits = jnp.einsum('bqhd,bqkhd->bhqk', qb, kg).astype(jnp.float32) * scale + bias.astype(jnp.float32)
        p = masked_softmax(logits, (dist >= 0)[:, None])
        return jnp.einsum('bhqk,bqkhd->bqhd', p.astype(vg.dtype), vg)

    starts = jnp.arange(s // QBLOCK, dtype=jnp.int32) * QBLOCK
    out = lax.map(block, (to_qblocks(q), to_qblocks(q_idx), to_qblocks(w_idx), starts))
    return from_qblocks(out)

def causal_depthwise_conv(x, w):
    c = x.shape[-1]
    return lax.conv_general_dilated(x, w.astype(x.dtype)[:, None, :], window_strides=(1,), padding=[(CONV_WIDTH - 1, 0)], dimension_numbers=('NWC', 'WIO', 'NWC'), feature_group_count=c)

def gated_deltanet_mixer(qkv, a_in, b_in, conv_w, a_log, dt_bias):
    b, s = qkv.shape[:2]
    n = s // GDN_CHUNK
    qkv = jax.nn.silu(causal_depthwise_conv(qkv, conv_w))
    q, k, v = jnp.split(qkv, 3, axis=-1)
    q = l2norm(split_heads(q, B_HEADS, B_HEAD_DIM)) * (B_HEAD_DIM ** -0.5)
    k = l2norm(split_heads(k, B_HEADS, B_HEAD_DIM))
    v = split_heads(v, B_HEADS, B_HEAD_DIM).astype(jnp.float32)
    beta = jax.nn.sigmoid(b_in.astype(jnp.float32))
    g = -jnp.exp(a_log.astype(jnp.float32)) * jax.nn.softplus(a_in.astype(jnp.float32) + dt_bias.astype(jnp.float32))

    def chunk(t):
        return jnp.moveaxis(t.reshape(b, n, GDN_CHUNK, *t.shape[2:]), 3, 2)

    q, k, v, beta, g = (chunk(t) for t in (q, k, v, beta, g))
    g_cum = jnp.cumsum(g, axis=-1)
    g_last = g_cum[..., -1]
    lower = jnp.tril(jnp.ones((GDN_CHUNK, GDN_CHUNK), dtype=bool))
    strict = jnp.tril(jnp.ones((GDN_CHUNK, GDN_CHUNK), dtype=bool), -1)
    diff = g_cum[..., :, None] - g_cum[..., None, :]
    decay = jnp.where(lower, jnp.exp(jnp.where(lower, diff, 0.0)), 0.0)
    k_beta = k * beta[..., None]
    a_mat = jnp.where(strict, jnp.einsum('bnhid,bnhjd->bnhij', k_beta, k) * decay, 0.0)
    eye = jnp.eye(GDN_CHUNK, dtype=jnp.float32)
    t_inv = lax.linalg.triangular_solve(eye + a_mat, jnp.broadcast_to(eye, a_mat.shape), left_side=True, lower=True)
    u = jnp.einsum('bnhij,bnhjd->bnhid', t_inv, v * beta[..., None])
    w = jnp.einsum('bnhij,bnhjd->bnhid', t_inv, k_beta * jnp.exp(g_cum)[..., None])
    attn = jnp.einsum('bnhid,bnhjd->bnhij', q, k) * decay
    q_dec = q * jnp.exp(g_cum)[..., None]
    k_dec = k * jnp.exp(g_last[..., None] - g_cum)[..., None]

    def step(state, xs):
        u_c, w_c, q_c, k_c, attn_c, gl_c = xs
        v_new = u_c - jnp.einsum('bhik,bhkv->bhiv', w_c, state)
        o = jnp.einsum('bhik,bhkv->bhiv', q_c, state) + jnp.einsum('bhij,bhjv->bhiv', attn_c, v_new)
        state = state * jnp.exp(gl_c)[..., None, None] + jnp.einsum('bhik,bhiv->bhkv', k_c, v_new)
        return state, o

    state0 = jnp.zeros((b, B_HEADS, B_HEAD_DIM, B_HEAD_DIM), jnp.float32)
    xs = tuple(jnp.moveaxis(t, 1, 0) for t in (u, w, q_dec, k_dec, attn, g_last))
    _, o = lax.scan(step, state0, xs)
    o = jnp.moveaxis(jnp.moveaxis(o, 0, 1), 2, 3)
    return o.reshape(b, s, B_HEADS, B_HEAD_DIM)

def compress_blocks(tok, pos, w1, w2):
    b, s, d = tok.shape
    n_cmp = (s - CMP_BLOCK) // CMP_STRIDE + 1
    idx = jnp.arange(n_cmp)[:, None] * CMP_STRIDE + jnp.arange(CMP_BLOCK)[None, :]
    blocks = tok[:, idx] + pos
    return jax.nn.silu(blocks.reshape(b, n_cmp, CMP_BLOCK * d) @ w1) @ w2

def nsa_mixer(q, kv, gates, k_norm, cmp_pos, phi_w1, phi_w2, bias_tab):
    b, s = q.shape[:2]
    scale = C_HEAD_DIM ** -0.5
    t_all = jnp.arange(s)
    k_cmp, v_cmp, k_sel, v_sel, k_win, v_win = (kv[:, :, i] for i in range(6))
    k_sel = rms_norm(k_sel, k_norm[1])
    k_win = rms_norm(k_win, k_norm[2])

    kc = rms_norm(compress_blocks(k_cmp, cmp_pos[0], phi_w1[0], phi_w2[0]), k_norm[0])
    vc = compress_blocks(v_cmp, cmp_pos[1], phi_w1[1], phi_w2[1])
    n_cmp = kc.shape[1]
    cmp_start = jnp.arange(n_cmp) * CMP_STRIDE
    cmp_end = cmp_start + CMP_BLOCK - 1
    cmp_valid = cmp_end[None, :] <= t_all[:, None]
    cmp_bias = jnp.transpose(bias_tab[t5_bucket(t_all[:, None] - cmp_end[None, :])], (2, 0, 1))
    logits = jnp.einsum('bqhd,bnd->bhqn', q, kc).astype(jnp.float32) * scale + cmp_bias.astype(jnp.float32)
    p_cmp = masked_softmax(logits, cmp_valid[None, None])
    o_cmp = jnp.einsum('bhqn,bnd->bqhd', p_cmp.astype(vc.dtype), vc)

    n_sb = s // SEL_BLOCK
    n_pick = min(N_SEL, n_sb)
    sb_start = jnp.arange(n_sb) * SEL_BLOCK
    overlap = ((cmp_start[:, None] < sb_start[None, :] + SEL_BLOCK) & (cmp_start[:, None] + CMP_BLOCK > sb_start[None, :])).astype(jnp.float32)
    importance = jnp.einsum('bhqn,nj->bqj', p_cmp, overlap)
    cur = t_all // SEL_BLOCK
    blk = jnp.arange(n_sb)
    forced = (blk[None, :] == 0) | (blk[None, :] == cur[:, None]) | (blk[None, :] == jnp.maximum(cur[:, None] - 1, 0))
    admissible = sb_start[None, :] <= t_all[:, None]
    importance = jnp.where(admissible[None], jnp.where(forced[None], FORCE_SCORE, importance), NEG_INF)
    _, sel = lax.top_k(importance, n_pick)

    k_blocks = k_sel.reshape(b, n_sb, SEL_BLOCK, C_HEAD_DIM)
    v_blocks = v_sel.reshape(b, n_sb, SEL_BLOCK, C_HEAD_DIM)
    k_win_pad = jnp.pad(k_win, ((0, 0), (WINDOW, 0), (0, 0)))
    v_win_pad = jnp.pad(v_win, ((0, 0), (WINDOW, 0), (0, 0)))
    bidx = jnp.arange(b)[:, None, None]
    n_keys = n_pick * SEL_BLOCK

    def block(args):
        qb, selb, start = args
        t = start + jnp.arange(QBLOCK)
        kg = k_blocks[bidx, selb].reshape(b, QBLOCK, n_keys, C_HEAD_DIM)
        vg = v_blocks[bidx, selb].reshape(b, QBLOCK, n_keys, C_HEAD_DIM)
        s_pos = (selb[..., None] * SEL_BLOCK + jnp.arange(SEL_BLOCK)).reshape(b, QBLOCK, n_keys)
        dist = t[None, :, None] - s_pos
        bias = jnp.transpose(bias_tab[t5_bucket(dist)], (0, 3, 1, 2))
        lg = jnp.einsum('bqhd,bqkd->bhqk', qb, kg).astype(jnp.float32) * scale + bias.astype(jnp.float32)
        p = masked_softmax(lg, (dist >= 0)[:, None])
        o_sel = jnp.einsum('bhqk,bqkd->bqhd', p.astype(vg.dtype), vg)
        kw = lax.dynamic_slice_in_dim(k_win_pad, start, QBLOCK + WINDOW, axis=1)
        vw = lax.dynamic_slice_in_dim(v_win_pad, start, QBLOCK + WINDOW, axis=1)
        s_w = start - WINDOW + jnp.arange(QBLOCK + WINDOW)
        dist_w = t[:, None] - s_w[None, :]
        valid_w = (s_w[None, :] >= 0) & (dist_w >= 0) & (dist_w < WINDOW)
        bias_w = jnp.transpose(bias_tab[t5_bucket(dist_w)], (2, 0, 1))
        lw = jnp.einsum('bqhd,bsd->bhqs', qb, kw).astype(jnp.float32) * scale + bias_w.astype(jnp.float32)
        pw = masked_softmax(lw, valid_w[None, None])
        o_win = jnp.einsum('bhqs,bsd->bqhd', pw.astype(vw.dtype), vw)
        return o_sel, o_win

    starts = jnp.arange(s // QBLOCK, dtype=jnp.int32) * QBLOCK
    o_sel, o_win = lax.map(block, (to_qblocks(q), to_qblocks(sel), starts))
    o_sel = from_qblocks(o_sel)
    o_win = from_qblocks(o_win)
    g = jax.nn.sigmoid(gates.astype(jnp.float32)).reshape(b, s, C_HEADS, 3)
    out = g[..., 0:1] * o_cmp + g[..., 1:2] * o_sel + g[..., 2:3] * o_win
    return out.astype(q.dtype)

def setup_inputs(seed: int = 0) -> dict:
    key = jax.random.key(seed)
    ks = jax.random.split(key, 22)
    f32 = jnp.float32

    def nrm(k, shape, scale):
        return jax.random.normal(k, shape, f32) * scale

    def gain(k, shape):
        return 1.0 + 0.02 * jax.random.normal(k, shape, f32)

    x = nrm(ks[0], (BATCH, SEQ, D_MODEL), 1.0)
    norm_g = gain(ks[1], (DEPTH, D_MODEL))
    w_in = nrm(ks[2], (DEPTH, D_MODEL, N_IN), D_MODEL ** -0.5)
    a_kv_norm = gain(ks[3], (DEPTH, A_KV_LATENT))
    a_w_ukv = nrm(ks[4], (DEPTH, A_KV_LATENT, 2 * A_WIDTH), A_KV_LATENT ** -0.5)
    a_q_norm = gain(ks[5], (DEPTH, A_HEAD_DIM))
    a_k_norm = gain(ks[6], (DEPTH, A_HEAD_DIM))
    b_conv = nrm(ks[7], (DEPTH, CONV_WIDTH, 3 * B_WIDTH), CONV_WIDTH ** -0.5)
    b_a_log = jnp.log(jax.random.uniform(ks[8], (DEPTH, B_HEADS), f32, 1.0, 16.0))
    dt = jnp.exp(jax.random.uniform(ks[9], (DEPTH, B_HEADS), f32, math.log(1e-3), math.log(1e-1)))
    b_dt_bias = dt + jnp.log(-jnp.expm1(-dt))
    b_out_norm = gain(ks[10], (DEPTH, B_HEAD_DIM))
    c_q_norm = gain(ks[11], (DEPTH, C_HEAD_DIM))
    c_k_norm = gain(ks[12], (DEPTH, 3, C_HEAD_DIM))
    c_cmp_pos = nrm(ks[13], (DEPTH, 2, CMP_BLOCK, C_HEAD_DIM), 0.02)
    c_phi_w1 = nrm(ks[14], (DEPTH, 2, CMP_BLOCK * C_HEAD_DIM, PHI_HIDDEN), (CMP_BLOCK * C_HEAD_DIM) ** -0.5)
    c_phi_w2 = nrm(ks[15], (DEPTH, 2, PHI_HIDDEN, C_HEAD_DIM), PHI_HIDDEN ** -0.5)
    w_branch = jnp.concatenate([nrm(ks[16], (DEPTH, A_WIDTH, D_MODEL), A_WIDTH ** -0.5), nrm(ks[17], (DEPTH, B_WIDTH, D_MODEL), B_WIDTH ** -0.5), nrm(ks[18], (DEPTH, C_WIDTH, D_MODEL), C_WIDTH ** -0.5)], axis=1)
    w_out = nrm(ks[19], (DEPTH, D_MODEL, D_MODEL), D_MODEL ** -0.5)
    rel_bias = nrm(ks[20], (N_BUCKETS, A_HEADS + C_HEADS), 0.2)
    return {'x': x, 'norm_g': norm_g, 'w_in': w_in, 'a_kv_norm': a_kv_norm, 'a_w_ukv': a_w_ukv, 'a_q_norm': a_q_norm, 'a_k_norm': a_k_norm, 'b_conv': b_conv, 'b_a_log': b_a_log, 'b_dt_bias': b_dt_bias, 'b_out_norm': b_out_norm, 'c_q_norm': c_q_norm, 'c_k_norm': c_k_norm, 'c_cmp_pos': c_cmp_pos, 'c_phi_w1': c_phi_w1, 'c_phi_w2': c_phi_w2, 'w_branch': w_branch, 'w_out': w_out, 'rel_bias': rel_bias}

def reference(x, norm_g, w_in, a_kv_norm, a_w_ukv, a_q_norm, a_k_norm, b_conv, b_a_log, b_dt_bias, b_out_norm, c_q_norm, c_k_norm, c_cmp_pos, c_phi_w1, c_phi_w2, w_branch, w_out, rel_bias):
    b, s, _ = x.shape
    bias_a = rel_bias[:, :A_HEADS]
    bias_c = rel_bias[:, A_HEADS:]
    for l in range(DEPTH):
        h = rms_norm(x, norm_g[l])
        proj = h @ w_in[l]
        a_part, b_part, c_part, gate_part = split_cols(proj, (sum(A_COLS), sum(B_COLS), sum(C_COLS), sum(G_COLS)))

        a_q, a_ckv, a_qi, a_ki, a_wi, a_z = split_cols(a_part, A_COLS)
        a_k, a_v = jnp.split(rms_norm(a_ckv, a_kv_norm[l]) @ a_w_ukv[l], 2, axis=-1)
        a_q = rms_norm(split_heads(a_q, A_HEADS, A_HEAD_DIM), a_q_norm[l])
        a_k = rms_norm(split_heads(a_k, A_HEADS, A_HEAD_DIM), a_k_norm[l])
        a_v = split_heads(a_v, A_HEADS, A_HEAD_DIM)
        o_a = dsa_mixer(a_q, a_k, a_v, split_heads(a_qi, IDX_HEADS, IDX_DIM), a_ki, a_wi, bias_a)
        y_a = o_a.reshape(b, s, A_WIDTH) * jax.nn.silu(a_z)

        b_qkv, b_a, b_b, b_z = split_cols(b_part, B_COLS)
        o_b = gated_deltanet_mixer(b_qkv, b_a, b_b, b_conv[l], b_a_log[l], b_dt_bias[l])
        y_b = rms_norm(o_b, b_out_norm[l]).reshape(b, s, B_WIDTH).astype(x.dtype) * jax.nn.silu(b_z)

        c_q, c_kv, c_g, c_z = split_cols(c_part, C_COLS)
        c_q = rms_norm(split_heads(c_q, C_HEADS, C_HEAD_DIM), c_q_norm[l])
        o_c = nsa_mixer(c_q, split_heads(c_kv, 6, C_HEAD_DIM), c_g, c_k_norm[l], c_cmp_pos[l], c_phi_w1[l], c_phi_w2[l], bias_c)
        y_c = o_c.reshape(b, s, C_WIDTH) * jax.nn.silu(c_z)

        wb = w_branch[l]
        g_a, g_b, g_c = jnp.split(jax.nn.sigmoid(gate_part), 3, axis=-1)
        merged = g_a * (y_a @ wb[:A_WIDTH]) + g_b * (y_b @ wb[A_WIDTH:A_WIDTH + B_WIDTH]) + g_c * (y_c @ wb[A_WIDTH + B_WIDTH:])
        x = x + (merged @ w_out[l]).astype(x.dtype)
    return x


_drawn_inputs = setup_inputs


def setup_inputs(seed=0):
    import zlib

    import numpy as np

    out = dict(_drawn_inputs(seed))
    spreads = {}
    factors = {'norm_g': 4.231,
     'a_kv_norm': 8.0,
     'a_q_norm': 8.0,
     'a_k_norm': 8.0,
     'b_out_norm': 29.613,
     'c_q_norm': 27.811,
     'c_k_norm': 28.909,
     'c_cmp_pos': 89.003,
     'rel_bias': 4.985}
    for name, (base, spread) in spreads.items():
        noise = np.random.default_rng([zlib.crc32(name.encode()), seed]).standard_normal(out[name].shape)
        drawn = base * np.exp(spread * noise) if base else spread * noise
        out[name] = __import__('jax').numpy.asarray(drawn.astype(out[name].dtype))
    for name, factor in factors.items():
        out[name] = (out[name] * factor).astype(out[name].dtype)
    return out
```

```python
import math
from contextlib import ExitStack

import numpy as np
import concourse.bass as bass
from concourse import mybir

P = 128
T, D = 512, 1024
NT, KC = T // P, D // P
EPS = 1e-6
NEG = -1e30
TAKEN = -3e38

A_HEADS, A_HD = 4, 64
IDX_HEADS = 8
TOPK = min(256, T // 4)
B_HEADS, B_HD = 4, 128
C_HEADS, C_HD = 4, 64
CMP_BLOCK, CMP_STRIDE, N_CMP = 32, 16, (T - 32) // 16 + 1
PHI = 256
N_BUCKETS, EXACT, MAX_DIST = 32, 16, 128
N_HEADS = A_HEADS + C_HEADS

A_Q, A_CKV, A_QI, A_KI = 0, 256, 384, 896
B_BASE = 1224
B_AB = B_BASE + 1536
C_BASE = B_AB + 8 + 512
C_VSEL = C_BASE + 256 + 192
G_BASE = 4188

CHUNKS = [
    ("w_in", A_Q, 384), ("w_in", A_QI, 512), ("w_in", A_KI, 328),
    ("w_in", B_BASE, 512), ("w_in", B_BASE + 512, 512), ("w_in", B_BASE + 1024, 512),
    ("w_in", B_AB, 260), ("w_in", B_AB + 260, 260),
    ("w_in", C_BASE, 448), ("w_in", C_VSEL, 460),
    ("phi", 0, PHI), ("phi", 1, PHI),
    ("w_in", G_BASE, 512), ("w_in", G_BASE + D, 512), ("w_in", G_BASE + 2 * D, 512),
    ("w_branch", 0, 512),
    ("w_in", G_BASE + 512, 512), ("w_in", G_BASE + D + 512, 512), ("w_in", G_BASE + 2 * D + 512, 512),
    ("w_branch", 512, 512), ("w_out", 0, 512), ("w_out", 512, 512),
]
(CH_A0, CH_QI, CH_A2, CH_B0, CH_B1, CH_B2, CH_B3, CH_B4, CH_C0, CH_C1, CH_PK, CH_PV,
 CH_G0, CH_G1, CH_G2, CH_WB0, CH_G3, CH_G4, CH_G5, CH_WB1, CH_WO0, CH_WO1) = range(22)

R_NORM, R_CONV, R_CKV, R_AQ, R_AK, R_CQ, R_CK, R_BOUT, R_POS, N_ROWS = 0, 8, 56, 57, 58, 59, 60, 63, 64, 96
F_IDENT, F_TRI, F_SEEN, F_HOT, N_FLOAT = 0, 128, 256, 260, 260 + 640
LEVELS = 7
S_REL = 640


def shape_constants():
    f = np.zeros((P, N_FLOAT), np.float32)
    i = np.arange(P)
    f[:, F_IDENT:F_IDENT + P] = np.eye(P)
    f[:, F_TRI:F_TRI + P] = i[:, None] <= i[None, :]
    f[:, F_SEEN] = i >= CMP_BLOCK - 1
    f[:, F_SEEN + 1:F_SEEN + 4] = 1.0
    dist = T - 1 - np.arange(S_REL)
    ratio = np.log(np.maximum(dist, 1).astype(np.float32) / EXACT) / math.log(MAX_DIST / EXACT)
    large = np.minimum(EXACT + (ratio * (N_BUCKETS - EXACT)).astype(np.int32), N_BUCKETS - 1)
    bucket = np.where(dist < 0, N_BUCKETS, np.where(dist < EXACT, dist, large))
    f[0:N_BUCKETS + 1, F_HOT:F_HOT + S_REL] = bucket[None, :] == np.arange(N_BUCKETS + 1)[:, None]
    m = np.zeros((P, 2 * LEVELS, P), np.float32)
    for n in range(LEVELS):
        b = 1 << n
        same = i[:, None] // (2 * b) == i[None, :] // (2 * b)
        low = same & (i[:, None] // b % 2 == 1) & (i[None, :] // b % 2 == 0)
        m[:, n] = low
        m[:, LEVELS + n] = low.T
    return f, m


class Uses:

    def __init__(self, banks, names):
        self.banks = banks
        self.at = {n: i for i, n in enumerate(names)}
        assert len(self.at) == len(names)

    def bank(self, name):
        return self.banks[self.at[name] % len(self.banks)]

    def filled(self, name):
        return self.at[name] + 1

    def free(self, name):
        return self.at[name] + 1 - len(self.banks)


class Steps:

    def __init__(self, sem, names):
        self.sem = sem
        self.n = {n: i + 1 for i, n in enumerate(names)}
        assert len(self.n) == len(names)

    def wait(self, eng, name):
        eng.wait_ge(self.sem, self.n[name])


def trunk(nc, x, norm_g, w_in, a_kv_norm, a_w_ukv, a_q_norm, a_k_norm, b_conv, b_a_log, b_dt_bias, b_out_norm,
          c_q_norm, c_k_norm, c_cmp_pos, c_phi_w1, c_phi_w2, w_branch, w_out, rel_bias, floats, masks, out, rel_rows):
    f32 = mybir.dt.float32
    u8 = mybir.dt.uint8
    ALU = mybir.AluOpType
    ACT = mybir.ActivationFunctionType
    AX = mybir.AxisListType
    ctx = ExitStack()
    with ctx:
        def sb(name, shape, dt=f32):
            return ctx.enter_context(nc.sbuf_tensor(name, shape, dt))

        def sem(name):
            return ctx.enter_context(nc.semaphore(name))

        hT = sb("hT", [P, KC, T])
        ring = sb("ring", [P, 2, KC * 512])
        early = sb("early", [P, 6144])
        work = sb("work", [P, 6144])
        late = sb("late", [P, 4608])
        qkvT = sb("qkvT", [P, 12, T + 3])
        strips = sb("strips", [P, N_HEADS, T])
        cmp_strip = sb("cmp_strip", [P, C_HEADS, NT, N_CMP])
        raw_a2 = sb("raw_a2", [P, NT, 328])
        raw_b = sb("raw_b", [P, NT, 520])
        raw_c1 = sb("raw_c1", [P, NT, 460])
        v_a = sb("v_a", [P, NT, 256])
        qT_a = sb("qT_a", [P, 2, T])
        kT_a = sb("kT_a", [P, 2, T])
        qT_c = sb("qT_c", [P, 2, T])
        kT_sel = sb("kT_sel", [P, T])
        kT_win = sb("kT_win", [P, T])
        o_c = sb("o_c", [P, NT, 256])
        consts = sb("consts", [P, F_HOT])
        level_masks = sb("level_masks", [P, 2 * LEVELS, P], u8)
        ones = sb("ones", [P, P])
        par = sb("par", [P, N_ROWS])
        small = sb("small", [P, 600])
        kcT = sb("kcT", [P, N_CMP + 1])
        cmp_v = sb("cmp_v", [N_CMP, 64])
        g_scale = sb("g_scale", [P, 16, 12])

        ident = consts[:, F_IDENT:F_IDENT + P]
        tri = consts[:, F_TRI:F_TRI + P]
        seen = consts[:, F_SEEN:F_SEEN + 4]

        x_in = early[:, 0:4096].rearrange("p (t d) -> p t d", t=NT)
        hot = early[:, 4096:4096 + S_REL]
        rel_row = early[0:N_HEADS, 4096 + S_REL:4096 + 2 * S_REL]
        rel33 = early[0:N_BUCKETS + 1, 5376:5376 + N_HEADS]
        par_rows = early[0:N_ROWS, 5384:5384 + P]
        squares = early[:, 0:2048]
        conv_acc = early[:, 2048:3072].rearrange("p (b n) -> p b n", b=2)
        raw_c0 = early[:, 3072:4864].rearrange("p (t n) -> p t n", t=NT)
        blocks = early[:, 4864:5856].rearrange("p (v c n) -> p v c n", v=2, c=16)
        hidT = early[:, 5856:5980].rearrange("p (v n) -> p v n", v=4)
        gates = early[:, 0:6144].rearrange("p (g n) -> p g n", g=12)
        raw_a0 = work[:, 0:1536].rearrange("p (t n) -> p t n", t=NT)
        qiT = work[:, 1536:3072].rearrange("p (m n) -> p m n", m=4)
        ukv = work[:, 3072:3584]
        ckvT = work[:, 3584:4096]
        kiT = work[:, 4096:4608]
        mask_floats = work[:, 3584:3584 + 2 * LEVELS * P].rearrange("p (n m) -> p n m", m=P)
        phi2 = work[:, 5632:5888].rearrange("p (k n) -> p k n", k=4)
        k_raw = work[:, 4608:5632].rearrange("p (t n) -> p t n", t=NT)
        mergedT = work[:, 0:4096].rearrange("p (c n) -> p c n", c=KC)

        def slot(t, n):
            return t[:, 512 * n:512 * n + 512].rearrange("p (h n) -> p h n", h=4)

        (g_tri, decay, decay_k, neg_nT, t_inv, t_invT, z_sb, v_tok, k_tok, attnT, resid, v_new) = (
            slot(work, n) for n in range(12))
        o_state, o_tok, state, o_sq, decay_n, u_scr = (slot(late, n) for n in range(6))
        scores = [late[:, 0:256], late[:, 256:640], late[:, 640:1152]]
        topk_work = [late[:, 1152:1664], late[:, 1664:2176]]
        relu_buf = [late[:, 2176:2688], late[:, 2688:3200]]
        probs = [late[:, 512 * n:512 * n + 512] for n in range(2)]
        probsT = [late[:, 1024 + 512 * n:1536 + 512 * n] for n in range(2)]
        bias_sel = [late[:, 2048 + 512 * n:2560 + 512 * n] for n in range(2)]
        keep_add = [late[:, 3456:3712], late[:, 3712:4096], late[:, 4096:4608]]
        x_again = late[:, 0:4096].rearrange("p (t d) -> p t d", t=NT)
        yT = qkvT[:, :, :].rearrange("p a b -> p (a b)")[:, 0:4096].rearrange("p (c n) -> p c n", c=KC)
        cmp_p = work[:, 0:496]
        cmp_pT = work[0:N_CMP, 512:2560].rearrange("p (u n) -> p u n", u=16)

        col = [0]

        def cols(n):
            col[0] += n
            return small[:, col[0] - n:col[0]]

        banks = [ctx.enter_context(nc.psum_tensor(f"bank{n}", [P, 512], f32)) for n in range(8)]
        s_names = [(c, t) for c in ("A0", "QI", "A2", "B0") for t in range(4)]
        s_names += [("idx", q, h) for q in range(1, NT) for h in range(IDX_HEADS)]
        s_names += [(c, t) for c in ("B1", "B2", "B3", "B4", "C0", "C1") for t in range(4)]
        s_names += ["hid"] + [("gate", g) for g in range(12)] + [("cp", q) for q in range(4)]
        units = [(m, q, h) for m in "A" for q in range(NT) for h in range(4)]
        units += [(m, q, h) for q in range(NT) for m in ("sel", "win") for h in range(4)]
        groups = [u[:2] for u in units[::4]]
        s_names += [("pT", *u) for u in units] + [("gate", g) for g in range(12, 24)]
        S = Uses(banks[0:3], s_names)
        v_names = ["par"] + [("x", t, a) for t in range(NT) for a in range(2)] + ["rel0", "rel1"]
        v_names += ["ckvT", "qT0", "qT1"] + [("ukv", t) for t in range(NT)] + ["kT0", "kT1", "kiT"]
        v_names += ["cqT0", "cqT1", "kcmp", "vcmp", "ksT", "kwT", "cmpkv", "kcT", "sums"]
        for c in range(NT):
            v_names += [(n, c) for n in ("gc", "kt", "vt", "kk", "qk", "n")]
            for l in range(1, LEVELS):
                v_names += [("z", c, l), ("ut", c, l)] + ([("u", c, l)] if l < LEVELS - 1 else [])
            v_names += ([("ks", c)] if c else []) + [("x2", c), ("o", c)] + ([("st", c)] if c < NT - 1 else [])
        v_names += ["cl0", "cl1"] + [("lg", *u) for u in units]
        v_names += [("yT", f) for f in range(KC)]
        v_names += [("br", j, b) for j in range(KC) for b in range(3)] + [("wo", n, t) for n in range(2) for t in range(NT)]
        V = Uses(banks[3:6], v_names)
        O = Uses(banks[6:8], [("os", c) for c in range(1, NT)] + [("oc", n) for n in range(2)] + [("o", *g) for g in groups])

        s_filled, s_drained = sem("scalar_banks_filled"), sem("scalar_banks_drained")
        v_filled, v_drained = sem("vector_banks_filled"), sem("vector_banks_drained")
        o_filled, o_drained = sem("out_banks_filled"), sem("out_banks_drained")
        w_loaded = [sem(f"weights_loaded{n}") for n in range(2)]
        phi_used = sem("phi_weights_used")
        x_loaded = [sem(f"x_loaded{t}") for t in range(NT)]
        in_loaded = sem("parameters_loaded")
        const_loaded = sem("constants_loaded")
        ukv_loaded = sem("ukv_loaded")
        fills = sem("fills_done")
        hot_ready = sem("rel_table_ready")
        row_stored, strips_loaded, cmp_strip_ready = sem("rel_rows_stored"), sem("strips_loaded"), sem("cmp_strip_ready")
        x_reloaded, out_stored = sem("x_reloaded"), sem("out_stored")
        v_step, p_step, a_step = sem("vector_step"), sem("pool_step"), sem("scalar_step")
        roots = ["x0", "x1", "x2", "x3", "A0", "Ak", "C0", "C1", "kc", "B"] + [("ob", c) for c in range(NT)]
        ROOT_IN = Steps(sem("root_input_ready"), roots)
        ROOT_OUT = Steps(sem("root_ready"), roots)
        SQ = Steps(sem("squares_ready"), ["A0", "Ak", "C0", "C1"] + [("B", m) for m in range(8)] + [("ob", c) for c in range(NT)])
        ssx_ready, h_ready = sem("x_square_sums_ready"), sem("h_ready")
        rows_ready = sem("rel_rows_ready")
        conv_ready, conv_done = sem("conv_ready"), sem("conv_silu_done")
        T_IN = Steps(sem("transpose_input_ready"), ["A0ckv", "A0q", "Ak", "Aki", "C0q", "C0blk", "C0ks", "C1kw", "kc"])
        score_ready, diag_ready = sem("score_ready"), sem("diagonal_masked")
        relu_used = sem("relu_used")
        keep_ready = sem("keep_ready")
        GATE_IN = Steps(sem("decay_input_ready"), ["g", "gc2"])
        GATE_OUT = Steps(sem("decay_exp_ready"), ["beta", "expa", "sp", "exps"])
        z_ready, sums_taken, gsum_ready = sem("z_gates_ready"), sem("squares_summed"), sem("log_decay_ready")
        gtri_ready = sem("cumulative_input_ready")
        diff_ready, exp_ready, decays_ready = sem("decay_difference_ready"), sem("decay_ready"), sem("decays_masked")
        g_names = []
        for c in range(NT):
            g_names += [(n, c) for n in ("kt", "nnt", "attn", "tt0")]
            for l in range(1, LEVELS):
                g_names += [("z", c, l), ("tt", c, l)] + ([("t", c, l)] if l < LEVELS - 1 else [])
            g_names += [("resid", c), ("vnew", c), ("oraw", c)] + ([("state", c)] if c < NT - 1 else [])
        GD = Steps(sem("deltanet_ready"), g_names)
        eye_ready = sem("inverse_reset")
        o_scaled = sem("deltanet_output_scaled")
        y_b = sem("y_b_ready")
        cl_ready, cexp_ready = sem("cmp_logits_ready"), sem("cmp_exp_ready")
        logits_ready, probs_ready, pv_done = sem("logits_ready"), sem("probs_ready"), sem("probsT_used")
        bias_ready = sem("selected_bias_ready")
        o_norm, y_ready = sem("output_normalised"), sem("y_ready")
        merge_ready, merged_ready = sem("branch_gated"), sem("merged_ready")
        out_ready = sem("out_ready")

        ss_x, ss_a, ss_k = cols(4), cols(20), cols(16)
        ss_c, ss_w, ss_kc, ss_b, ss_o = cols(20), cols(4), cols(1), cols(32), cols(16)
        root = cols(32)
        newton = cols(32)
        max8 = cols(16)
        beta_t, g_t, sp_a, sp_b, neg_exp_a, dt_b = cols(16), cols(16), cols(16), cols(16), cols(4), cols(4)
        rq, rk, nk = cols(16), cols(16), cols(16)
        sums_sb = cols(64)
        mx, nmx, rsum, gsum = cols(48), cols(48), cols(48), cols(4)
        cmx, crs = cols(16), cols(16)
        fac = cols(4)
        (gc_, gl_, egc, negegc, egl, ekd, kd_s, n_s, a_s, rqs) = (g_scale[:, :, n] for n in range(10))
        assert col[0] <= 600, col[0]

        def bc(ap, n):
            return ap.unsqueeze(2).to_broadcast([ap.shape[0], ap.shape[1], n])

        def heads(ap, c):
            return bc(ap[:, 4 * c:4 * c + 4], P)

        def over_heads(ap):
            return ap.unsqueeze(1).to_broadcast([P, 4, P])

        chunk_end = {c: (s_filled, S.filled((n, 3))) for c, n in (
            (CH_A0, "A0"), (CH_QI, "QI"), (CH_A2, "A2"), (CH_B0, "B0"), (CH_B1, "B1"), (CH_B2, "B2"), (CH_B3, "B3"),
            (CH_B4, "B4"), (CH_C0, "C0"), (CH_C1, "C1"))}
        chunk_end.update({CH_PK: (phi_used, 1), CH_PV: (phi_used, 2), CH_WB0: (v_filled, V.filled(("br", 3, 2))),
                          CH_WB1: (v_filled, V.filled(("br", KC - 1, 2)))})
        chunk_end.update({c: (s_filled, S.filled(("gate", 4 * n + 3)))
                          for n, c in enumerate((CH_G0, CH_G1, CH_G2, CH_G3, CH_G4, CH_G5))})

        block = ctx.enter_context(nc.Block())

        @block.sync
        def _(sp):
            for t in range(NT):
                sp.dma_start(x_in[:, t, :], x[0, t * P:(t + 1) * P, :]).then_inc(x_loaded[t], 16)

            def load(c):
                src, c0, n = CHUNKS[c]
                if c >= 2:
                    sp.wait_ge(*chunk_end[c - 2])
                dst = ring[:, c % 2, 0:KC * n].rearrange("p (k n) -> p k n", k=KC)
                if src == "phi":
                    dst = ring[:, c % 2, :].rearrange("p (k n) -> p k n", k=16)
                    ap = c_phi_w1[0, c0].rearrange("(k p) n -> p k n", p=P)
                else:
                    ap = {"w_in": w_in, "w_branch": w_branch, "w_out": w_out}[src][0].rearrange(
                        "(k p) n -> p k n", p=P)[:, :, c0:c0 + n]
                sp.dma_start(dst, ap).then_inc(w_loaded[c % 2], 16)

            load(0)
            load(1)
            sp.wait_ge(rows_ready, 1)
            sp.dma_start(rel_rows[:, :, :], rel_row.unsqueeze(1).to_broadcast([N_HEADS, P, S_REL])).then_inc(row_stored, 16)
            sp.wait_ge(row_stored, 16)
            sp.dma_start(strips[:, :, :], bass.AP(rel_rows.tensor, P - 1, [[S_REL - 1, P], [P * S_REL, N_HEADS], [1, T]])).then_inc(strips_loaded, 16)
            for c in range(2, len(CHUNKS)):
                load(c)
            sp.wait_ge(y_ready, NT * 2)
            sp.dma_start(x_again, x[0].rearrange("(t p) d -> p t d", p=P)).then_inc(x_reloaded, 16)
            for n in range(2):
                for t in range(NT):
                    sp.wait_ge(out_ready, NT * n + t + 1)
                    sp.dma_start(out[0, t * P:(t + 1) * P, 512 * n:512 * n + 512],
                                 x_again[:, t, 512 * n:512 * n + 512]).then_inc(out_stored, 16)
            sp.wait_ge(out_stored, 16 * 2 * NT)

        @block.gpsimd
        def _(gp):
            step = [0]

            def hold(ins):
                step[0] += 1
                ins.then_inc(p_step, 1)
                gp.wait_ge(p_step, step[0])

            gp.memset(ones[:, :], 1.0).then_inc(fills, 1)
            gp.memset(qkvT[:, :, 0:3], 0.0).then_inc(fills, 1)
            gp.memset(cmp_strip[:, :, :, :], NEG).then_inc(fills, 1)
            gp.wait_ge(fills, 3)
            hold(gp.memset(early[N_BUCKETS:N_BUCKETS + 1, 5376:5376 + N_HEADS], NEG))
            gp.nop().then_inc(hot_ready, 1)
            gp.wait_ge(const_loaded, 16 * 7)
            hold(gp.tensor_copy(level_masks[:, :, :], mask_floats))

            gp.wait_ge(s_drained, S.filled(("A0", 3)))
            gp.tensor_tensor(squares[:, 0:1536], work[:, 0:1536], work[:, 0:1536], ALU.mult).then_inc(SQ.sem, 1)
            gp.wait_ge(strips_loaded, 16)
            gp.wait_ge(fills, 3)
            for q in range(NT):
                n = min(N_CMP, 7 + 8 * q)
                first = 415 - P * q
                ins = gp.tensor_copy(cmp_strip[:, :, q, 0:n], strips[:, A_HEADS:, first:first + 16 * (n - 1) + 1:16])
            ins.then_inc(cmp_strip_ready, 1)
            gp.wait_ge(v_drained, V.filled(("ukv", 3)))
            gp.wait_ge(ROOT_OUT.sem, ROOT_OUT.n["A0"])
            kf = work[:, 4608:5632]
            gp.tensor_tensor(squares[:, 0:1024], kf, kf, ALU.mult).then_inc(SQ.sem, 1)
            for q in range(1, NT):
                gp.wait_ge(score_ready, q)
                d = scores[q - 1][:, P * q:P * q + P]
                gp.affine_select(out=d, in_=d, compare_op=ALU.is_ge, fill=NEG, base=0, pattern=[[-1, P]],
                                 channel_multiplier=1).then_inc(diag_ready, 1)
            gp.wait_ge(s_drained, S.filled(("C0", 3)))
            sq_c = squares[:, 0:1280].rearrange("p (t g d) -> p t g d", t=NT, d=64)
            gp.tensor_tensor(sq_c[:, :, 0:4, :], raw_c0[:, :, 0:256].rearrange("p t (g d) -> p t g d", d=64),
                             raw_c0[:, :, 0:256].rearrange("p t (g d) -> p t g d", d=64), ALU.mult)
            gp.tensor_tensor(sq_c[:, :, 4, :], raw_c0[:, :, 384:448], raw_c0[:, :, 384:448], ALU.mult).then_inc(SQ.sem, 1)
            gp.wait_ge(s_drained, S.filled(("C1", 3)))
            sq_w = squares[:, 1280:1536].rearrange("p (t d) -> p t d", t=NT)
            gp.tensor_tensor(sq_w, raw_c1[:, :, 64:128], raw_c1[:, :, 64:128], ALU.mult).then_inc(SQ.sem, 1)
            for m in range(8):
                gp.wait_ge(conv_done, m + 1)
                if m == 0:
                    gp.wait_ge(v_filled, V.filled("kwT"))
                if m >= 4:
                    gp.wait_ge(sums_taken, m - 3)
                gp.tensor_tensor(squares[:, 512 * (m % 4):512 * (m % 4) + 512], qkvT[:, m, 3:T + 3], qkvT[:, m, 3:T + 3],
                                 ALU.mult).then_inc(SQ.sem, 1)
            for c in range(NT):
                if c == 0:
                    GATE_IN.wait(gp, "gc2")
                    gp.wait_ge(z_ready, 1)
                else:
                    gp.wait_ge(v_filled, V.filled(("gc", c - 1)))
                gp.tensor_tensor(g_tri, over_heads(tri), heads(g_t, c), ALU.mult).then_inc(gtri_ready, 1)
                if c > 0:
                    gp.wait_ge(v_filled, V.filled(("x2", c - 1)))
                    GD.wait(gp, ("tt", c - 1, LEVELS - 1))
                gp.tensor_copy(t_inv, over_heads(ident)).then_inc(eye_ready, 1)
                gp.tensor_copy(t_invT, over_heads(ident)).then_inc(eye_ready, 1)
                gp.wait_ge(exp_ready, c + 1)
                if c > 0:
                    gp.wait_ge(v_filled, V.filled(("o", c - 1)))
                hold(gp.tensor_tensor(decay_k, decay, over_heads(tri), ALU.mult))
                gp.tensor_tensor(decay_n, decay_k, heads(n_s, c), ALU.mult).then_inc(decays_ready, 1)
                gp.tensor_tensor(attnT, decay_k, heads(rk, c), ALU.mult).then_inc(decays_ready, 1)
                GD.wait(gp, ("oraw", c))
                hold(gp.tensor_tensor(o_tok, o_tok, heads(rqs, c), ALU.mult))
                gp.tensor_tensor(o_sq, o_tok, o_tok, ALU.mult).then_inc(SQ.sem, 1)
                gp.wait_ge(o_scaled, c + 1)
                zb = raw_b[:, c, 8:520].rearrange("p (h d) -> p h d", h=4)
                gp.tensor_tensor(zb, zb, o_tok, ALU.mult).then_inc(y_b, 1)
            n = 0
            for q in range(1, NT):
                for h in range(4):
                    if n >= 2:
                        gp.wait_ge(logits_ready, 4 + n - 1)
                    else:
                        gp.wait_ge(y_b, NT)
                        GD.wait(gp, ("oraw", NT - 1))
                    L = P * (q + 1)
                    gp.tensor_tensor(bias_sel[n % 2][:, 0:L], strips[:, h, T - L:T], keep_add[q - 1], ALU.add).then_inc(bias_ready, 1)
                    n += 1
            for g, (m, q) in enumerate(groups):
                if m == "A":
                    gp.wait_ge(o_norm, g + 1)
                    za = raw_a2[:, q, 72:328]
                    gp.tensor_tensor(za, za, o_c[:, q, :], ALU.mult).then_inc(y_ready, 1)
                elif m == "win":
                    gp.wait_ge(o_norm, g + 1)
                    zc = raw_c1[:, q, 204:460]
                    gp.tensor_tensor(zc, zc, o_c[:, q, :], ALU.mult).then_inc(y_ready, 1)
            for j in range(KC):
                gp.wait_ge(merge_ready, j + 1)
                a, b, c_ = (gates[:, (b * 4 + j % 4), :] for b in range(3))
                hold(gp.tensor_tensor(a, a, b, ALU.add))
                gp.tensor_tensor(mergedT[:, j, :], a, c_, ALU.add).then_inc(merged_ready, 1)

        @block.scalar
        def _(act):
            for src, dst in (
                (norm_g[0].rearrange("(k p) -> k p", p=P), par_rows[R_NORM:R_NORM + 8, :]),
                (b_conv[0].rearrange("w (m p) -> w m p", p=P)[0], par_rows[R_CONV:R_CONV + 12, :]),
                (b_conv[0].rearrange("w (m p) -> w m p", p=P)[1], par_rows[R_CONV + 12:R_CONV + 24, :]),
                (b_conv[0].rearrange("w (m p) -> w m p", p=P)[2], par_rows[R_CONV + 24:R_CONV + 36, :]),
                (b_conv[0].rearrange("w (m p) -> w m p", p=P)[3], par_rows[R_CONV + 36:R_CONV + 48, :]),
                (a_kv_norm, par_rows[R_CKV:R_CKV + 1, :]),
                (a_q_norm, par_rows[R_AQ:R_AQ + 1, 0:64]), (a_q_norm, par_rows[R_AQ:R_AQ + 1, 64:128]),
                (a_k_norm, par_rows[R_AK:R_AK + 1, 0:64]), (a_k_norm, par_rows[R_AK:R_AK + 1, 64:128]),
                (c_q_norm, par_rows[R_CQ:R_CQ + 1, 0:64]), (c_q_norm, par_rows[R_CQ:R_CQ + 1, 64:128]),
                (c_k_norm[0], par_rows[R_CK:R_CK + 3, 0:64]), (c_k_norm[0], par_rows[R_CK:R_CK + 3, 64:128]),
                (b_out_norm, par_rows[R_BOUT:R_BOUT + 1, :]),
                (c_cmp_pos[0].rearrange("v (c a) d -> (v c) (a d)", a=2), par_rows[R_POS:R_POS + 32, :]),
            ):
                act.dma_start(dst, src).then_inc(in_loaded, 16)
            for src, dst in (
                (floats[:, 0:F_HOT], consts[:, :]), (floats[:, F_HOT:N_FLOAT], hot), (masks, mask_floats),
                (rel_bias, rel33[0:N_BUCKETS, :]),
                (b_dt_bias.to_broadcast([P, 4]), dt_b), (b_a_log.to_broadcast([P, 4]), neg_exp_a),
                (c_phi_w2[0].rearrange("v (k p) n -> p (v k) n", p=P), phi2),
            ):
                act.dma_start(dst, src).then_inc(const_loaded, 16)
            act.dma_start(ukv, a_w_ukv[0]).then_inc(ukv_loaded, 16)
            step = [0]

            def hold(ins):
                step[0] += 1
                ins.then_inc(a_step, 1)
                act.wait_ge(a_step, step[0])

            def sqrt(name, src, n):
                ROOT_IN.wait(act, name)
                nc.scalar.activation(root[0:src.shape[0], 0:n], src, ACT.Sqrt).then_inc(ROOT_OUT.sem, 1)

            def drain(name, dst, n=512, func=ACT.Copy, rows=P):
                act.wait_ge(s_filled, S.filled(name))
                nc.scalar.activation(dst, S.bank(name)[0:rows, 0:n], func).then_inc(s_drained, 1)

            for t in range(NT):
                act.wait_ge(x_loaded[t], 16)
                nc.scalar.activation(late[:, D * t:D * t + D], x_in[:, t, :], ACT.Square, accum_out=ss_x[:, t:t + 1]).then_inc(ssx_ready, 1)
            for t in range(NT):
                sqrt(f"x{t}", ss_x[:, t:t + 1], 1)
            for t in range(NT):
                drain(("A0", t), raw_a0[:, t, :], 384)
            sqrt("A0", ss_a, 20)
            for t in range(NT):
                drain(("QI", t), qiT[:, t, :], 384)
            for t in range(NT):
                drain(("A2", t), raw_a2[:, t, :], 328)
            sqrt("Ak", ss_k, 16)
            for t in range(NT):
                drain(("B0", t), qkvT[:, t, 3:T + 3])
            n = 0
            for q in range(1, NT):
                for h in range(IDX_HEADS):
                    if n >= 2:
                        act.wait_ge(relu_used, n - 1)
                    L = P * (q + 1)
                    drain(("idx", q, h), relu_buf[n % 2][:, 0:L], L, ACT.Relu)
                    n += 1

            def silu_conv(m):
                act.wait_ge(conv_ready, m + 1)
                nc.scalar.activation(qkvT[:, m, 3:T + 3], conv_acc[:, m % 2, :], ACT.Silu).then_inc(conv_done, 1)

            m = 0
            for k, name in enumerate(("B1", "B2", "B3", "B4", "C0", "C1")):
                if k == 4:
                    act.wait_ge(row_stored, 16)
                for t in range(NT):
                    if k >= 4:
                        for _ in range(2 if k == 4 else 1):
                            silu_conv(m)
                            m += 1
                    if k < 2:
                        drain((name, t), qkvT[:, 4 + 4 * k + t, 3:T + 3])
                    elif k < 4:
                        drain((name, t), raw_b[:, t, 260 * (k - 2):260 * (k - 2) + 260], 260)
                    elif k == 4:
                        drain((name, t), raw_c0[:, t, :], 448)
                    else:
                        drain((name, t), raw_c1[:, t, :], 460)
            sqrt("C0", ss_c, 20)
            sqrt("C1", ss_w, 4)
            act.wait_ge(s_drained, S.filled(("C1", 3)))
            nc.scalar.activation(raw_a2[:, :, 72:328], raw_a2[:, :, 72:328], ACT.Silu)
            nc.scalar.activation(raw_b[:, :, 8:520], raw_b[:, :, 8:520], ACT.Silu)
            nc.scalar.activation(raw_c1[:, :, 204:460], raw_c1[:, :, 204:460], ACT.Silu).then_inc(z_ready, 1)
            act.wait_ge(s_filled, S.filled("hid"))
            nc.scalar.activation(early[:, 5856:5980], S.bank("hid")[:, 0:124], ACT.Silu).then_inc(s_drained, 1)
            sqrt("kc", ss_kc[0:N_CMP, :], 1)
            nc.scalar.activation(raw_c1[:, :, 192:204], raw_c1[:, :, 192:204], ACT.Sigmoid)
            nc.scalar.activation(beta_t.rearrange("p (c h) -> p c h", c=NT), raw_b[:, :, 4:8], ACT.Sigmoid).then_inc(GATE_OUT.sem, 1)
            act.wait_ge(const_loaded, 16 * 7)
            nc.scalar.activation(neg_exp_a, neg_exp_a, ACT.Exp).then_inc(GATE_OUT.sem, 1)
            GATE_IN.wait(act, "g")
            hold(nc.scalar.activation(sp_b, sp_b, ACT.Exp, scale=-1.0))
            nc.scalar.activation(sp_b, sp_b, ACT.Ln, bias=1.0).then_inc(GATE_OUT.sem, 1)
            sqrt("B", ss_b, 32)
            GATE_IN.wait(act, "gc2")
            nc.scalar.activation(egc, gc_, ACT.Exp)
            nc.scalar.activation(egl, gl_, ACT.Exp)
            nc.scalar.activation(ekd, kd_s, ACT.Exp).then_inc(GATE_OUT.sem, 1)

            for c in range(NT):
                act.wait_ge(diff_ready, c + 1)
                hold(nc.scalar.activation(decay, decay, ACT.Relu, scale=-1.0))
                nc.scalar.activation(decay, decay, ACT.Exp, scale=-1.0).then_inc(exp_ready, 1)
                for g in range(3 * c, 3 * c + 3):
                    if g == 0:
                        act.wait_ge(v_filled, V.filled("sums"))
                    drain(("gate", g), gates[:, g, :], func=ACT.Sigmoid)
                if c > 0:
                    act.wait_ge(o_filled, O.filled(("os", c)))
                    if c > 1:
                        GD.wait(act, ("oraw", c - 1))
                    for h in range(4):
                        ins = nc.scalar.activation(o_state[:, h, :], O.bank(("os", c))[:, h * P:(h + 1) * P], ACT.Copy,
                                                   scale=egc[:, 4 * c + h:4 * c + h + 1])
                    ins.then_inc(o_drained, 1)
                sqrt(("ob", c), ss_o[:, 4 * c:4 * c + 4], 4)
            act.wait_ge(cl_ready, 1)
            nc.scalar.activation(cmp_p, cmp_p, ACT.Exp).then_inc(cexp_ready, 1)
            for q in range(NT):
                drain(("cp", q), cmp_pT[:, 4 * q:4 * q + 4, :].rearrange("p a b -> p (a b)"), rows=N_CMP)

            def exps(u):
                m, q, h = units[u]
                L = P * (q + 1)
                act.wait_ge(logits_ready, u + 1)
                nc.scalar.activation(probs[u % 2][:, 0:L], probs[u % 2][:, 0:L], ACT.Exp, bias=nmx[:, u:u + 1],
                                     accum_out=rsum[:, u:u + 1]).then_inc(probs_ready, 1)

            exps(0)
            for u, (m, q, h) in enumerate(units):
                if u + 1 < len(units):
                    exps(u + 1)
                L = P * (q + 1)
                if u >= 2:
                    act.wait_ge(pv_done, u - 1)
                drain(("pT", m, q, h), probsT[u % 2][:, 0:L], L)
            for g in range(12, 24):
                b, j = (g - 12) // 4, (g - 12) % 4
                act.wait_ge(merged_ready, 4)
                drain(("gate", g), gates[:, 4 * b + j, :], func=ACT.Sigmoid)

        @block.vector
        def _(ve):
            step = [0]
            count = {}

            def hold(ins):
                step[0] += 1
                ins.then_inc(v_step, 1)
                ve.wait_ge(v_step, step[0])

            def filled(name):
                ve.wait_ge(v_filled, V.filled(name))
                return V.bank(name)

            def inv_root(name, ss, n, inv_n, hold_last=True):
                rows = ss.shape[0]
                ve.tensor_scalar(ss, ss, inv_n, EPS, ALU.mult, ALU.add).then_inc(ROOT_IN.sem, 1)
                ROOT_OUT.wait(ve, name)
                y, w = root[0:rows, 0:n], newton[0:rows, 0:n]
                hold(ve.reciprocal(y, y))
                hold(ve.tensor_tensor(w, y, y, ALU.mult))
                hold(ve.tensor_tensor(w, w, ss, ALU.mult))
                hold(ve.tensor_scalar(w, w, -0.5, 1.5, ALU.mult, ALU.add))
                return y, w

            filled_par = filled("par")
            ve.tensor_copy(par[:, :], filled_par[:, 0:N_ROWS]).then_inc(v_drained, 1)
            ve.wait_ge(v_drained, 1)
            for t in range(NT):
                ve.wait_ge(ssx_ready, t + 1)
                s = ss_x[:, t:t + 1]
                y, w = inv_root(f"x{t}", s, 1, 1.0 / D)
                hold(ve.tensor_tensor(s, y, w, ALU.mult))
                ve.tensor_scalar(x_in[:, t, :], x_in[:, t, :], s, None, ALU.mult).then_inc(h_ready, 1)
            for t in range(NT):
                for a in range(2):
                    ps = filled(("x", t, a))[:, :].rearrange("p (k n) -> p k n", k=4)
                    ve.tensor_tensor(hT[:, 4 * a:4 * a + 4, t * P:(t + 1) * P], ps,
                                     bc(par[:, R_NORM + 4 * a:R_NORM + 4 * a + 4], P), ALU.mult).then_inc(v_drained, 1)
            for n in range(2):
                ps = filled(f"rel{n}")
                ve.tensor_copy(rel_row[:, 320 * n:320 * n + 320], ps[0:N_HEADS, 0:320]).then_inc(v_drained, 1)
            ve.wait_ge(v_drained, V.filled("rel1"))
            ve.nop().then_inc(rows_ready, 1)

            SQ.wait(ve, "A0")
            sq = squares[:, 0:1536].rearrange("p (t n) -> p t n", t=NT)
            ssq = ss_a.rearrange("p (t g) -> p t g", t=NT)
            ve.tensor_reduce(ssq[:, :, 0:4], sq[:, :, 0:256].rearrange("p t (g d) -> p t g d", d=64), AX.X, ALU.add)
            hold(ve.tensor_reduce(ssq[:, :, 4], sq[:, :, 256:384], AX.X, ALU.add))
            hold(ve.tensor_scalar(ssq[:, :, 4], ssq[:, :, 4], 0.5, None, ALU.mult))
            y, w = inv_root("A0", ss_a, 20, 1.0 / 64)
            hold(ve.tensor_tensor(ss_a, y, w, ALU.mult))
            ckv = raw_a0[:, :, 256:384]
            ve.tensor_tensor(ckv, ckv, bc(ssq[:, :, 4], P), ALU.mult).then_inc(T_IN.sem, 1)
            for g in range(4):
                q_g = raw_a0[:, :, 64 * g:64 * g + 64]
                ins = ve.tensor_tensor(q_g, q_g, bc(ssq[:, :, g], 64), ALU.mult)
            ins.then_inc(T_IN.sem, 1)
            ve.tensor_scalar(ckvT, filled("ckvT")[:, :], par[:, R_CKV:R_CKV + 1], None, ALU.mult).then_inc(v_drained, 1)
            for m in range(2):
                ve.tensor_scalar(qT_a[:, m, :], filled(f"qT{m}")[:, :], par[:, R_AQ:R_AQ + 1], A_HD ** -0.5,
                                 ALU.mult, ALU.mult).then_inc(v_drained, 1)
            for t in range(NT):
                ps = filled(("ukv", t))
                ve.tensor_copy(k_raw[:, t, :], ps[:, 0:256])
                ve.tensor_copy(v_a[:, t, :], ps[:, 256:512]).then_inc(v_drained, 1)
            SQ.wait(ve, "Ak")
            hold(ve.tensor_reduce(ss_k, squares[:, 0:1024].rearrange("p (g d) -> p g d", d=64), AX.X, ALU.add))
            y, w = inv_root("Ak", ss_k, 16, 1.0 / 64)
            hold(ve.tensor_tensor(ss_k, y, w, ALU.mult))
            kf = work[:, 4608:5632].rearrange("p (g d) -> p g d", d=64)
            ve.tensor_tensor(kf, kf, bc(ss_k, 64), ALU.mult).then_inc(T_IN.sem, 1)
            ve.wait_ge(s_drained, S.filled(("A2", 3)))
            ki2 = squares[:, 1024:1536].rearrange("p (t a d) -> p t a d", t=NT, a=2)
            for a in range(2):
                ins = ve.tensor_copy(ki2[:, :, a, :], raw_a2[:, :, 0:64])
            ins.then_inc(T_IN.sem, 1)
            hold(ve.tensor_scalar(raw_a2[:, :, 64:72], raw_a2[:, :, 64:72], IDX_HEADS ** -0.5, 64 ** -0.5, ALU.mult, ALU.mult))
            for m in range(2):
                ve.tensor_scalar(kT_a[:, m, :], filled(f"kT{m}")[:, :], par[:, R_AK:R_AK + 1], None, ALU.mult).then_inc(v_drained, 1)
            ve.tensor_copy(kiT, filled("kiT")[:, :]).then_inc(v_drained, 1)
            ve.wait_ge(v_drained, V.filled("kiT"))
            n = 0
            for q in range(1, NT):
                L = P * (q + 1)
                for h in range(IDX_HEADS):
                    ve.wait_ge(s_drained, S.filled(("idx", q, h)))
                    r, wi = relu_buf[n % 2][:, 0:L], raw_a2[:, q, 64 + h:65 + h]
                    if h == 0:
                        ins = ve.tensor_scalar(scores[q - 1], r, wi, None, ALU.mult)
                    else:
                        ins = ve.scalar_tensor_tensor(scores[q - 1], r, wi, scores[q - 1], ALU.mult, ALU.add)
                    n += 1
                    ins.then_inc(relu_used, 1)
                    ve.wait_ge(relu_used, n)
                ve.nop().then_inc(score_ready, 1)

            def conv(m):
                name = (("B0", "B1", "B2")[m // 4], m % 4)
                ve.wait_ge(s_drained, S.filled(name))
                if m >= 2:
                    ve.wait_ge(conv_done, m - 1)
                acc = conv_acc[:, m % 2, :]
                tap = [par[:, R_CONV + 12 * w + m:R_CONV + 12 * w + m + 1] for w in range(4)]
                hold(ve.tensor_scalar(acc, qkvT[:, m, 0:T], tap[0], None, ALU.mult))
                for w in range(1, 4):
                    ins = ve.scalar_tensor_tensor(acc, qkvT[:, m, w:w + T], tap[w], acc, ALU.mult, ALU.add)
                    if w < 3:
                        hold(ins)
                ins.then_inc(conv_ready, 1)

            ve.wait_ge(fills, 3)
            for q in range(1, NT):
                L = P * (q + 1)
                ve.wait_ge(diag_ready, q)
                src = scores[q - 1]
                for r in range(TOPK // 8):
                    m8 = max8[:, 8 * (r % 2):8 * (r % 2) + 8]
                    hold(ve.max(m8, src))
                    dst = topk_work[r % 2][:, 0:L]
                    hold(ve.match_replace(dst, m8, src, TAKEN))
                    src = dst
                hold(ve.tensor_scalar(src, src, TAKEN, -NEG, ALU.is_equal, ALU.mult))
                ve.tensor_scalar(keep_add[q - 1], src, NEG, None, ALU.add).then_inc(keep_ready, 1)
            ve.wait_ge(keep_ready, 3)
            for m in range(12):
                conv(m)

            SQ.wait(ve, "C0")
            hold(ve.tensor_reduce(ss_c, squares[:, 0:1280].rearrange("p (g d) -> p g d", d=64), AX.X, ALU.add))
            y, w = inv_root("C0", ss_c, 20, 1.0 / 64)
            hold(ve.tensor_tensor(ss_c, y, w, ALU.mult))
            ssc = ss_c.rearrange("p (t g) -> p t g", t=NT)
            for g in range(4):
                q_g = raw_c0[:, :, 64 * g:64 * g + 64]
                ins = ve.tensor_tensor(q_g, q_g, bc(ssc[:, :, g], 64), ALU.mult)
            ins.then_inc(T_IN.sem, 1)
            dup = squares[:, 0:2048].rearrange("p (s t a d) -> p s t a d", s=4, t=NT, a=2)
            T_IN.wait(ve, "C0q")
            SQ.wait(ve, "C1")
            hold(ve.tensor_reduce(ss_w, squares[:, 1280:1536].rearrange("p (t d) -> p t d", t=NT), AX.X, ALU.add))
            y, w = inv_root("C1", ss_w, 4, 1.0 / 64)
            hold(ve.tensor_tensor(ss_w, y, w, ALU.mult))
            for s in range(2):
                for a in range(2):
                    ins = ve.tensor_copy(dup[:, s, :, a, :], raw_c0[:, :, 256 + 64 * s:320 + 64 * s])
            ins.then_inc(T_IN.sem, 1)
            for a in range(2):
                ins = ve.tensor_tensor(dup[:, 2, :, a, :], raw_c0[:, :, 384:448], bc(ssc[:, :, 4], 64), ALU.mult)
            ins.then_inc(T_IN.sem, 1)
            for a in range(2):
                ins = ve.tensor_tensor(dup[:, 3, :, a, :], raw_c1[:, :, 64:128], bc(ss_w, 64), ALU.mult)
            ins.then_inc(T_IN.sem, 1)
            for m in range(2):
                ve.tensor_scalar(qT_c[:, m, :], filled(f"cqT{m}")[:, :], par[:, R_CQ:R_CQ + 1], C_HD ** -0.5,
                                 ALU.mult, ALU.mult).then_inc(v_drained, 1)
            for v, name in enumerate(("kcmp", "vcmp")):
                ps = filled(name)[:, :].rearrange("p (m q) -> p m q", q=16)
                for a in range(2):
                    for half in range(2):
                        src = ps[64 * a:64 * a + 64, half:half + N_CMP, a:16:2].rearrange("p m q -> p q m")
                        pos = par[64 * a:64 * a + 64, R_POS + 16 * v + 8 * half:R_POS + 16 * v + 8 * half + 8]
                        ins = ve.tensor_tensor(blocks[64 * a:64 * a + 64, v, 8 * half:8 * half + 8, :], src,
                                               bc(pos, N_CMP), ALU.add)
                ins.then_inc(v_drained, 1)
            ve.tensor_scalar(kT_sel[:, :], filled("ksT")[:, :], par[:, R_CK + 1:R_CK + 2], None, ALU.mult).then_inc(v_drained, 1)
            ve.tensor_scalar(kT_win[:, :], filled("kwT")[:, :], par[:, R_CK + 2:R_CK + 3], None, ALU.mult).then_inc(v_drained, 1)

            ps = filled("cmpkv")
            kc, vc, kc2 = raw_c0[0:N_CMP, 1, 0:64], cmp_v[:, :], raw_c0[0:N_CMP, 1, 64:128]
            ve.tensor_copy(kc, ps[0:N_CMP, 0:64])
            ve.tensor_copy(vc, ps[0:N_CMP, 64:128]).then_inc(v_drained, 1)
            ve.wait_ge(v_drained, V.filled("cmpkv"))
            hold(ve.tensor_tensor(kc2, kc, kc, ALU.mult))
            s = ss_kc[0:N_CMP, :]
            hold(ve.tensor_reduce(s, kc2, AX.X, ALU.add))
            y, w = inv_root("kc", s, 1, 1.0 / 64)
            hold(ve.tensor_tensor(s, y, w, ALU.mult))
            kdup = raw_c0[0:N_CMP, 0, 0:128]
            for a in range(2):
                ins = ve.tensor_scalar(kdup[:, 64 * a:64 * a + 64], kc, s, None, ALU.mult)
            ins.then_inc(T_IN.sem, 1)
            ve.tensor_scalar(kcT[:, 0:N_CMP], filled("kcT")[:, 0:N_CMP], par[:, R_CK:R_CK + 1], None, ALU.mult).then_inc(v_drained, 1)

            ve.wait_ge(const_loaded, 16 * 7)
            sa = sp_a.rearrange("p (c h) -> p c h", c=NT)
            hold(ve.tensor_tensor(sa, raw_b[:, :, 0:4], dt_b.unsqueeze(1).to_broadcast([P, NT, 4]), ALU.add))
            hold(ve.scalar_tensor_tensor(sp_b, sp_a, -1.0, sp_a, ALU.mult, ALU.max))
            hold(ve.tensor_scalar(sp_a, sp_a, 0.0, None, ALU.max))
            ve.nop().then_inc(GATE_IN.sem, 1)
            GATE_OUT.wait(ve, "sp")
            hold(ve.tensor_tensor(sp_a, sp_a, sp_b, ALU.add))
            gt = g_t.rearrange("p (c h) -> p c h", c=NT)
            hold(ve.tensor_tensor(gt, sa, neg_exp_a.unsqueeze(1).to_broadcast([P, NT, 4]), ALU.mult))
            hold(ve.tensor_scalar(g_t, g_t, -1.0, None, ALU.mult))
            ve.nop().then_inc(gsum_ready, 1)
            ps = filled("sums")
            ve.tensor_copy(sums_sb, ps[:, 0:64]).then_inc(v_drained, 1)
            ve.wait_ge(v_drained, V.filled("sums"))
            ve.tensor_copy(ss_b, sums_sb[:, 32:64])
            ve.tensor_copy(gc_, sums_sb[:, 0:16])
            ve.tensor_copy(gl_, sums_sb[:, 16:32])
            hold(ve.tensor_tensor(kd_s, sums_sb[:, 16:32], sums_sb[:, 0:16], ALU.subtract))
            y, w = inv_root("B", ss_b, 32, 1.0)
            hold(ve.tensor_tensor(y, y, w, ALU.mult))
            hold(ve.tensor_scalar(rqs, y[:, 0:16], B_HD ** -0.5, None, ALU.mult))
            hold(ve.tensor_copy(rk, y[:, 16:32]))
            hold(ve.tensor_tensor(nk, ss_b[:, 16:32], rk, ALU.mult))
            hold(ve.tensor_tensor(a_s, beta_t, rk, ALU.mult))
            hold(ve.tensor_tensor(n_s, a_s, rk, ALU.mult))
            hold(ve.tensor_scalar(n_s, n_s, -1.0, None, ALU.mult))
            ve.nop().then_inc(GATE_IN.sem, 1)
            GATE_OUT.wait(ve, "exps")
            hold(ve.tensor_scalar(negegc, egc, -1.0, None, ALU.mult))
            hold(ve.tensor_tensor(kd_s, ekd, rk, ALU.mult))

            def bank4(name):
                return filled(name)[:, :].rearrange("p (h n) -> p h n", h=4)

            for c in range(NT):
                def ready(ins, name):
                    ins.then_inc(GD.sem, 1)

                ps = bank4(("gc", c))
                if c > 0:
                    ve.wait_ge(decays_ready, 2 * c)
                ve.tensor_tensor(decay, ps, heads(gc_, c), ALU.subtract).then_inc(v_drained, 1)
                ve.wait_ge(v_drained, V.filled(("gc", c)))
                ve.nop().then_inc(diff_ready, 1)
                ve.tensor_tensor(k_tok, bank4(("kt", c)), heads(kd_s, c), ALU.mult).then_inc(v_drained, 1)
                ve.tensor_tensor(v_tok, bank4(("vt", c)), heads(nk, c), ALU.mult).then_inc(v_drained, 1)
                ve.wait_ge(v_drained, V.filled(("vt", c)))
                ve.nop().then_inc(GD.sem, 1)
                ve.wait_ge(decays_ready, 2 * c + 2)
                ve.tensor_tensor(neg_nT, bank4(("kk", c)), decay_n, ALU.mult).then_inc(v_drained, 1)
                ve.wait_ge(v_drained, V.filled(("kk", c)))
                ve.nop().then_inc(GD.sem, 1)
                ve.tensor_tensor(attnT, bank4(("qk", c)), attnT, ALU.mult).then_inc(v_drained, 1)
                ve.wait_ge(v_drained, V.filled(("qk", c)))
                ve.nop().then_inc(GD.sem, 1)
                ve.wait_ge(eye_ready, 2 * c + 2)

                def put(dst, n, src):
                    return ve.copy_predicated(dst, level_masks[:, n, :].unsqueeze(1).to_broadcast([P, 4, P]), src)

                put(t_invT, LEVELS, neg_nT)
                put(t_inv, 0, bank4(("n", c))).then_inc(v_drained, 1)
                ve.wait_ge(v_drained, V.filled(("n", c)))
                ve.nop().then_inc(GD.sem, 1)
                for l in range(1, LEVELS):
                    ve.tensor_copy(z_sb, bank4(("z", c, l))).then_inc(v_drained, 1)
                    ve.wait_ge(v_drained, V.filled(("z", c, l)))
                    ve.nop().then_inc(GD.sem, 1)
                    name = ("u", c, l) if l < LEVELS - 1 else ("ut", c, l)
                    filled(name)
                    put(t_invT, LEVELS + l, bank4(("ut", c, l))).then_inc(v_drained, 1)
                    ve.wait_ge(v_drained, V.filled(("ut", c, l)))
                    ve.nop().then_inc(GD.sem, 1)
                    if l < LEVELS - 1:
                        put(t_inv, l, bank4(("u", c, l))).then_inc(v_drained, 1)
                        ve.wait_ge(v_drained, V.filled(("u", c, l)))
                        ve.nop().then_inc(GD.sem, 1)
                if c == 0:
                    hold(ve.tensor_copy(resid, v_tok))
                else:
                    ps = bank4(("ks", c))
                    for h in range(4):
                        ins = ve.scalar_tensor_tensor(resid[:, h, :], ps[:, h, :], negegc[:, 4 * c + h:4 * c + h + 1],
                                                      v_tok[:, h, :], ALU.mult, ALU.add)
                    ins.then_inc(v_drained, 1)
                    ve.wait_ge(v_drained, V.filled(("ks", c)))
                ve.nop().then_inc(GD.sem, 1)
                ve.tensor_tensor(v_new, bank4(("x2", c)), heads(a_s, c), ALU.mult).then_inc(v_drained, 1)
                ve.wait_ge(v_drained, V.filled(("x2", c)))
                ve.nop().then_inc(GD.sem, 1)
                ps = bank4(("o", c))
                if c == 0:
                    ve.tensor_copy(o_tok, ps).then_inc(v_drained, 1)
                else:
                    ve.wait_ge(o_drained, O.filled(("os", c)))
                    ve.wait_ge(y_b, c)
                    ve.tensor_tensor(o_tok, ps, o_state, ALU.add).then_inc(v_drained, 1)
                ve.wait_ge(v_drained, V.filled(("o", c)))
                ve.nop().then_inc(GD.sem, 1)
                if c < NT - 1:
                    ps = bank4(("st", c))
                    if c == 0:
                        ve.tensor_copy(state, ps).then_inc(v_drained, 1)
                    else:
                        for h in range(4):
                            ins = ve.scalar_tensor_tensor(state[:, h, :], state[:, h, :], egl[:, 4 * c + h:4 * c + h + 1],
                                                          ps[:, h, :], ALU.mult, ALU.add)
                        ins.then_inc(v_drained, 1)
                    ve.wait_ge(v_drained, V.filled(("st", c)))
                    ve.nop().then_inc(GD.sem, 1)
                SQ.wait(ve, ("ob", c))
                so = ss_o[:, 4 * c:4 * c + 4]
                hold(ve.tensor_reduce(so, o_sq, AX.X, ALU.add))
                y, w = inv_root(("ob", c), so, 4, 1.0 / B_HD)
                hold(ve.tensor_tensor(so, y, w, ALU.mult))
                ve.tensor_tensor(o_tok, o_tok, bc(so, P), ALU.mult).then_inc(o_scaled, 1)

            cpv = cmp_p.rearrange("p (q h n) -> p q h n", q=NT, h=C_HEADS)
            ve.wait_ge(cmp_strip_ready, 1)
            for a in range(2):
                ps = filled(f"cl{a}")[:, 0:248].rearrange("p (q h n) -> p q h n", q=NT, h=2)
                ve.tensor_tensor(cpv[:, :, a::2, :], ps, cmp_strip[:, a::2, :, :].rearrange("p h q n -> p q h n"),
                                 ALU.add).then_inc(v_drained, 1)
            ve.wait_ge(v_drained, V.filled("cl1"))
            cpg = cmp_p.rearrange("p (g n) -> p g n", g=16)
            hold(ve.tensor_reduce(cmx, cpg, AX.X, ALU.max))
            ve.tensor_tensor(cpg, cpg, bc(cmx, N_CMP), ALU.subtract).then_inc(cl_ready, 1)
            ve.wait_ge(cexp_ready, 1)
            hold(ve.tensor_reduce(crs, cpg, AX.X, ALU.add))
            hold(ve.reciprocal(crs, crs))
            crq = crs.rearrange("p (q h) -> p q h", q=NT)
            hold(ve.tensor_scalar(crq[:, 0, :], crq[:, 0, :], seen[:, 0:1], None, ALU.mult))
            gate = raw_c1[:, :, 192:204].rearrange("p t (h k) -> p t h k", k=3)
            hold(ve.tensor_tensor(crq, crq, gate[:, :, :, 0], ALU.mult))

            def cmp_out():
                for n in range(2):
                    ve.wait_ge(o_filled, O.filled(("oc", n)))
                    ps = O.bank(("oc", n))[:, :].rearrange("p (g d) -> p g d", d=64)
                    ve.tensor_tensor(o_cg[:, 8 * n:8 * n + 8, :], ps, bc(crs[:, 8 * n:8 * n + 8], 64), ALU.mult).then_inc(o_drained, 1)

            o_cg = work[:, 2560:3584].rearrange("p (g d) -> p g d", d=64)

            def logits(u):
                m, q, h = units[u]
                L = P * (q + 1)
                ps = filled(("lg", m, q, h))
                if u >= 2:
                    ve.wait_ge(s_filled, S.filled(("pT", *units[u - 2])))
                if m == "A":
                    if q:
                        ve.wait_ge(bias_ready, u - 3)
                    b = bias_sel[u % 2][:, 0:L] if q else strips[:, h, T - L:T]
                else:
                    b = strips[:, A_HEADS + h, T - L:T]
                ve.tensor_tensor_reduce(out=probs[u % 2][:, 0:L], in0=ps[:, 0:L], in1=b, scale=1.0, scalar=-3e38,
                                        op0=ALU.add, op1=ALU.max, accum_out=mx[:, u:u + 1]).then_inc(v_drained, 1)
                ve.wait_ge(v_drained, V.filled(("lg", m, q, h)))
                ve.tensor_scalar(nmx[:, u:u + 1], mx[:, u:u + 1], -1.0, None, ALU.mult).then_inc(logits_ready, 1)

            def finish(g):
                m, q = groups[g]
                ve.wait_ge(probs_ready, 4 * g + 4)
                hold(ve.reciprocal(fac, rsum[:, 4 * g:4 * g + 4]))
                if m != "A":
                    hold(ve.tensor_tensor(fac, fac, gate[:, q, :, 1 if m == "sel" else 2], ALU.mult))
                ve.wait_ge(o_filled, O.filled(("o", m, q)))
                ps = O.bank(("o", m, q))[:, 0:256].rearrange("p (h d) -> p h d", h=4)
                oc = o_c[:, q, :].rearrange("p (h d) -> p h d", h=4)
                if m == "A":
                    ve.tensor_tensor(oc, ps, bc(fac, 64), ALU.mult).then_inc(o_drained, 1)
                    ve.wait_ge(o_drained, O.filled(("o", m, q)))
                elif m == "sel":
                    ve.wait_ge(y_ready, q + 1)
                    hold(ve.tensor_copy(oc, o_cg[:, 4 * q:4 * q + 4, :]))
                if m != "A":
                    tmp = cmp_p[:, 0:256].rearrange("p (h d) -> p h d", h=4)
                    ve.tensor_tensor(tmp, ps, bc(fac, 64), ALU.mult).then_inc(o_drained, 1)
                    ve.wait_ge(o_drained, O.filled(("o", m, q)))
                    hold(ve.tensor_tensor(oc, oc, tmp, ALU.add))
                ve.nop().then_inc(o_norm, 1)

            ve.wait_ge(y_b, NT)
            logits(0)
            logits(1)
            cmp_out()
            for u in range(len(units)):
                if u + 2 < len(units):
                    logits(u + 2)
                if u % 4 == 3 and u >= 7:
                    finish(u // 4 - 1)
            finish(len(groups) - 1)

            for f in range(KC):
                ps = filled(("yT", f))
                if 2 <= f < 6:
                    ins = ve.tensor_scalar(yT[:, f, :], ps[:, :], par[:, R_BOUT:R_BOUT + 1], None, ALU.mult)
                else:
                    ins = ve.tensor_copy(yT[:, f, :], ps[:, :])
                ins.then_inc(v_drained, 1)
            for j in range(KC):
                if j >= 4:
                    ve.wait_ge(s_drained, S.filled(("gate", 12 + 8 + j - 4)))
                for b in range(3):
                    g = gates[:, 4 * b + j % 4, :]
                    ins = ve.tensor_tensor(g, filled(("br", j, b))[:, :], g, ALU.mult)
                    ins.then_inc(v_drained, 1)
                ve.wait_ge(v_drained, V.filled(("br", j, 2)))
                ve.nop().then_inc(merge_ready, 1)
            ve.wait_ge(x_reloaded, 16)
            for n in range(2):
                for t in range(NT):
                    xr = x_again[:, t, 512 * n:512 * n + 512]
                    ve.tensor_tensor(xr, filled(("wo", n, t))[:, :], xr, ALU.add).then_inc(v_drained, 1)
                    ve.wait_ge(v_drained, V.filled(("wo", n, t)))
                    ve.nop().then_inc(out_ready, 1)

        @block.tensor
        def _(pe):
            mm = nc.tensor.matmul

            def v_bank(name):
                if V.free(name) > 0:
                    pe.wait_ge(v_drained, V.free(name))
                return V.bank(name)

            def s_bank(name):
                if S.free(name) > 0:
                    pe.wait_ge(s_drained, S.free(name))
                return S.bank(name)

            def o_bank(name):
                if O.free(name) > 0:
                    pe.wait_ge(o_drained, O.free(name))
                return O.bank(name)

            def weights(c, k=KC):
                pe.wait_ge(w_loaded[c % 2], 16 * (c // 2 + 1))
                n = CHUNKS[c][2]
                return ring[:, c % 2, 0:k * n].rearrange("p (k n) -> p k n", k=k)

            def project_tokens(c, name):
                w, n = weights(c), CHUNKS[c][2]
                for t in range(NT):
                    ps = s_bank((name, t))
                    for k in range(KC):
                        ins = mm(ps[:, 0:n], hT[:, k, t * P:(t + 1) * P], w[:, k, :], start=k == 0, stop=k == KC - 1)
                    ins.then_inc(s_filled, 1)

            def project_features(c, name, first=0):
                w = weights(c)
                for m in range(4):
                    ps = s_bank((name, m))
                    for k in range(KC):
                        ins = mm(ps[:, 0:T - first], w[:, k, m * P:(m + 1) * P], hT[:, k, first:T], start=k == 0, stop=k == KC - 1)
                    ins.then_inc(s_filled, 1)

            def transposes(name, sources, rows=P, cols_=P):
                ps = v_bank(name)
                for n, src in enumerate(sources):
                    ins = nc.tensor.transpose(ps[0:cols_, n * rows:n * rows + rows], src, ident[0:rows, 0:rows])
                ins.then_inc(v_filled, 1)

            pe.wait_ge(const_loaded, 16 * 7)
            pe.wait_ge(in_loaded, 16 * 16)
            transposes("par", [par_rows], N_ROWS)
            for t in range(NT):
                pe.wait_ge(h_ready, t + 1)
                for a in range(2):
                    transposes(("x", t, a), [x_in[:, t, (4 * a + k) * P:(4 * a + k + 1) * P] for k in range(4)])
            pe.wait_ge(hot_ready, 1)
            for n in range(2):
                ps = v_bank(f"rel{n}")
                mm(ps[0:N_HEADS, 0:320], rel33, hot[0:N_BUCKETS + 1, 320 * n:320 * n + 320], start=True, stop=True).then_inc(v_filled, 1)
            pe.wait_ge(v_drained, V.filled(("x", NT - 1, 1)))
            project_tokens(CH_A0, "A0")
            project_features(CH_QI, "QI", P)
            T_IN.wait(pe, "A0ckv")
            transposes("ckvT", [raw_a0[:, t, 256:384] for t in range(NT)])
            T_IN.wait(pe, "A0q")
            for m in range(2):
                transposes(f"qT{m}", [raw_a0[:, t, m * P:(m + 1) * P] for t in range(NT)])
            pe.wait_ge(v_drained, V.filled("ckvT"))
            pe.wait_ge(ukv_loaded, 16)
            for t in range(NT):
                ps = v_bank(("ukv", t))
                mm(ps[:, :], ckvT[:, t * P:(t + 1) * P], ukv, start=True, stop=True).then_inc(v_filled, 1)
            project_tokens(CH_A2, "A2")
            T_IN.wait(pe, "Ak")
            for m in range(2):
                transposes(f"kT{m}", [k_raw[:, t, m * P:(m + 1) * P] for t in range(NT)])
            T_IN.wait(pe, "Aki")
            transposes("kiT", [squares[:, 1024 + P * t:1152 + P * t] for t in range(NT)])
            project_features(CH_B0, "B0")
            pe.wait_ge(v_drained, V.filled("kiT"))
            for q in range(1, NT):
                for h in range(IDX_HEADS):
                    L, r = P * (q + 1), 64 * (h % 2)
                    ps = s_bank(("idx", q, h))
                    mm(ps[:, 0:L], qiT[r:r + 64, h // 2, (q - 1) * P:q * P], kiT[r:r + 64, 0:L], start=True, stop=True).then_inc(s_filled, 1)
            project_features(CH_B1, "B1")
            project_features(CH_B2, "B2")
            for c, name in ((CH_B3, "B3"), (CH_B4, "B4"), (CH_C0, "C0"), (CH_C1, "C1")):
                project_tokens(c, name)
            T_IN.wait(pe, "C0q")
            for m in range(2):
                transposes(f"cqT{m}", [raw_c0[:, t, m * P:(m + 1) * P] for t in range(NT)])
            for n, (name, inp) in enumerate((("kcmp", "C0blk"), ("vcmp", "C0blk"), ("ksT", "C0ks"), ("kwT", "C1kw"))):
                T_IN.wait(pe, inp)
                transposes(name, [squares[:, 512 * n + P * t:512 * n + P * t + P] for t in range(NT)])
            ps = s_bank("hid")
            for v in range(2):
                w = weights(CH_PK + v, 16)
                pe.wait_ge(v_drained, V.filled(("kcmp", "vcmp")[v]))
                for h in range(2):
                    for k in range(16):
                        ins = mm(ps[:, (2 * v + h) * N_CMP:(2 * v + h + 1) * N_CMP], w[:, k, h * P:(h + 1) * P],
                                 blocks[:, v, k, :], start=k == 0, stop=k == 15)
                ins.then_inc(phi_used, 1)
            pe.wait_ge(phi_used, 2)
            pe.nop().then_inc(s_filled, 1)
            pe.wait_ge(s_drained, S.filled("hid"))
            ps = v_bank("cmpkv")
            for v in range(2):
                for h in range(2):
                    ins = mm(ps[0:N_CMP, 64 * v:64 * v + 64], hidT[:, 2 * v + h, :], phi2[:, 2 * v + h, :], start=h == 0, stop=h == 1)
            ins.then_inc(v_filled, 1)
            T_IN.wait(pe, "kc")
            transposes("kcT", [raw_c0[0:N_CMP, 0, 0:128]], N_CMP)
            ps = v_bank("sums")
            for m in range(8):
                SQ.wait(pe, ("B", m))
                for t in range(NT):
                    c0 = 32 + 16 * (m // 4) + 4 * t + m % 4
                    ins = mm(ps[:, c0:c0 + 1], squares[:, 512 * (m % 4) + t * P:512 * (m % 4) + (t + 1) * P], ones[:, 0:1],
                             start=True, stop=True)
                ins.then_inc(sums_taken, 1)
            pe.wait_ge(gsum_ready, 1)
            mm(ps[:, 0:16], tri, g_t, start=True, stop=True)
            mm(ps[:, 16:32], ones[:, :], g_t, start=True, stop=True).then_inc(v_filled, 1)

            def gate_products():
                for g in range(24):
                    if g % 4 == 0:
                        w = weights((CH_G0, CH_G1, CH_G2, CH_G3, CH_G4, CH_G5)[g // 4])
                    ps = s_bank(("gate", g))
                    for k in range(KC):
                        ins = mm(ps[:, :], w[:, k, g % 4 * P:(g % 4 + 1) * P], hT[:, k, :], start=k == 0, stop=k == KC - 1)
                        if k == KC - 1:
                            ins.then_inc(s_filled, 1)
                        yield

            gate_steps = gate_products()

            def fill(n):
                for _ in range(n):
                    next(gate_steps)

            def four(name, lhs, rhs, ring_=None):
                ps = v_bank(name) if ring_ is None else o_bank(name)
                for h in range(4):
                    ins = mm(ps[:, h * P:(h + 1) * P], lhs(h), rhs(h), start=True, stop=True)
                ins.then_inc(v_filled if ring_ is None else o_filled, 1)

            pe.wait_ge(conv_done, 12)
            for c in range(NT):
                tok = slice(3 + c * P, 3 + (c + 1) * P)
                qc, kc_, vc_ = (lambda h, m=m: qkvT[:, 4 * m + h, tok] for m in range(3))
                pe.wait_ge(gtri_ready, c + 1)
                ps = v_bank(("gc", c))
                mm(ps[:, :], ones[:, :], g_tri.rearrange("p h n -> p (h n)"), start=True, stop=True).then_inc(v_filled, 1)
                transposes(("kt", c), [kc_(h) for h in range(4)])
                transposes(("vt", c), [vc_(h) for h in range(4)])
                four(("kk", c), kc_, kc_)
                four(("qk", c), kc_, qc)
                fill(2)
                GD.wait(pe, ("nnt", c))
                transposes(("n", c), [neg_nT[:, h, :] for h in range(4)])
                GD.wait(pe, ("tt0", c))
                for l in range(1, LEVELS):
                    four(("z", c, l), lambda h: neg_nT[:, h, :], lambda h: t_inv[:, h, :])
                    fill(2)
                    GD.wait(pe, ("z", c, l))
                    four(("ut", c, l), lambda h: z_sb[:, h, :], lambda h: t_invT[:, h, :])
                    if l < LEVELS - 1:
                        four(("u", c, l), lambda h: t_invT[:, h, :], lambda h: z_sb[:, h, :])
                    if l < LEVELS - 1:
                        fill(2)
                        GD.wait(pe, ("t", c, l))
                if c > 0:
                    GD.wait(pe, ("state", c - 1))
                    four(("ks", c), kc_, lambda h: state[:, h, :])
                    four(("os", c), qc, lambda h: state[:, h, :], O)
                GD.wait(pe, ("resid", c))
                four(("x2", c), lambda h: t_invT[:, h, :], lambda h: resid[:, h, :])
                GD.wait(pe, ("vnew", c))
                four(("o", c), lambda h: attnT[:, h, :], lambda h: v_new[:, h, :])
                if c < NT - 1:
                    four(("st", c), lambda h: k_tok[:, h, :], lambda h: v_new[:, h, :])

            for a in range(2):
                ps, r = v_bank(f"cl{a}"), 64 * a
                for q in range(NT):
                    for m in range(2):
                        u = 2 * q + m
                        ins = mm(ps[:, u * N_CMP:(u + 1) * N_CMP], qT_c[r:r + 64, m, q * P:(q + 1) * P], kcT[r:r + 64, 0:N_CMP],
                                 start=True, stop=True)
                ins.then_inc(v_filled, 1)

            def unit_logits(u):
                m, q, h = units[u]
                qT, kT = {"A": (qT_a, kT_a[:, h // 2, :]), "sel": (qT_c, kT_sel), "win": (qT_c, kT_win)}[m]
                r, L = 64 * (h % 2), P * (q + 1)
                ps = v_bank(("lg", m, q, h))
                mm(ps[:, 0:L], qT[r:r + 64, h // 2, q * P:(q + 1) * P], kT[r:r + 64, 0:L], start=True, stop=True).then_inc(v_filled, 1)

            unit_logits(0)
            unit_logits(1)
            pe.wait_ge(cexp_ready, 1)
            for q in range(NT):
                ps = s_bank(("cp", q))
                for h in range(4):
                    ins = nc.tensor.transpose(ps[0:N_CMP, h * P:(h + 1) * P], cmp_p[:, (4 * q + h) * N_CMP:(4 * q + h + 1) * N_CMP], ident)
                ins.then_inc(s_filled, 1)
            for n in range(2):
                ps = o_bank(("oc", n))
                pe.wait_ge(s_drained, S.filled(("cp", 2 * n + 1)))
                for u in range(8):
                    ins = mm(ps[:, 64 * u:64 * u + 64], cmp_pT[:, 8 * n + u, :], cmp_v[:, :], start=True, stop=True)
                ins.then_inc(o_filled, 1)

            def unit_out(u):
                m, q, h = units[u]
                ps = O.bank(("o", m, q)) if h else o_bank(("o", m, q))
                pe.wait_ge(s_drained, S.filled(("pT", m, q, h)))
                for k in range(q + 1):
                    v = {"A": v_a[:, k, 64 * h:64 * h + 64], "sel": raw_c1[:, k, 0:64], "win": raw_c1[:, k, 128:192]}[m]
                    ins = mm(ps[:, 64 * h:64 * h + 64], probsT[u % 2][:, k * P:(k + 1) * P], v, start=k == 0, stop=k == q)
                ins.then_inc(pv_done, 1)
                if h == 3:
                    pe.wait_ge(pv_done, u + 1)
                    pe.nop().then_inc(o_filled, 1)

            for u, (m, q, h) in enumerate(units):
                pe.wait_ge(probs_ready, u + 1)
                ps = s_bank(("pT", m, q, h))
                for k in range(q + 1):
                    ins = nc.tensor.transpose(ps[:, k * P:(k + 1) * P], probs[u % 2][:, k * P:(k + 1) * P], ident)
                ins.then_inc(s_filled, 1)
                if u + 2 < len(units):
                    unit_logits(u + 2)
                if u >= 1:
                    unit_out(u - 1)
            unit_out(len(units) - 1)

            pe.wait_ge(y_b, NT)
            pe.wait_ge(y_ready, 2 * NT)
            sources = [(raw_a2, 72), (raw_a2, 200)] + [(raw_b, 8 + P * n) for n in range(4)] + [(raw_c1, 204), (raw_c1, 332)]
            for f, (raw, c0) in enumerate(sources):
                transposes(("yT", f), [raw[:, t, c0:c0 + P] for t in range(NT)])
            pe.wait_ge(v_drained, V.filled(("yT", KC - 1)))

            def branches(j0, w):
                for j in range(j0, j0 + 4):
                    for b, rows in enumerate(((0, 2), (2, 6), (6, 8))):
                        ps = v_bank(("br", j, b))
                        for k in range(*rows):
                            ins = mm(ps[:, :], w[:, k, j % 4 * P:(j % 4 + 1) * P], yT[:, k, :], start=k == rows[0], stop=k == rows[1] - 1)
                        ins.then_inc(v_filled, 1)

            branches(0, weights(CH_WB0))
            fill(12 * KC)
            branches(4, weights(CH_WB1))
            pe.wait_ge(merged_ready, KC)
            for n in range(2):
                w = weights(CH_WO0 + n)
                for t in range(NT):
                    ps = v_bank(("wo", n, t))
                    for k in range(KC):
                        ins = mm(ps[:, :], mergedT[:, k, t * P:(t + 1) * P], w[:, k, :], start=k == 0, stop=k == KC - 1)
                    ins.then_inc(v_filled, 1)


NAMES = ["x", "norm_g", "w_in", "a_kv_norm", "a_w_ukv", "a_q_norm", "a_k_norm", "b_conv", "b_a_log", "b_dt_bias",
         "b_out_norm", "c_q_norm", "c_k_norm", "c_cmp_pos", "c_phi_w1", "c_phi_w2", "w_branch", "w_out", "rel_bias"]


def kernel(**inputs):
    import concourse.bacc as bacc
    from concourse.bass_utils import run_bass_kernel_spmd

    nc = bacc.Bacc("TRN2", target_bir_lowering=False, num_devices=1)
    floats, masks = shape_constants()
    arrays, args = {}, []
    for name, a in [(n, np.ascontiguousarray(inputs[n])) for n in NAMES] + [("floats", floats), ("masks", masks)]:
        arrays[f"in_{name}"] = a
        args.append(nc.dram_tensor(f"in_{name}", a.shape, mybir.dt.from_np(a.dtype), kind="ExternalInput").ap())
    out = nc.dram_tensor("out_x", (1, T, D), mybir.dt.float32, kind="ExternalOutput").ap()
    rel_rows = nc.dram_tensor("rel_rows", (N_HEADS, P, S_REL), mybir.dt.float32, kind="Internal").ap()
    trunk(nc, *args, out, rel_rows)
    r = run_bass_kernel_spmd(nc, [arrays], core_ids=[0])
    return r.results[0]["out_x"]
```

```python
import math
from contextlib import ExitStack

import numpy as np
import concourse.bass as bass
from concourse import mybir

P = 128
T, D = 512, 1024
NT, KC = T // P, D // P
EPS = 1e-6
NEG = -1e30
TAKEN = -3e38

A_HEADS, A_HD = 4, 64
IDX_HEADS = 8
TOPK = min(256, T // 4)
B_HEADS, B_HD = 4, 128
C_HEADS, C_HD = 4, 64
CMP_BLOCK, CMP_STRIDE, N_CMP = 32, 16, (T - 32) // 16 + 1
PHI = 256
N_BUCKETS, EXACT, MAX_DIST = 32, 16, 128
N_HEADS = A_HEADS + C_HEADS

A_Q, A_CKV, A_QI, A_KI = 0, 256, 384, 896
B_BASE = 1224
B_AB = B_BASE + 1536
C_BASE = B_AB + 8 + 512
C_VSEL = C_BASE + 256 + 192
G_BASE = 4188

CHUNKS = [
    ("w_in", C_BASE, 448), ("w_in", C_VSEL, 460),
    ("w_in", A_Q, 384), ("w_in", A_QI, 512), ("w_in", A_KI, 328),
    ("phi", 0, PHI), ("phi", 1, PHI),
    ("w_in", B_BASE, 512), ("w_in", B_BASE + 512, 512), ("w_in", B_BASE + 1024, 512),
    ("w_in", B_AB, 260), ("w_in", B_AB + 260, 260),
    ("w_in", G_BASE, 512), ("w_in", G_BASE + D, 512), ("w_in", G_BASE + 2 * D, 512),
    ("w_in", G_BASE + 512, 512), ("w_in", G_BASE + D + 512, 512), ("w_in", G_BASE + 2 * D + 512, 512),
    ("w_branch", 0, 512), ("w_branch", 512, 512), ("w_out", 0, 512), ("w_out", 512, 512),
]
W_SCALE, Y_SCALE = 64.0, 1.0 / 16
STAGES, PAIRS = 3, 6
(CH_C0, CH_C1, CH_A0, CH_QI, CH_A2, CH_PK, CH_PV, CH_B0, CH_B1, CH_B2, CH_B3, CH_B4,
 CH_G0, CH_G1, CH_G2, CH_G3, CH_G4, CH_G5, CH_WB0, CH_WB1, CH_WO0, CH_WO1) = range(22)

R_NORM, R_CONV, R_CKV, R_AQ, R_AK, R_CQ, R_CK, R_BOUT, R_POS, N_ROWS = 0, 8, 56, 57, 58, 59, 60, 63, 64, 96
F_IDENT, F_TRI, F_SEEN, F_HOT, N_FLOAT = 0, 128, 256, 260, 260 + 640
LEVELS = 7
S_REL = 640


def shape_constants():
    f = np.zeros((P, N_FLOAT), np.float32)
    i = np.arange(P)
    f[:, F_IDENT:F_IDENT + P] = np.eye(P)
    f[:, F_TRI:F_TRI + P] = i[:, None] <= i[None, :]
    f[:, F_SEEN] = i >= CMP_BLOCK - 1
    f[:, F_SEEN + 1:F_SEEN + 4] = 1.0
    dist = T - 1 - np.arange(S_REL)
    ratio = np.log(np.maximum(dist, 1).astype(np.float32) / EXACT) / math.log(MAX_DIST / EXACT)
    large = np.minimum(EXACT + (ratio * (N_BUCKETS - EXACT)).astype(np.int32), N_BUCKETS - 1)
    bucket = np.where(dist < 0, N_BUCKETS, np.where(dist < EXACT, dist, large))
    f[0:N_BUCKETS + 1, F_HOT:F_HOT + S_REL] = bucket[None, :] == np.arange(N_BUCKETS + 1)[:, None]
    m = np.zeros((P, 2 * LEVELS, P), np.float32)
    for n in range(LEVELS):
        b = 1 << n
        same = i[:, None] // (2 * b) == i[None, :] // (2 * b)
        low = same & (i[:, None] // b % 2 == 1) & (i[None, :] // b % 2 == 0)
        m[:, n] = low
        m[:, LEVELS + n] = low.T
    return f, m


class Uses:

    def __init__(self, banks, names):
        self.banks = banks
        self.at = {n: i for i, n in enumerate(names)}
        assert len(self.at) == len(names)

    def bank(self, name):
        return self.banks[self.at[name] % len(self.banks)]

    def filled(self, name):
        return self.at[name] + 1

    def free(self, name):
        return self.at[name] + 1 - len(self.banks)


class Steps:

    def __init__(self, sem, names):
        self.sem = sem
        self.n = {n: i + 1 for i, n in enumerate(names)}
        assert len(self.n) == len(names)

    def wait(self, eng, name):
        eng.wait_ge(self.sem, self.n[name])


def trunk(nc, x, norm_g, w_in, a_kv_norm, a_w_ukv, a_q_norm, a_k_norm, b_conv, b_a_log, b_dt_bias, b_out_norm,
          c_q_norm, c_k_norm, c_cmp_pos, c_phi_w1, c_phi_w2, w_branch, w_out, rel_bias, floats, masks, out, rel_rows):
    f32 = mybir.dt.float32
    f16 = mybir.dt.float16
    u8 = mybir.dt.uint8
    ALU = mybir.AluOpType
    ACT = mybir.ActivationFunctionType
    AX = mybir.AxisListType
    ctx = ExitStack()
    with ctx:
        def sb(name, shape, dt=f32):
            return ctx.enter_context(nc.sbuf_tensor(name, shape, dt))

        def sem(name):
            return ctx.enter_context(nc.semaphore(name))

        hT_hi = sb("hT_hi", [P, KC, T], f16)
        hT_lo = sb("hT_lo", [P, KC, T], f16)
        stage = sb("stage", [P, STAGES, 1024])
        w_hi = sb("w_hi", [P, PAIRS, 1024], f16)
        w_lo = sb("w_lo", [P, PAIRS, 1024], f16)
        early = sb("early", [P, 6144])
        work = sb("work", [P, 6144])
        late = sb("late", [P, 4608])
        qkvT = sb("qkvT", [P, 12, T + 3])
        strips = sb("strips", [P, N_HEADS, T])
        cmp_strip = sb("cmp_strip", [P, C_HEADS, NT, N_CMP])
        raw_a2 = sb("raw_a2", [P, NT, 328])
        raw_b = sb("raw_b", [P, NT, 520])
        raw_c1 = sb("raw_c1", [P, NT, 460])
        v_a = sb("v_a", [P, NT, 256])
        qT_a = sb("qT_a", [P, 2, T])
        kT_a = sb("kT_a", [P, 2, T])
        qT_c = sb("qT_c", [P, 2, T])
        kT_sel = sb("kT_sel", [P, T])
        kT_win = sb("kT_win", [P, T])
        consts = sb("consts", [P, F_HOT])
        level_masks = sb("level_masks", [P, 2 * LEVELS, P], u8)
        ones = sb("ones", [P, P])
        par = sb("par", [P, N_ROWS])
        small = sb("small", [P, 600])
        kcT = sb("kcT", [P, N_CMP + 1])
        cmp_v = sb("cmp_v", [N_CMP, 64])
        g_scale = sb("g_scale", [P, 16, 12])

        ident = consts[:, F_IDENT:F_IDENT + P]
        tri = consts[:, F_TRI:F_TRI + P]
        seen = consts[:, F_SEEN:F_SEEN + 4]

        x_in = early[:, 0:4096].rearrange("p (t d) -> p t d", t=NT)
        rel_row = work[0:N_HEADS, 0:S_REL]
        hot = work[:, S_REL:2 * S_REL]
        rel33 = work[0:N_BUCKETS + 1, 1280:1280 + N_HEADS]
        par_rows = work[0:N_ROWS, 1288:1288 + P]
        squares = early[:, 0:2048]
        conv_acc = early[:, 2048:3072].rearrange("p (b n) -> p b n", b=2)
        raw_c0 = early[:, 3072:4864].rearrange("p (t n) -> p t n", t=NT)
        blocks = early[:, 4864:5856].rearrange("p (v c n) -> p v c n", v=2, c=16)
        hidT = early[:, 5856:5980].rearrange("p (v n) -> p v n", v=4)
        gates = early[:, 0:6144].rearrange("p (g n) -> p g n", g=12)
        raw_a0 = work[:, 0:1536].rearrange("p (t n) -> p t n", t=NT)
        qiT = work[:, 1536:3072].rearrange("p (m n) -> p m n", m=4)
        ukv = work[:, 3072:3584]
        ckvT = work[:, 3584:4096]
        kiT = work[:, 4096:4608]
        mask_floats = work[:, 3584:3584 + 2 * LEVELS * P].rearrange("p (n m) -> p n m", m=P)
        phi2 = work[:, 5632:5888].rearrange("p (k n) -> p k n", k=4)
        k_raw = work[:, 4608:5632].rearrange("p (t n) -> p t n", t=NT)
        merged_parts = work[:, 0:4096].bitcast(f16).rearrange("p (c a n) -> p c a n", c=KC, a=2)
        o_c = work[:, 3584:4608].rearrange("p (t n) -> p t n", t=NT)

        def slot(t, n):
            return t[:, 512 * n:512 * n + 512].rearrange("p (h n) -> p h n", h=4)

        (g_tri, decay, decay_k, neg_nT, t_inv, t_invT, z_sb, v_tok, k_tok, attnT, resid, v_new) = (
            slot(work, n) for n in range(12))
        o_state, o_tok, state, o_sq, decay_n, u_scr = (slot(late, n) for n in range(6))
        scores = [late[:, 0:256], late[:, 256:640], early[:, 4608:5120]]
        topk_work = [late[:, 1152:1664], late[:, 1664:2176]]
        topk_work_last = [early[:, 5120:5632], early[:, 5632:6144]]
        relu_buf = [late[:, 2176:2688], late[:, 2688:3200]]
        probs = [late[:, 512 * n:512 * n + 512] for n in range(2)]
        probsT = [late[:, 1024 + 512 * n:1536 + 512 * n] for n in range(2)]
        bias_sel = [late[:, 2048 + 512 * n:2560 + 512 * n] for n in range(2)]
        keep_add = [late[:, 3456:3712], late[:, 3712:4096], late[:, 4096:4608]]
        x_again = late[:, 0:4096].rearrange("p (t d) -> p t d", t=NT)
        qkv_flat = qkvT[:, :, :].rearrange("p a b -> p (a b)")
        h_full = qkv_flat[:, 0:4096].rearrange("p (c n) -> p c n", c=KC)
        gates_b = qkv_flat[:, 0:6144].rearrange("p (g n) -> p g n", g=12)
        yT_parts = strips[:, :, :].bitcast(f16).rearrange("p c (a n) -> p c a n", a=2)
        cmp_p = work[:, 0:496]
        cmp_pT = work[0:N_CMP, 512:2560].rearrange("p (u n) -> p u n", u=16)

        col = [0]

        def cols(n):
            col[0] += n
            return small[:, col[0] - n:col[0]]

        banks = [ctx.enter_context(nc.psum_tensor(f"bank{n}", [P, 512], f32)) for n in range(8)]
        s_names = [(c, t) for c in ("C0", "C1", "A0", "QI", "A2", "B0") for t in range(4)]
        s_names += [("idx", q, h) for q in range(1, NT) for h in range(IDX_HEADS)]
        s_names += [(c, t) for c in ("B1", "B2", "B3", "B4") for t in range(4)]
        s_names += [("cp", q) for q in range(4)]
        units = [(m, q, h) for m in "A" for q in range(NT) for h in range(4)]
        units += [(m, q, h) for q in range(NT) for m in ("sel", "win") for h in range(4)]
        groups = [u[:2] for u in units[::4]]
        s_names += [("pT", *u) for u in units]
        S = Uses(banks[0:2], s_names)
        G = Uses(banks[2:4], range(24))
        v_names = ["par"] + [("x", t, a) for t in range(NT) for a in range(2)] + ["rel0", "rel1"]
        v_names += ["cqT0", "cqT1", "kcmp", "vcmp", "ksT", "kwT"]
        v_names += ["ckvT", "qT0", "qT1"] + [("ukv", t) for t in range(NT)] + ["kT0", "kT1", "kiT", "cmpkv", "kcT", "sums"]
        for c in range(NT):
            v_names += [(n, c) for n in ("gc", "kt", "vt", "kk", "qk", "n")]
            for l in range(1, LEVELS):
                v_names += [("z", c, l), ("ut", c, l)] + ([("u", c, l)] if l < LEVELS - 1 else [])
            v_names += ([("ks", c)] if c else []) + [("x2", c), ("o", c)] + ([("st", c)] if c < NT - 1 else [])
        v_names += ["cl0", "cl1"] + [("lg", *u) for u in units]
        v_names += [("yT", f) for f in range(KC)]
        v_names += [("br", j, b) for j in range(KC) for b in range(3)] + [("wo", n, t) for n in range(2) for t in range(NT)]
        V = Uses(banks[4:6], v_names)
        O = Uses(banks[6:8], [("os", c) for c in range(1, NT)] + [("oc", n) for n in range(2)] + [("o", *g) for g in groups])

        s_filled, s_drained = sem("scalar_banks_filled"), sem("scalar_banks_drained")
        v_filled, v_drained = sem("vector_banks_filled"), sem("vector_banks_drained")
        o_filled, o_drained = sem("out_banks_filled"), sem("out_banks_drained")
        g_filled, g_drained = sem("gate_banks_filled"), sem("gate_banks_drained")
        w_loaded = [sem(f"weights_loaded{n}") for n in range(STAGES)]
        scaled, hi_ready, lo_ready = sem("weights_scaled"), sem("weights_hi_ready"), sem("weights_lo_ready")
        hid_filled, hid_ready = sem("hidden_banks_filled"), sem("hidden_ready")
        pair_used, phi_used = sem("weight_pairs_used"), sem("phi_weights_used")
        x_loaded = [sem(f"x_loaded{t}") for t in range(NT)]
        in_loaded = sem("parameters_loaded")
        const_loaded = sem("constants_loaded")
        ukv_loaded = sem("ukv_loaded")
        fills = sem("fills_done")
        hot_ready = sem("rel_table_ready")
        row_stored, strips_loaded, cmp_strip_ready = sem("rel_rows_stored"), sem("strips_loaded"), sem("cmp_strip_ready")
        x_reloaded, out_stored = sem("x_reloaded"), sem("out_stored")
        v_step, p_step, a_step = sem("vector_step"), sem("pool_step"), sem("scalar_step")
        roots = ["x0", "x1", "x2", "x3", "C0", "C1", "A0", "Ak", "kc", "B"] + [("ob", c) for c in range(NT)]
        ROOT_IN = Steps(sem("root_input_ready"), roots)
        ROOT_OUT = Steps(sem("root_ready"), roots)
        SQ = Steps(sem("squares_ready"), ["C0", "C1", "A0", "Ak"] + [("B", m) for m in range(8)] + [("ob", c) for c in range(NT)])
        ssx_ready, h_ready, h_full_ready = sem("x_square_sums_ready"), sem("h_ready"), sem("hT_full_ready")
        h_hi_ready, h_lo_ready = sem("hT_hi_ready"), sem("hT_lo_ready")
        rows_ready = sem("rel_rows_ready")
        conv_ready, conv_done = sem("conv_ready"), sem("conv_silu_done")
        T_IN = Steps(sem("transpose_input_ready"), ["C0q", "C0blk", "C0ks", "C1kw", "A0ckv", "A0q", "Ak", "Aki", "kc"])
        score_ready, diag_ready = sem("score_ready"), sem("diagonal_masked")
        relu_used = sem("relu_used")
        keep_ready = sem("keep_ready")
        GATE_IN = Steps(sem("decay_input_ready"), ["g", "gc2"])
        GATE_OUT = Steps(sem("decay_exp_ready"), ["beta", "expa", "sp", "exps"])
        z_ready, sums_taken, gsum_ready = sem("z_gates_ready"), sem("squares_summed"), sem("log_decay_ready")
        gtri_ready = sem("cumulative_input_ready")
        diff_ready, exp_ready, decays_ready = sem("decay_difference_ready"), sem("decay_ready"), sem("decays_masked")
        g_names = []
        for c in range(NT):
            g_names += [(n, c) for n in ("kt", "nnt", "attn", "tt0")]
            for l in range(1, LEVELS):
                g_names += [("z", c, l), ("tt", c, l)] + ([("t", c, l)] if l < LEVELS - 1 else [])
            g_names += [("resid", c), ("vnew", c), ("oraw", c)] + ([("state", c)] if c < NT - 1 else [])
        GD = Steps(sem("deltanet_ready"), g_names)
        eye_ready = sem("inverse_reset")
        o_scaled = sem("deltanet_output_scaled")
        y_b = sem("y_b_ready")
        cl_ready, cexp_ready = sem("cmp_logits_ready"), sem("cmp_exp_ready")
        logits_ready, probs_ready, pv_done = sem("logits_ready"), sem("probs_ready"), sem("probsT_used")
        bias_ready = sem("selected_bias_ready")
        o_norm, y_ready = sem("output_normalised"), sem("y_ready")
        merge_ready, sum_ready, merged_ready = sem("branch_gated"), sem("branches_added"), sem("merged_ready")
        yT_hi_ready, m_hi_ready = sem("yT_hi_ready"), sem("merged_hi_ready")
        out_ready = sem("out_ready")

        ss_x, ss_a, ss_k = cols(4), cols(20), cols(16)
        ss_c, ss_w, ss_kc, ss_b, ss_o = cols(20), cols(4), cols(1), cols(32), cols(16)
        root = cols(32)
        newton = cols(32)
        max8 = cols(16)
        beta_t, g_t, sp_a, sp_b, neg_exp_a, dt_b = cols(16), cols(16), cols(16), cols(16), cols(4), cols(4)
        rq, rk, nk = cols(16), cols(16), cols(16)
        sums_sb = cols(64)
        mx, nmx, rsum, gsum = cols(48), cols(48), cols(48), cols(4)
        cmx, crs = cols(16), cols(16)
        fac = cols(4)
        bout_s = cols(1)
        (gc_, gl_, egc, negegc, egl, ekd, kd_s, n_s, a_s, rqs) = (g_scale[:, :, n] for n in range(10))
        assert col[0] <= 600, col[0]

        def bc(ap, n):
            return ap.unsqueeze(2).to_broadcast([ap.shape[0], ap.shape[1], n])

        def heads(ap, c):
            return bc(ap[:, 4 * c:4 * c + 4], P)

        def over_heads(ap):
            return ap.unsqueeze(1).to_broadcast([P, 4, P])

        order = [(c, j) for c in range(CH_A2 + 1) for j in range(4)]
        for v, c in ((CH_PK, CH_B0), (CH_PV, CH_B1)):
            order += [(v, 0), (c, 0), (v, 1), (c, 1), (v, 2), (c, 2), (c, 3), (v, 3)]
        order += [(c, j) for c in range(CH_B2, len(CHUNKS)) for j in range(4)]
        pieces, n_pairs, n_phi = [], 0, 0
        for c, j in order:
            phi_piece = CHUNKS[c][0] == "phi"
            pieces.append((c, j, n_phi if phi_piece else n_pairs))
            n_phi, n_pairs = n_phi + phi_piece, n_pairs + (not phi_piece)
        piece_at = {(c, j): n for n, (c, j, _) in enumerate(pieces)}
        pair_at = {(c, j): k for c, j, k in pieces if CHUNKS[c][0] != "phi"}
        split_chunks = [c for c in range(len(CHUNKS)) if CHUNKS[c][0] != "phi"]
        GATE_CHUNKS = (CH_G0, CH_G1, CH_G2, CH_G3, CH_G4, CH_G5)

        def after(c):
            return split_chunks[split_chunks.index(c) + 1]

        FOLLOW = ((0,), (1,), (2, 3), ())
        WITH_GATE = ((0,), (1,), (), (2, 3))

        def attention_splits(u):
            g = 12 + u // 4
            c = GATE_CHUNKS[g // 4]
            if g % 4 == 3:
                return [(after(c), 2 + u % 4 - 1)] if u % 4 in (1, 2) else []
            return [(after(c), g % 4)] if u % 4 == 3 and g % 4 < 2 else []

        def final_splits(j):
            c = CH_WB0 if j < 4 else CH_WB1
            return [(after(c), k) for k in FOLLOW[j % 4]]

        def gate_tile(j, b):
            return gates[:, 4 * b + j, :] if j < 4 else gates_b[:, 4 * b + j - 4, :]

        def piece_view(t, c, n_rows=2):
            n = CHUNKS[c][2]
            return t[:, 0:n_rows * n].rearrange("p (k n) -> p k n", k=n_rows)

        block = ctx.enter_context(nc.Block())

        @block.sync
        def _(sp):
            for t in range(NT):
                sp.dma_start(x_in[:, t, :], x[0, t * P:(t + 1) * P, :]).then_inc(x_loaded[t], 16)

            def load(n):
                c, j, k = pieces[n]
                src, c0, width = CHUNKS[c]
                if n >= STAGES:
                    pc, _, pk = pieces[n - STAGES]
                    sp.wait_ge(phi_used if CHUNKS[pc][0] == "phi" else lo_ready, pk + 1)
                if src == "phi":
                    dst = piece_view(stage[:, n % STAGES, :], c, 4)
                    ap = c_phi_w1[0, c0].rearrange("(k p) n -> p k n", p=P)[:, 4 * j:4 * j + 4, :]
                else:
                    dst = piece_view(stage[:, n % STAGES, :], c)
                    ap = {"w_in": w_in, "w_branch": w_branch, "w_out": w_out}[src][0].rearrange(
                        "(k p) n -> p k n", p=P)[:, 2 * j:2 * j + 2, c0:c0 + width]
                sp.dma_start(dst, ap).then_inc(w_loaded[n % STAGES], 16)

            for n in range(2 * STAGES):
                load(n)
            sp.wait_ge(rows_ready, 1)
            sp.dma_start(rel_rows[:, :, :], rel_row.unsqueeze(1).to_broadcast([N_HEADS, P, S_REL])).then_inc(row_stored, 16)
            sp.wait_ge(row_stored, 16)
            sp.dma_start(strips[:, :, :], bass.AP(rel_rows.tensor, P - 1, [[S_REL - 1, P], [P * S_REL, N_HEADS], [1, T]])).then_inc(strips_loaded, 16)
            for n in range(2 * STAGES, piece_at[CH_WO0, 0]):
                load(n)
            sp.wait_ge(y_ready, NT * 2)
            sp.dma_start(x_again, x[0].rearrange("(t p) d -> p t d", p=P)).then_inc(x_reloaded, 16)
            for n in range(piece_at[CH_WO0, 0], len(pieces)):
                load(n)
            for n in range(2):
                for t in range(NT):
                    sp.wait_ge(out_ready, NT * n + t + 1)
                    sp.dma_start(out[0, t * P:(t + 1) * P, 512 * n:512 * n + 512],
                                 x_again[:, t, 512 * n:512 * n + 512]).then_inc(out_stored, 16)
            sp.wait_ge(out_stored, 16 * 2 * NT)

        @block.gpsimd
        def _(gp):
            step = [0]

            def hold(ins):
                step[0] += 1
                ins.then_inc(p_step, 1)
                gp.wait_ge(p_step, step[0])

            gp.memset(ones[:, :], 1.0).then_inc(fills, 1)
            gp.memset(cmp_strip[:, :, :, :], NEG).then_inc(fills, 1)
            def lo_split(c, j):
                k = pair_at[c, j]
                gp.wait_ge(hi_ready, k + 1)
                gp.tensor_tensor(piece_view(w_lo[:, k % PAIRS, :], c), piece_view(stage[:, piece_at[c, j] % STAGES, :], c),
                                 piece_view(w_hi[:, k % PAIRS, :], c), ALU.subtract).then_inc(lo_ready, 1)

            def follow(c, t):
                for j in FOLLOW[t]:
                    lo_split(after(c), j)

            gp.wait_ge(fills, 2)
            hold(gp.memset(work[N_BUCKETS:N_BUCKETS + 1, 1280:1280 + N_HEADS], NEG))
            gp.nop().then_inc(hot_ready, 1)
            gp.wait_ge(const_loaded, 16 * 7)
            hold(gp.tensor_copy(level_masks[:, :, :], mask_floats))
            for j in range(4):
                lo_split(CH_C0, j)
            gp.wait_ge(h_lo_ready, 2 * NT)
            gp.memset(qkvT[:, :, 0:3], 0.0).then_inc(fills, 1)
            for t in range(4):
                follow(CH_C0, t)
            gp.wait_ge(s_drained, S.filled(("C0", 3)))
            sq_c = squares[:, 0:1280].rearrange("p (t g d) -> p t g d", t=NT, d=64)
            gp.tensor_tensor(sq_c[:, :, 0:4, :], raw_c0[:, :, 0:256].rearrange("p t (g d) -> p t g d", d=64),
                             raw_c0[:, :, 0:256].rearrange("p t (g d) -> p t g d", d=64), ALU.mult)
            gp.tensor_tensor(sq_c[:, :, 4, :], raw_c0[:, :, 384:448], raw_c0[:, :, 384:448], ALU.mult).then_inc(SQ.sem, 1)
            for t in range(4):
                follow(CH_C1, t)
            gp.wait_ge(s_drained, S.filled(("C1", 3)))
            sq_w = squares[:, 1280:1536].rearrange("p (t d) -> p t d", t=NT)
            gp.tensor_tensor(sq_w, raw_c1[:, :, 64:128], raw_c1[:, :, 64:128], ALU.mult).then_inc(SQ.sem, 1)
            for t in range(4):
                follow(CH_A0, t)
            gp.wait_ge(s_drained, S.filled(("A0", 3)))
            gp.wait_ge(v_filled, V.filled("kwT"))
            gp.tensor_tensor(squares[:, 0:1536], work[:, 0:1536], work[:, 0:1536], ALU.mult).then_inc(SQ.sem, 1)
            for t in range(4):
                follow(CH_QI, t)
            gp.wait_ge(v_drained, V.filled(("ukv", 3)))
            kf = work[:, 4608:5632]
            gp.tensor_tensor(squares[:, 0:1024], kf, kf, ALU.mult).then_inc(SQ.sem, 1)
            gp.wait_ge(strips_loaded, 16)
            for q in range(NT):
                n = min(N_CMP, 7 + 8 * q)
                first = 415 - P * q
                ins = gp.tensor_copy(cmp_strip[:, :, q, 0:n], strips[:, A_HEADS:, first:first + 16 * (n - 1) + 1:16])
            ins.then_inc(cmp_strip_ready, 1)
            for c in (CH_A2, CH_B0):
                for t in range(4):
                    follow(c, t)
            for q in range(1, NT):
                gp.wait_ge(score_ready, q)
                d = scores[q - 1][:, P * q:P * q + P]
                gp.affine_select(out=d, in_=d, compare_op=ALU.is_ge, fill=NEG, base=0, pattern=[[-1, P]],
                                 channel_multiplier=1).then_inc(diag_ready, 1)
            def squares_b(m):
                gp.wait_ge(conv_done, m + 1)
                if m >= 4:
                    gp.wait_ge(sums_taken, m - 3)
                gp.tensor_tensor(squares[:, 512 * (m % 4):512 * (m % 4) + 512], qkvT[:, m, 3:T + 3], qkvT[:, m, 3:T + 3],
                                 ALU.mult).then_inc(SQ.sem, 1)

            for c in (CH_B1, CH_B2, CH_B3, CH_B4):
                for t in range(4):
                    follow(c, t)
                if c == CH_B2:
                    for m in range(4):
                        squares_b(m)
            for m in range(4, 8):
                squares_b(m)
            for c in range(NT):
                if c == 0:
                    GATE_IN.wait(gp, "gc2")
                else:
                    gp.wait_ge(v_filled, V.filled(("gc", c - 1)))
                gp.tensor_tensor(g_tri, over_heads(tri), heads(g_t, c), ALU.mult).then_inc(gtri_ready, 1)
                if c > 0:
                    gp.wait_ge(v_filled, V.filled(("x2", c - 1)))
                    GD.wait(gp, ("tt", c - 1, LEVELS - 1))
                gp.tensor_copy(t_inv, over_heads(ident)).then_inc(eye_ready, 1)
                gp.tensor_copy(t_invT, over_heads(ident)).then_inc(eye_ready, 1)
                gp.wait_ge(exp_ready, c + 1)
                if c > 0:
                    gp.wait_ge(v_filled, V.filled(("o", c - 1)))
                hold(gp.tensor_tensor(decay_k, decay, over_heads(tri), ALU.mult))
                gp.tensor_tensor(decay_n, decay_k, heads(n_s, c), ALU.mult).then_inc(decays_ready, 1)
                gp.tensor_tensor(attnT, decay_k, heads(rk, c), ALU.mult).then_inc(decays_ready, 1)
                for g in range(3 * c, 3 * c + 3):
                    for j in WITH_GATE[g % 4]:
                        lo_split(after(GATE_CHUNKS[g // 4]), j)
                GD.wait(gp, ("oraw", c))
                hold(gp.tensor_tensor(o_tok, o_tok, heads(rqs, c), ALU.mult))
                gp.tensor_tensor(o_sq, o_tok, o_tok, ALU.mult).then_inc(SQ.sem, 1)
                gp.wait_ge(o_scaled, c + 1)
                gp.wait_ge(z_ready, 1)
                zb = raw_b[:, c, 8:520].rearrange("p (h d) -> p h d", h=4)
                gp.tensor_tensor(zb, zb, o_tok, ALU.mult).then_inc(y_b, 1)
            def join(u):
                m, q, h = units[u]
                if u == 4:
                    gp.wait_ge(y_b, NT)
                elif u >= 6:
                    gp.wait_ge(logits_ready, u - 1)
                L = P * (q + 1)
                gp.tensor_tensor(bias_sel[u % 2][:, 0:L], strips[:, h, T - L:T], keep_add[q - 1], ALU.add).then_inc(bias_ready, 1)

            def gate_z(g):
                m, q = groups[g]
                z = raw_a2[:, q, 72:328] if m == "A" else raw_c1[:, q, 204:460]
                if m != "sel":
                    gp.wait_ge(o_norm, g + 1)
                    gp.tensor_tensor(z, z, o_c[:, q, :], ALU.mult).then_inc(y_ready, 1)

            join(4)
            join(5)
            for u in range(len(units)):
                if u >= 4 and u + 2 < 16:
                    join(u + 2)
                for c, j in attention_splits(u):
                    lo_split(c, j)
                if u % 4 == 3 and u >= 7:
                    gate_z(u // 4 - 1)
            gate_z(len(groups) - 1)
            for j in range(KC):
                gp.wait_ge(merge_ready, j + 1)
                a, b, c_ = (gate_tile(j, b) for b in range(3))
                hold(gp.tensor_tensor(a, a, b, ALU.add))
                gp.tensor_tensor(a, a, c_, ALU.add).then_inc(sum_ready, 1)
                for c, k in final_splits(j):
                    lo_split(c, k)
            for t in range(4):
                follow(CH_WO0, t)

        @block.scalar
        def _(act):
            for src, dst in (
                (norm_g[0].rearrange("(k p) -> k p", p=P), par_rows[R_NORM:R_NORM + 8, :]),
                (b_conv[0].rearrange("w (m p) -> w m p", p=P)[0], par_rows[R_CONV:R_CONV + 12, :]),
                (b_conv[0].rearrange("w (m p) -> w m p", p=P)[1], par_rows[R_CONV + 12:R_CONV + 24, :]),
                (b_conv[0].rearrange("w (m p) -> w m p", p=P)[2], par_rows[R_CONV + 24:R_CONV + 36, :]),
                (b_conv[0].rearrange("w (m p) -> w m p", p=P)[3], par_rows[R_CONV + 36:R_CONV + 48, :]),
                (a_kv_norm, par_rows[R_CKV:R_CKV + 1, :]),
                (a_q_norm, par_rows[R_AQ:R_AQ + 1, 0:64]), (a_q_norm, par_rows[R_AQ:R_AQ + 1, 64:128]),
                (a_k_norm, par_rows[R_AK:R_AK + 1, 0:64]), (a_k_norm, par_rows[R_AK:R_AK + 1, 64:128]),
                (c_q_norm, par_rows[R_CQ:R_CQ + 1, 0:64]), (c_q_norm, par_rows[R_CQ:R_CQ + 1, 64:128]),
                (c_k_norm[0], par_rows[R_CK:R_CK + 3, 0:64]), (c_k_norm[0], par_rows[R_CK:R_CK + 3, 64:128]),
                (b_out_norm, par_rows[R_BOUT:R_BOUT + 1, :]),
                (c_cmp_pos[0].rearrange("v (c a) d -> (v c) (a d)", a=2), par_rows[R_POS:R_POS + 32, :]),
            ):
                act.dma_start(dst, src).then_inc(in_loaded, 16)
            for src, dst in (
                (floats[:, 0:F_HOT], consts[:, :]), (floats[:, F_HOT:N_FLOAT], hot), (masks, mask_floats),
                (rel_bias, rel33[0:N_BUCKETS, :]),
                (b_dt_bias.to_broadcast([P, 4]), dt_b), (b_a_log.to_broadcast([P, 4]), neg_exp_a),
                (c_phi_w2[0].rearrange("v (k p) n -> p (v k) n", p=P), phi2),
            ):
                act.dma_start(dst, src).then_inc(const_loaded, 16)
            act.dma_start(ukv, a_w_ukv[0]).then_inc(ukv_loaded, 16)
            step = [0]

            def hold(ins):
                step[0] += 1
                ins.then_inc(a_step, 1)
                act.wait_ge(a_step, step[0])

            def sqrt(name, src, n):
                ROOT_IN.wait(act, name)
                nc.scalar.activation(root[0:src.shape[0], 0:n], src, ACT.Sqrt).then_inc(ROOT_OUT.sem, 1)

            def drain(name, dst, n=512, func=ACT.Copy, rows=P, scale=1.0):
                act.wait_ge(s_filled, S.filled(name))
                nc.scalar.activation(dst, S.bank(name)[0:rows, 0:n], func, scale=scale).then_inc(s_drained, 1)

            def hi_split(c, j):
                n, k = piece_at[c, j], pair_at[c, j]
                act.wait_ge(w_loaded[n % STAGES], 16 * (n // STAGES + 1))
                full = piece_view(stage[:, n % STAGES, :], c)
                nc.scalar.activation(full, full, ACT.Copy, scale=W_SCALE).then_inc(scaled, 1)
                act.wait_ge(scaled, k + 1)
                if k >= PAIRS:
                    act.wait_ge(pair_used, k - PAIRS + 1)
                    act.wait_ge(lo_ready, k - PAIRS + 1)
                nc.scalar.activation(piece_view(w_hi[:, k % PAIRS, :], c), full, ACT.Copy).then_inc(hi_ready, 1)

            def follow(c, t):
                for j in FOLLOW[t]:
                    hi_split(after(c), j)

            def drain_chunk(c, name, dst, n=512):
                for t in range(4):
                    if t < 3:
                        drain((name, t), dst(t), n, scale=1.0 / W_SCALE)
                        follow(c, t)
                    else:
                        drain((name, t), dst(t), n, scale=1.0 / W_SCALE)

            def drain_gate(g):
                act.wait_ge(g_filled, G.filled(g))
                b, j = g // 4 % 3, g % 4 + 4 * (g // 12)
                nc.scalar.activation(gate_tile(j, b), G.bank(g)[:, :], ACT.Sigmoid, scale=1.0 / W_SCALE).then_inc(g_drained, 1)

            for t in range(NT):
                act.wait_ge(x_loaded[t], 16)
                nc.scalar.activation(late[:, D * t:D * t + D], x_in[:, t, :], ACT.Square, accum_out=ss_x[:, t:t + 1]).then_inc(ssx_ready, 1)
            for t in range(NT):
                sqrt(f"x{t}", ss_x[:, t:t + 1], 1)
            for j in range(4):
                hi_split(CH_C0, j)
            for n in range(2 * NT):
                act.wait_ge(h_full_ready, n + 1)
                t, a = n // 2, n % 2
                nc.scalar.activation(hT_hi[:, 4 * a:4 * a + 4, t * P:(t + 1) * P], h_full[:, 4 * a:4 * a + 4, t * P:(t + 1) * P],
                                     ACT.Copy).then_inc(h_hi_ready, 1)
            drain_chunk(CH_C0, "C0", lambda t: raw_c0[:, t, :], 448)
            drain_chunk(CH_C1, "C1", lambda t: raw_c1[:, t, :], 460)
            sqrt("C0", ss_c, 20)
            sqrt("C1", ss_w, 4)
            act.wait_ge(row_stored, 16)
            drain_chunk(CH_A0, "A0", lambda t: raw_a0[:, t, :], 384)
            sqrt("A0", ss_a, 20)
            drain_chunk(CH_QI, "QI", lambda t: qiT[:, t, :], 384)
            drain_chunk(CH_A2, "A2", lambda t: raw_a2[:, t, :], 328)
            sqrt("Ak", ss_k, 16)
            act.wait_ge(fills, 3)
            drain_chunk(CH_B0, "B0", lambda t: qkvT[:, t, 3:T + 3])
            act.wait_ge(hid_filled, 1)
            for h in range(2):
                ins = nc.scalar.activation(hidT[:, h::2, :], banks[2 + h][:, 0:2 * N_CMP].rearrange("p (v n) -> p v n", v=2), ACT.Silu)
            ins.then_inc(hid_ready, 1)
            n = 0
            for q in range(1, NT):
                for h in range(IDX_HEADS):
                    if n >= 2:
                        act.wait_ge(relu_used, n - 1)
                    L = P * (q + 1)
                    drain(("idx", q, h), relu_buf[n % 2][:, 0:L], L, ACT.Relu)
                    n += 1
            sqrt("kc", ss_kc[0:N_CMP, :], 1)

            def silu_conv(m):
                act.wait_ge(conv_ready, m + 1)
                nc.scalar.activation(qkvT[:, m, 3:T + 3], conv_acc[:, m % 2, :], ACT.Silu).then_inc(conv_done, 1)

            drain_chunk(CH_B1, "B1", lambda t: qkvT[:, 4 + t, 3:T + 3])
            for m in range(4):
                silu_conv(m)
            drain_chunk(CH_B2, "B2", lambda t: qkvT[:, 8 + t, 3:T + 3])
            for m in range(4, 8):
                silu_conv(m)
            drain_chunk(CH_B3, "B3", lambda t: raw_b[:, t, 0:260], 260)
            silu_conv(8)
            silu_conv(9)
            drain_chunk(CH_B4, "B4", lambda t: raw_b[:, t, 260:520], 260)
            silu_conv(10)
            silu_conv(11)
            act.wait_ge(s_drained, S.filled(("B4", 3)))
            nc.scalar.activation(raw_c1[:, :, 192:204], raw_c1[:, :, 192:204], ACT.Sigmoid)
            nc.scalar.activation(beta_t.rearrange("p (c h) -> p c h", c=NT), raw_b[:, :, 4:8], ACT.Sigmoid).then_inc(GATE_OUT.sem, 1)
            act.wait_ge(const_loaded, 16 * 7)
            nc.scalar.activation(neg_exp_a, neg_exp_a, ACT.Exp).then_inc(GATE_OUT.sem, 1)
            GATE_IN.wait(act, "g")
            hold(nc.scalar.activation(sp_b, sp_b, ACT.Exp, scale=-1.0))
            nc.scalar.activation(sp_b, sp_b, ACT.Ln, bias=1.0).then_inc(GATE_OUT.sem, 1)
            sqrt("B", ss_b, 32)
            GATE_IN.wait(act, "gc2")
            nc.scalar.activation(egc, gc_, ACT.Exp)
            nc.scalar.activation(egl, gl_, ACT.Exp)
            nc.scalar.activation(ekd, kd_s, ACT.Exp).then_inc(GATE_OUT.sem, 1)

            for c in range(NT):
                act.wait_ge(diff_ready, c + 1)
                hold(nc.scalar.activation(decay, decay, ACT.Relu, scale=-1.0))
                nc.scalar.activation(decay, decay, ACT.Exp, scale=-1.0).then_inc(exp_ready, 1)
                if c == 0:
                    for z in (raw_a2[:, :, 72:328], raw_c1[:, :, 204:460], raw_b[:, :, 8:520]):
                        ins = nc.scalar.activation(z, z, ACT.Silu)
                    ins.then_inc(z_ready, 1)
                for g in range(3 * c, 3 * c + 3):
                    if g == 0:
                        act.wait_ge(v_filled, V.filled("sums"))
                    if g % 4 != 3:
                        drain_gate(g)
                    for j in WITH_GATE[g % 4]:
                        hi_split(after(GATE_CHUNKS[g // 4]), j)
                    if g % 4 == 3:
                        drain_gate(g)
                if c > 0:
                    act.wait_ge(o_filled, O.filled(("os", c)))
                    if c > 1:
                        GD.wait(act, ("oraw", c - 1))
                    for h in range(4):
                        ins = nc.scalar.activation(o_state[:, h, :], O.bank(("os", c))[:, h * P:(h + 1) * P], ACT.Copy,
                                                   scale=egc[:, 4 * c + h:4 * c + h + 1])
                    ins.then_inc(o_drained, 1)
                sqrt(("ob", c), ss_o[:, 4 * c:4 * c + 4], 4)
            act.wait_ge(cl_ready, 1)
            nc.scalar.activation(cmp_p, cmp_p, ACT.Exp).then_inc(cexp_ready, 1)
            for q in range(NT):
                drain(("cp", q), cmp_pT[:, 4 * q:4 * q + 4, :].rearrange("p a b -> p (a b)"), rows=N_CMP)

            def exps(u):
                m, q, h = units[u]
                L = P * (q + 1)
                act.wait_ge(logits_ready, u + 1)
                nc.scalar.activation(probs[u % 2][:, 0:L], probs[u % 2][:, 0:L], ACT.Exp, bias=nmx[:, u:u + 1],
                                     accum_out=rsum[:, u:u + 1]).then_inc(probs_ready, 1)

            exps(0)
            for u, (m, q, h) in enumerate(units):
                if u + 1 < len(units):
                    exps(u + 1)
                L = P * (q + 1)
                if u >= 2:
                    act.wait_ge(pv_done, u - 1)
                drain(("pT", m, q, h), probsT[u % 2][:, 0:L], L)
                for c, j in attention_splits(u):
                    hi_split(c, j)
                if u % 4 == 3:
                    drain_gate(12 + u // 4)
            nc.scalar.activation(bout_s, par[:, R_BOUT:R_BOUT + 1], ACT.Copy, scale=Y_SCALE).then_inc(a_step, 1)
            act.wait_ge(a_step, 1)
            for f in range(KC):
                act.wait_ge(v_filled, V.filled(("yT", f)))
                nc.scalar.activation(yT_parts[:, f, 0, :], V.bank(("yT", f))[:, :], ACT.Copy,
                                     scale=bout_s if 2 <= f < 6 else Y_SCALE).then_inc(yT_hi_ready, 1)
            for j in range(KC):
                act.wait_ge(sum_ready, j + 1)
                nc.scalar.activation(merged_parts[:, j, 0, :], gate_tile(j, 0), ACT.Copy, scale=Y_SCALE).then_inc(m_hi_ready, 1)
                for c, k in final_splits(j):
                    hi_split(c, k)
            for t in range(4):
                follow(CH_WO0, t)

        @block.vector
        def _(ve):
            step = [0]
            count = {}

            def hold(ins):
                step[0] += 1
                ins.then_inc(v_step, 1)
                ve.wait_ge(v_step, step[0])

            def filled(name):
                ve.wait_ge(v_filled, V.filled(name))
                return V.bank(name)

            def inv_root(name, ss, n, inv_n, hold_last=True):
                rows = ss.shape[0]
                ve.tensor_scalar(ss, ss, inv_n, EPS, ALU.mult, ALU.add).then_inc(ROOT_IN.sem, 1)
                ROOT_OUT.wait(ve, name)
                y, w = root[0:rows, 0:n], newton[0:rows, 0:n]
                hold(ve.reciprocal(y, y))
                hold(ve.tensor_tensor(w, y, y, ALU.mult))
                hold(ve.tensor_tensor(w, w, ss, ALU.mult))
                hold(ve.tensor_scalar(w, w, -0.5, 1.5, ALU.mult, ALU.add))
                return y, w

            filled_par = filled("par")
            ve.tensor_copy(par[:, :], filled_par[:, 0:N_ROWS]).then_inc(v_drained, 1)
            ve.wait_ge(v_drained, 1)
            for t in range(NT):
                ve.wait_ge(ssx_ready, t + 1)
                s = ss_x[:, t:t + 1]
                y, w = inv_root(f"x{t}", s, 1, 1.0 / D)
                hold(ve.tensor_tensor(s, y, w, ALU.mult))
                ve.tensor_scalar(x_in[:, t, :], x_in[:, t, :], s, None, ALU.mult).then_inc(h_ready, 1)
            def h_lo(n):
                part = (slice(0, P), slice(4 * (n % 2), 4 * (n % 2) + 4), slice(n // 2 * P, n // 2 * P + P))
                ve.wait_ge(h_hi_ready, n + 1)
                ve.tensor_tensor(hT_lo[part], h_full[part], hT_hi[part], ALU.subtract).then_inc(h_lo_ready, 1)

            for t in range(NT):
                for a in range(2):
                    ps = filled(("x", t, a))[:, :].rearrange("p (k n) -> p k n", k=4)
                    ve.tensor_tensor(h_full[:, 4 * a:4 * a + 4, t * P:(t + 1) * P], ps,
                                     bc(par[:, R_NORM + 4 * a:R_NORM + 4 * a + 4], P), ALU.mult).then_inc(v_drained, 1)
                    ve.wait_ge(v_drained, V.filled(("x", t, a)))
                    ve.nop().then_inc(h_full_ready, 1)
                    if t or a:
                        h_lo(2 * t + a - 1)
            h_lo(2 * NT - 1)
            for n in range(2):
                ps = filled(f"rel{n}")
                ve.tensor_copy(rel_row[:, 320 * n:320 * n + 320], ps[0:N_HEADS, 0:320]).then_inc(v_drained, 1)
            ve.wait_ge(v_drained, V.filled("rel1"))
            ve.nop().then_inc(rows_ready, 1)

            SQ.wait(ve, "C0")
            hold(ve.tensor_reduce(ss_c, squares[:, 0:1280].rearrange("p (g d) -> p g d", d=64), AX.X, ALU.add))
            y, w = inv_root("C0", ss_c, 20, 1.0 / 64)
            hold(ve.tensor_tensor(ss_c, y, w, ALU.mult))
            ssc = ss_c.rearrange("p (t g) -> p t g", t=NT)
            for g in range(4):
                q_g = raw_c0[:, :, 64 * g:64 * g + 64]
                ins = ve.tensor_tensor(q_g, q_g, bc(ssc[:, :, g], 64), ALU.mult)
            ins.then_inc(T_IN.sem, 1)
            dup = squares[:, 0:2048].rearrange("p (s t a d) -> p s t a d", s=4, t=NT, a=2)
            T_IN.wait(ve, "C0q")
            SQ.wait(ve, "C1")
            hold(ve.tensor_reduce(ss_w, squares[:, 1280:1536].rearrange("p (t d) -> p t d", t=NT), AX.X, ALU.add))
            y, w = inv_root("C1", ss_w, 4, 1.0 / 64)
            hold(ve.tensor_tensor(ss_w, y, w, ALU.mult))
            for s in range(2):
                for a in range(2):
                    ins = ve.tensor_copy(dup[:, s, :, a, :], raw_c0[:, :, 256 + 64 * s:320 + 64 * s])
            ins.then_inc(T_IN.sem, 1)
            for a in range(2):
                ins = ve.tensor_tensor(dup[:, 2, :, a, :], raw_c0[:, :, 384:448], bc(ssc[:, :, 4], 64), ALU.mult)
            ins.then_inc(T_IN.sem, 1)
            for a in range(2):
                ins = ve.tensor_tensor(dup[:, 3, :, a, :], raw_c1[:, :, 64:128], bc(ss_w, 64), ALU.mult)
            ins.then_inc(T_IN.sem, 1)
            for m in range(2):
                ve.tensor_scalar(qT_c[:, m, :], filled(f"cqT{m}")[:, :], par[:, R_CQ:R_CQ + 1], C_HD ** -0.5,
                                 ALU.mult, ALU.mult).then_inc(v_drained, 1)
            for v, name in enumerate(("kcmp", "vcmp")):
                ps = filled(name)[:, :].rearrange("p (m q) -> p m q", q=16)
                for a in range(2):
                    for half in range(2):
                        src = ps[64 * a:64 * a + 64, half:half + N_CMP, a:16:2].rearrange("p m q -> p q m")
                        pos = par[64 * a:64 * a + 64, R_POS + 16 * v + 8 * half:R_POS + 16 * v + 8 * half + 8]
                        ins = ve.tensor_tensor(blocks[64 * a:64 * a + 64, v, 8 * half:8 * half + 8, :], src,
                                               bc(pos, N_CMP), ALU.add)
                ins.then_inc(v_drained, 1)
            ve.tensor_scalar(kT_sel[:, :], filled("ksT")[:, :], par[:, R_CK + 1:R_CK + 2], None, ALU.mult).then_inc(v_drained, 1)
            ve.tensor_scalar(kT_win[:, :], filled("kwT")[:, :], par[:, R_CK + 2:R_CK + 3], None, ALU.mult).then_inc(v_drained, 1)

            SQ.wait(ve, "A0")
            sq = squares[:, 0:1536].rearrange("p (t n) -> p t n", t=NT)
            ssq = ss_a.rearrange("p (t g) -> p t g", t=NT)
            ve.tensor_reduce(ssq[:, :, 0:4], sq[:, :, 0:256].rearrange("p t (g d) -> p t g d", d=64), AX.X, ALU.add)
            hold(ve.tensor_reduce(ssq[:, :, 4], sq[:, :, 256:384], AX.X, ALU.add))
            hold(ve.tensor_scalar(ssq[:, :, 4], ssq[:, :, 4], 0.5, None, ALU.mult))
            y, w = inv_root("A0", ss_a, 20, 1.0 / 64)
            hold(ve.tensor_tensor(ss_a, y, w, ALU.mult))
            ckv = raw_a0[:, :, 256:384]
            ve.tensor_tensor(ckv, ckv, bc(ssq[:, :, 4], P), ALU.mult).then_inc(T_IN.sem, 1)
            for g in range(4):
                q_g = raw_a0[:, :, 64 * g:64 * g + 64]
                ins = ve.tensor_tensor(q_g, q_g, bc(ssq[:, :, g], 64), ALU.mult)
            ins.then_inc(T_IN.sem, 1)
            ve.tensor_scalar(ckvT, filled("ckvT")[:, :], par[:, R_CKV:R_CKV + 1], None, ALU.mult).then_inc(v_drained, 1)
            for m in range(2):
                ve.tensor_scalar(qT_a[:, m, :], filled(f"qT{m}")[:, :], par[:, R_AQ:R_AQ + 1], A_HD ** -0.5,
                                 ALU.mult, ALU.mult).then_inc(v_drained, 1)
            for t in range(NT):
                ps = filled(("ukv", t))
                ve.tensor_copy(k_raw[:, t, :], ps[:, 0:256])
                ve.tensor_copy(v_a[:, t, :], ps[:, 256:512]).then_inc(v_drained, 1)
            SQ.wait(ve, "Ak")
            hold(ve.tensor_reduce(ss_k, squares[:, 0:1024].rearrange("p (g d) -> p g d", d=64), AX.X, ALU.add))
            y, w = inv_root("Ak", ss_k, 16, 1.0 / 64)
            hold(ve.tensor_tensor(ss_k, y, w, ALU.mult))
            kf = work[:, 4608:5632].rearrange("p (g d) -> p g d", d=64)
            ve.tensor_tensor(kf, kf, bc(ss_k, 64), ALU.mult).then_inc(T_IN.sem, 1)
            ve.wait_ge(s_drained, S.filled(("A2", 3)))
            ki2 = squares[:, 1024:1536].rearrange("p (t a d) -> p t a d", t=NT, a=2)
            for a in range(2):
                ins = ve.tensor_copy(ki2[:, :, a, :], raw_a2[:, :, 0:64])
            ins.then_inc(T_IN.sem, 1)
            hold(ve.tensor_scalar(raw_a2[:, :, 64:72], raw_a2[:, :, 64:72], IDX_HEADS ** -0.5, 64 ** -0.5, ALU.mult, ALU.mult))
            for m in range(2):
                ve.tensor_scalar(kT_a[:, m, :], filled(f"kT{m}")[:, :], par[:, R_AK:R_AK + 1], None, ALU.mult).then_inc(v_drained, 1)
            ve.tensor_copy(kiT, filled("kiT")[:, :]).then_inc(v_drained, 1)
            ve.wait_ge(v_drained, V.filled("kiT"))
            n = 0
            for q in range(1, NT):
                L = P * (q + 1)
                for h in range(IDX_HEADS):
                    ve.wait_ge(s_drained, S.filled(("idx", q, h)))
                    r, wi = relu_buf[n % 2][:, 0:L], raw_a2[:, q, 64 + h:65 + h]
                    if h == 0:
                        ins = ve.tensor_scalar(scores[q - 1], r, wi, None, ALU.mult)
                    else:
                        ins = ve.scalar_tensor_tensor(scores[q - 1], r, wi, scores[q - 1], ALU.mult, ALU.add)
                    n += 1
                    ins.then_inc(relu_used, 1)
                    ve.wait_ge(relu_used, n)
                ve.nop().then_inc(score_ready, 1)

            def conv(m):
                name = (("B0", "B1", "B2")[m // 4], m % 4)
                ve.wait_ge(s_drained, S.filled(name))
                if m >= 2:
                    ve.wait_ge(conv_done, m - 1)
                acc = conv_acc[:, m % 2, :]
                tap = [par[:, R_CONV + 12 * w + m:R_CONV + 12 * w + m + 1] for w in range(4)]
                hold(ve.tensor_scalar(acc, qkvT[:, m, 0:T], tap[0], None, ALU.mult))
                for w in range(1, 4):
                    ins = ve.scalar_tensor_tensor(acc, qkvT[:, m, w:w + T], tap[w], acc, ALU.mult, ALU.add)
                    if w < 3:
                        hold(ins)
                ins.then_inc(conv_ready, 1)

            ps = filled("cmpkv")
            kc, vc, kc2 = raw_c0[0:N_CMP, 1, 0:64], cmp_v[:, :], raw_c0[0:N_CMP, 1, 64:128]
            ve.tensor_copy(kc, ps[0:N_CMP, 0:64])
            ve.tensor_copy(vc, ps[0:N_CMP, 64:128]).then_inc(v_drained, 1)
            ve.wait_ge(v_drained, V.filled("cmpkv"))
            hold(ve.tensor_tensor(kc2, kc, kc, ALU.mult))
            s = ss_kc[0:N_CMP, :]
            hold(ve.tensor_reduce(s, kc2, AX.X, ALU.add))
            y, w = inv_root("kc", s, 1, 1.0 / 64)
            hold(ve.tensor_tensor(s, y, w, ALU.mult))
            kdup = raw_c0[0:N_CMP, 0, 0:128]
            for a in range(2):
                ins = ve.tensor_scalar(kdup[:, 64 * a:64 * a + 64], kc, s, None, ALU.mult)
            ins.then_inc(T_IN.sem, 1)
            def topk(q):
                ve.wait_ge(diag_ready, q)
                src = scores[q - 1]
                for r in range(TOPK // 8):
                    m8 = max8[:, 8 * (r % 2):8 * (r % 2) + 8]
                    hold(ve.max(m8, src))
                    dst = (topk_work_last if q == NT - 1 else topk_work)[r % 2][:, 0:P * (q + 1)]
                    hold(ve.match_replace(dst, m8, src, TAKEN))
                    src = dst
                    if r < TOPK // 8 - 1:
                        yield
                hold(ve.tensor_scalar(src, src, TAKEN, -NEG, ALU.is_equal, ALU.mult))
                ve.tensor_scalar(keep_add[q - 1], src, NEG, None, ALU.add).then_inc(keep_ready, 1)
                yield

            for q in range(1, NT - 1):
                for _ in topk(q):
                    pass
                for m in range(4 * q - 4, 4 * q):
                    conv(m)
                if q == 1:
                    ve.tensor_scalar(kcT[:, 0:N_CMP], filled("kcT")[:, 0:N_CMP], par[:, R_CK:R_CK + 1], None, ALU.mult).then_inc(v_drained, 1)

            for m in range(8, 12):
                conv(m)
            topk_last = topk(NT - 1)

            ve.wait_ge(const_loaded, 16 * 7)
            sa = sp_a.rearrange("p (c h) -> p c h", c=NT)
            hold(ve.tensor_tensor(sa, raw_b[:, :, 0:4], dt_b.unsqueeze(1).to_broadcast([P, NT, 4]), ALU.add))
            hold(ve.scalar_tensor_tensor(sp_b, sp_a, -1.0, sp_a, ALU.mult, ALU.max))
            hold(ve.tensor_scalar(sp_a, sp_a, 0.0, None, ALU.max))
            ve.nop().then_inc(GATE_IN.sem, 1)
            GATE_OUT.wait(ve, "sp")
            hold(ve.tensor_tensor(sp_a, sp_a, sp_b, ALU.add))
            gt = g_t.rearrange("p (c h) -> p c h", c=NT)
            hold(ve.tensor_tensor(gt, sa, neg_exp_a.unsqueeze(1).to_broadcast([P, NT, 4]), ALU.mult))
            hold(ve.tensor_scalar(g_t, g_t, -1.0, None, ALU.mult))
            ve.nop().then_inc(gsum_ready, 1)
            ps = filled("sums")
            ve.tensor_copy(sums_sb, ps[:, 0:64]).then_inc(v_drained, 1)
            ve.wait_ge(v_drained, V.filled("sums"))
            ve.tensor_copy(ss_b, sums_sb[:, 32:64])
            ve.tensor_copy(gc_, sums_sb[:, 0:16])
            ve.tensor_copy(gl_, sums_sb[:, 16:32])
            hold(ve.tensor_tensor(kd_s, sums_sb[:, 16:32], sums_sb[:, 0:16], ALU.subtract))
            y, w = inv_root("B", ss_b, 32, 1.0)
            hold(ve.tensor_tensor(y, y, w, ALU.mult))
            hold(ve.tensor_scalar(rqs, y[:, 0:16], B_HD ** -0.5, None, ALU.mult))
            hold(ve.tensor_copy(rk, y[:, 16:32]))
            hold(ve.tensor_tensor(nk, ss_b[:, 16:32], rk, ALU.mult))
            hold(ve.tensor_tensor(a_s, beta_t, rk, ALU.mult))
            hold(ve.tensor_tensor(n_s, a_s, rk, ALU.mult))
            hold(ve.tensor_scalar(n_s, n_s, -1.0, None, ALU.mult))
            ve.nop().then_inc(GATE_IN.sem, 1)
            GATE_OUT.wait(ve, "exps")
            hold(ve.tensor_scalar(negegc, egc, -1.0, None, ALU.mult))
            hold(ve.tensor_tensor(kd_s, ekd, rk, ALU.mult))

            def bank4(name):
                return filled(name)[:, :].rearrange("p (h n) -> p h n", h=4)

            for c in range(NT):
                def ready(ins, name):
                    ins.then_inc(GD.sem, 1)

                ps = bank4(("gc", c))
                if c > 0:
                    ve.wait_ge(decays_ready, 2 * c)
                ve.tensor_tensor(decay, ps, heads(gc_, c), ALU.subtract).then_inc(v_drained, 1)
                ve.wait_ge(v_drained, V.filled(("gc", c)))
                ve.nop().then_inc(diff_ready, 1)
                ve.tensor_tensor(k_tok, bank4(("kt", c)), heads(kd_s, c), ALU.mult).then_inc(v_drained, 1)
                ve.tensor_tensor(v_tok, bank4(("vt", c)), heads(nk, c), ALU.mult).then_inc(v_drained, 1)
                ve.wait_ge(v_drained, V.filled(("vt", c)))
                ve.nop().then_inc(GD.sem, 1)
                ve.wait_ge(decays_ready, 2 * c + 2)
                ve.tensor_tensor(neg_nT, bank4(("kk", c)), decay_n, ALU.mult).then_inc(v_drained, 1)
                ve.wait_ge(v_drained, V.filled(("kk", c)))
                ve.nop().then_inc(GD.sem, 1)
                ve.tensor_tensor(attnT, bank4(("qk", c)), attnT, ALU.mult).then_inc(v_drained, 1)
                ve.wait_ge(v_drained, V.filled(("qk", c)))
                ve.nop().then_inc(GD.sem, 1)
                ve.wait_ge(eye_ready, 2 * c + 2)

                def put(dst, n, src):
                    return ve.copy_predicated(dst, level_masks[:, n, :].unsqueeze(1).to_broadcast([P, 4, P]), src)

                put(t_invT, LEVELS, neg_nT)
                put(t_inv, 0, bank4(("n", c))).then_inc(v_drained, 1)
                ve.wait_ge(v_drained, V.filled(("n", c)))
                ve.nop().then_inc(GD.sem, 1)
                for l in range(1, LEVELS):
                    ve.tensor_copy(z_sb, bank4(("z", c, l))).then_inc(v_drained, 1)
                    ve.wait_ge(v_drained, V.filled(("z", c, l)))
                    ve.nop().then_inc(GD.sem, 1)
                    name = ("u", c, l) if l < LEVELS - 1 else ("ut", c, l)
                    filled(name)
                    put(t_invT, LEVELS + l, bank4(("ut", c, l))).then_inc(v_drained, 1)
                    ve.wait_ge(v_drained, V.filled(("ut", c, l)))
                    ve.nop().then_inc(GD.sem, 1)
                    if l < LEVELS - 1:
                        put(t_inv, l, bank4(("u", c, l))).then_inc(v_drained, 1)
                        ve.wait_ge(v_drained, V.filled(("u", c, l)))
                        ve.nop().then_inc(GD.sem, 1)
                    next(topk_last, None)
                if c == 0:
                    hold(ve.tensor_copy(resid, v_tok))
                else:
                    ps = bank4(("ks", c))
                    for h in range(4):
                        ins = ve.scalar_tensor_tensor(resid[:, h, :], ps[:, h, :], negegc[:, 4 * c + h:4 * c + h + 1],
                                                      v_tok[:, h, :], ALU.mult, ALU.add)
                    ins.then_inc(v_drained, 1)
                    ve.wait_ge(v_drained, V.filled(("ks", c)))
                ve.nop().then_inc(GD.sem, 1)
                ve.tensor_tensor(v_new, bank4(("x2", c)), heads(a_s, c), ALU.mult).then_inc(v_drained, 1)
                ve.wait_ge(v_drained, V.filled(("x2", c)))
                ve.nop().then_inc(GD.sem, 1)
                ps = bank4(("o", c))
                if c == 0:
                    ve.tensor_copy(o_tok, ps).then_inc(v_drained, 1)
                else:
                    ve.wait_ge(o_drained, O.filled(("os", c)))
                    ve.wait_ge(y_b, c)
                    ve.tensor_tensor(o_tok, ps, o_state, ALU.add).then_inc(v_drained, 1)
                ve.wait_ge(v_drained, V.filled(("o", c)))
                ve.nop().then_inc(GD.sem, 1)
                if c < NT - 1:
                    ps = bank4(("st", c))
                    if c == 0:
                        ve.tensor_copy(state, ps).then_inc(v_drained, 1)
                    else:
                        for h in range(4):
                            ins = ve.scalar_tensor_tensor(state[:, h, :], state[:, h, :], egl[:, 4 * c + h:4 * c + h + 1],
                                                          ps[:, h, :], ALU.mult, ALU.add)
                        ins.then_inc(v_drained, 1)
                    ve.wait_ge(v_drained, V.filled(("st", c)))
                    ve.nop().then_inc(GD.sem, 1)
                SQ.wait(ve, ("ob", c))
                so = ss_o[:, 4 * c:4 * c + 4]
                hold(ve.tensor_reduce(so, o_sq, AX.X, ALU.add))
                y, w = inv_root(("ob", c), so, 4, 1.0 / B_HD)
                hold(ve.tensor_tensor(so, y, w, ALU.mult))
                ve.tensor_tensor(o_tok, o_tok, bc(so, P), ALU.mult).then_inc(o_scaled, 1)

            cpv = cmp_p.rearrange("p (q h n) -> p q h n", q=NT, h=C_HEADS)
            ve.wait_ge(cmp_strip_ready, 1)
            for a in range(2):
                ps = filled(f"cl{a}")[:, 0:248].rearrange("p (q h n) -> p q h n", q=NT, h=2)
                ve.tensor_tensor(cpv[:, :, a::2, :], ps, cmp_strip[:, a::2, :, :].rearrange("p h q n -> p q h n"),
                                 ALU.add).then_inc(v_drained, 1)
            ve.wait_ge(v_drained, V.filled("cl1"))
            cpg = cmp_p.rearrange("p (g n) -> p g n", g=16)
            hold(ve.tensor_reduce(cmx, cpg, AX.X, ALU.max))
            ve.tensor_tensor(cpg, cpg, bc(cmx, N_CMP), ALU.subtract).then_inc(cl_ready, 1)
            ve.wait_ge(cexp_ready, 1)
            hold(ve.tensor_reduce(crs, cpg, AX.X, ALU.add))
            hold(ve.reciprocal(crs, crs))
            crq = crs.rearrange("p (q h) -> p q h", q=NT)
            hold(ve.tensor_scalar(crq[:, 0, :], crq[:, 0, :], seen[:, 0:1], None, ALU.mult))
            gate = raw_c1[:, :, 192:204].rearrange("p t (h k) -> p t h k", k=3)
            hold(ve.tensor_tensor(crq, crq, gate[:, :, :, 0], ALU.mult))

            def cmp_out():
                for n in range(2):
                    ve.wait_ge(o_filled, O.filled(("oc", n)))
                    ps = O.bank(("oc", n))[:, :].rearrange("p (g d) -> p g d", d=64)
                    ve.tensor_tensor(o_cg[:, 8 * n:8 * n + 8, :], ps, bc(crs[:, 8 * n:8 * n + 8], 64), ALU.mult).then_inc(o_drained, 1)

            o_cg = work[:, 2560:3584].rearrange("p (g d) -> p g d", d=64)

            def logits(u):
                m, q, h = units[u]
                L = P * (q + 1)
                ps = filled(("lg", m, q, h))
                if u >= 2:
                    ve.wait_ge(s_filled, S.filled(("pT", *units[u - 2])))
                if m == "A":
                    if q:
                        ve.wait_ge(bias_ready, u - 3)
                    b = bias_sel[u % 2][:, 0:L] if q else strips[:, h, T - L:T]
                else:
                    b = strips[:, A_HEADS + h, T - L:T]
                ve.tensor_tensor_reduce(out=probs[u % 2][:, 0:L], in0=ps[:, 0:L], in1=b, scale=1.0, scalar=-3e38,
                                        op0=ALU.add, op1=ALU.max, accum_out=mx[:, u:u + 1]).then_inc(v_drained, 1)
                ve.wait_ge(v_drained, V.filled(("lg", m, q, h)))
                ve.tensor_scalar(nmx[:, u:u + 1], mx[:, u:u + 1], -1.0, None, ALU.mult).then_inc(logits_ready, 1)

            def finish(g):
                m, q = groups[g]
                ve.wait_ge(probs_ready, 4 * g + 4)
                hold(ve.reciprocal(fac, rsum[:, 4 * g:4 * g + 4]))
                if m != "A":
                    hold(ve.tensor_tensor(fac, fac, gate[:, q, :, 1 if m == "sel" else 2], ALU.mult))
                ve.wait_ge(o_filled, O.filled(("o", m, q)))
                ps = O.bank(("o", m, q))[:, 0:256].rearrange("p (h d) -> p h d", h=4)
                oc = o_c[:, q, :].rearrange("p (h d) -> p h d", h=4)
                if m == "A":
                    ve.tensor_tensor(oc, ps, bc(fac, 64), ALU.mult).then_inc(o_drained, 1)
                    ve.wait_ge(o_drained, O.filled(("o", m, q)))
                elif m == "sel":
                    ve.wait_ge(y_ready, q + 1)
                    hold(ve.tensor_copy(oc, o_cg[:, 4 * q:4 * q + 4, :]))
                if m != "A":
                    tmp = cmp_p[:, 0:256].rearrange("p (h d) -> p h d", h=4)
                    ve.tensor_tensor(tmp, ps, bc(fac, 64), ALU.mult).then_inc(o_drained, 1)
                    ve.wait_ge(o_drained, O.filled(("o", m, q)))
                    hold(ve.tensor_tensor(oc, oc, tmp, ALU.add))
                ve.nop().then_inc(o_norm, 1)

            ve.wait_ge(y_b, NT)
            logits(0)
            logits(1)
            cmp_out()
            for u in range(len(units)):
                if u + 2 < len(units):
                    logits(u + 2)
                if u % 4 == 3 and u >= 7:
                    finish(u // 4 - 1)
            finish(len(groups) - 1)

            ve.wait_ge(yT_hi_ready, 1)
            for f in range(KC):
                ps = filled(("yT", f))
                ve.wait_ge(yT_hi_ready, f + 1)
                ve.scalar_tensor_tensor(yT_parts[:, f, 1, :], ps[:, :], bout_s if 2 <= f < 6 else Y_SCALE,
                                        yT_parts[:, f, 0, :], ALU.mult, ALU.subtract).then_inc(v_drained, 1)

            def merged_lo(j):
                ve.wait_ge(m_hi_ready, j + 1)
                ve.scalar_tensor_tensor(merged_parts[:, j, 1, :], gate_tile(j, 0), Y_SCALE, merged_parts[:, j, 0, :],
                                        ALU.mult, ALU.subtract).then_inc(merged_ready, 1)

            ve.wait_ge(g_drained, 24)
            for j in range(KC):
                for b in range(3):
                    g = gate_tile(j, b)
                    ins = ve.scalar_tensor_tensor(g, filled(("br", j, b))[:, :], 1.0 / (W_SCALE * Y_SCALE), g, ALU.mult, ALU.mult)
                    ins.then_inc(v_drained, 1)
                ve.wait_ge(v_drained, V.filled(("br", j, 2)))
                ve.nop().then_inc(merge_ready, 1)
                if j:
                    merged_lo(j - 1)
            merged_lo(KC - 1)
            ve.wait_ge(x_reloaded, 16)
            for n in range(2):
                for t in range(NT):
                    xr = x_again[:, t, 512 * n:512 * n + 512]
                    ve.scalar_tensor_tensor(xr, filled(("wo", n, t))[:, :], 1.0 / (W_SCALE * Y_SCALE), xr, ALU.mult,
                                            ALU.add).then_inc(v_drained, 1)
                    ve.wait_ge(v_drained, V.filled(("wo", n, t)))
                    ve.nop().then_inc(out_ready, 1)

        @block.tensor
        def _(pe):
            mm = nc.tensor.matmul

            def v_bank(name):
                if V.free(name) > 0:
                    pe.wait_ge(v_drained, V.free(name))
                return V.bank(name)

            def s_bank(name):
                if S.free(name) > 0:
                    pe.wait_ge(s_drained, S.free(name))
                return S.bank(name)

            def o_bank(name):
                if O.free(name) > 0:
                    pe.wait_ge(o_drained, O.free(name))
                return O.bank(name)

            def part(c, k, m0, m1):
                slot_ = pair_at[c, k // 2] % PAIRS
                return tuple(piece_view(w[:, slot_, :], c)[:, k % 2, m0:m1] for w in (w_hi, w_lo))

            def ready_pair(c, k):
                if k % 2 == 0:
                    pe.wait_ge(lo_ready, pair_at[c, k // 2] + 1)

            def product(ps, lhs, rhs, start, stop):
                mm(ps, lhs[0], rhs[0], start=start, stop=False)
                mm(ps, lhs[0], rhs[1], start=False, stop=False)
                return mm(ps, lhs[1], rhs[0], start=False, stop=stop)

            def project(c, name, token_major, first=0, between=None):
                n = CHUNKS[c][2]
                for t in range(4):
                    ps = s_bank((name, t))
                    for k in range(KC):
                        if t == 0:
                            ready_pair(c, k)
                        if token_major:
                            ins = product(ps[:, 0:n], [h[:, k, t * P:(t + 1) * P] for h in (hT_hi, hT_lo)],
                                          part(c, k, 0, n), k == 0, k == KC - 1)
                        else:
                            ins = product(ps[:, 0:T - first], part(c, k, t * P, (t + 1) * P),
                                          [h[:, k, first:T] for h in (hT_hi, hT_lo)], k == 0, k == KC - 1)
                        if t == 3 and k % 2 and k < KC - 1:
                            ins.then_inc(pair_used, 1)
                    ins.then_inc(s_filled, 1)
                    if t == 3:
                        release(s_filled, S.filled((name, 3)))
                    if between:
                        between(t)

            def release(filled, n):
                pe.wait_ge(filled, n)
                pe.nop().then_inc(pair_used, 1)

            def transposes(name, sources, rows=P, cols_=P):
                ps = v_bank(name)
                for n, src in enumerate(sources):
                    ins = nc.tensor.transpose(ps[0:cols_, n * rows:n * rows + rows], src, ident[0:rows, 0:rows])
                ins.then_inc(v_filled, 1)

            pe.wait_ge(const_loaded, 16 * 7)
            pe.wait_ge(in_loaded, 16 * 16)
            transposes("par", [par_rows], N_ROWS)
            for t in range(NT):
                pe.wait_ge(h_ready, t + 1)
                for a in range(2):
                    transposes(("x", t, a), [x_in[:, t, (4 * a + k) * P:(4 * a + k + 1) * P] for k in range(4)])
            pe.wait_ge(hot_ready, 1)
            for n in range(2):
                ps = v_bank(f"rel{n}")
                mm(ps[0:N_HEADS, 0:320], rel33, hot[0:N_BUCKETS + 1, 320 * n:320 * n + 320], start=True, stop=True).then_inc(v_filled, 1)
            pe.wait_ge(h_lo_ready, 2 * NT)
            hid = banks[2:4]

            def phi(v, j):
                n = piece_at[CH_PK + v, j]
                if j == 0:
                    pe.wait_ge(v_drained, V.filled(("kcmp", "vcmp")[v]))
                pe.wait_ge(w_loaded[n % STAGES], 16 * (n // STAGES + 1))
                w = piece_view(stage[:, n % STAGES, :], CH_PK, 4)
                for h in range(2):
                    for k in range(4):
                        ins = mm(hid[h][:, v * N_CMP:(v + 1) * N_CMP], w[:, k, h * P:(h + 1) * P], blocks[:, v, 4 * j + k, :],
                                 start=j + k == 0, stop=4 * j + k == 15)
                ins.then_inc(phi_used, 1)

            project(CH_C0, "C0", True)
            project(CH_C1, "C1", True)
            project(CH_A0, "A0", True)
            T_IN.wait(pe, "C0q")
            for m in range(2):
                transposes(f"cqT{m}", [raw_c0[:, t, m * P:(m + 1) * P] for t in range(NT)])
            for n, (name, inp) in enumerate((("kcmp", "C0blk"), ("vcmp", "C0blk"), ("ksT", "C0ks"), ("kwT", "C1kw"))):
                T_IN.wait(pe, inp)
                transposes(name, [squares[:, 512 * n + P * t:512 * n + P * t + P] for t in range(NT)])
            project(CH_QI, "QI", False, P)
            T_IN.wait(pe, "A0ckv")
            transposes("ckvT", [raw_a0[:, t, 256:384] for t in range(NT)])
            T_IN.wait(pe, "A0q")
            for m in range(2):
                transposes(f"qT{m}", [raw_a0[:, t, m * P:(m + 1) * P] for t in range(NT)])
            pe.wait_ge(v_drained, V.filled("ckvT"))
            pe.wait_ge(ukv_loaded, 16)
            for t in range(NT):
                ps = v_bank(("ukv", t))
                mm(ps[:, :], ckvT[:, t * P:(t + 1) * P], ukv, start=True, stop=True).then_inc(v_filled, 1)
            project(CH_A2, "A2", True, between=lambda t: phi(0, t))
            T_IN.wait(pe, "Ak")
            for m in range(2):
                transposes(f"kT{m}", [k_raw[:, t, m * P:(m + 1) * P] for t in range(NT)])
            T_IN.wait(pe, "Aki")
            transposes("kiT", [squares[:, 1024 + P * t:1152 + P * t] for t in range(NT)])
            project(CH_B0, "B0", False, between=lambda t: phi(1, t))
            pe.wait_ge(phi_used, 8)
            pe.nop().then_inc(hid_filled, 1)
            pe.wait_ge(v_drained, V.filled("kiT"))
            for q in range(1, NT):
                for h in range(IDX_HEADS):
                    L, r = P * (q + 1), 64 * (h % 2)
                    ps = s_bank(("idx", q, h))
                    mm(ps[:, 0:L], qiT[r:r + 64, h // 2, (q - 1) * P:q * P], kiT[r:r + 64, 0:L], start=True, stop=True).then_inc(s_filled, 1)
            pe.wait_ge(hid_ready, 1)
            ps = v_bank("cmpkv")
            for v in range(2):
                for h in range(2):
                    ins = mm(ps[0:N_CMP, 64 * v:64 * v + 64], hidT[:, 2 * v + h, :], phi2[:, 2 * v + h, :], start=h == 0, stop=h == 1)
            ins.then_inc(v_filled, 1)
            project(CH_B1, "B1", False)
            T_IN.wait(pe, "kc")
            transposes("kcT", [raw_c0[0:N_CMP, 0, 0:128]], N_CMP)
            project(CH_B2, "B2", False)
            project(CH_B3, "B3", True)
            project(CH_B4, "B4", True)
            ps = v_bank("sums")
            for m in range(8):
                SQ.wait(pe, ("B", m))
                for t in range(NT):
                    c0 = 32 + 16 * (m // 4) + 4 * t + m % 4
                    ins = mm(ps[:, c0:c0 + 1], squares[:, 512 * (m % 4) + t * P:512 * (m % 4) + (t + 1) * P], ones[:, 0:1],
                             start=True, stop=True)
                ins.then_inc(sums_taken, 1)
            pe.wait_ge(gsum_ready, 1)
            mm(ps[:, 0:16], tri, g_t, start=True, stop=True)
            mm(ps[:, 16:32], ones[:, :], g_t, start=True, stop=True).then_inc(v_filled, 1)

            def gate_products():
                for g in range(24):
                    c, m = GATE_CHUNKS[g // 4], g % 4 * P
                    if G.free(g) > 0:
                        pe.wait_ge(g_drained, G.free(g))
                    for k in range(KC):
                        if g % 4 == 0:
                            ready_pair(c, k)
                        ins = product(G.bank(g)[:, :], part(c, k, m, m + P), (hT_hi[:, k, :], hT_lo[:, k, :]), k == 0, k == KC - 1)
                        if k == KC - 1:
                            ins.then_inc(g_filled, 1)
                            if g % 4 == 3:
                                release(g_filled, g + 1)
                        elif g % 4 == 3 and k % 2:
                            ins.then_inc(pair_used, 1)
                        yield

            gate_steps = gate_products()

            def fill(n):
                for _ in range(n):
                    next(gate_steps)

            def four(name, lhs, rhs, ring_=None):
                ps = v_bank(name) if ring_ is None else o_bank(name)
                for h in range(4):
                    ins = mm(ps[:, h * P:(h + 1) * P], lhs(h), rhs(h), start=True, stop=True)
                ins.then_inc(v_filled if ring_ is None else o_filled, 1)

            pe.wait_ge(conv_done, 12)
            for c in range(NT):
                tok = slice(3 + c * P, 3 + (c + 1) * P)
                qc, kc_, vc_ = (lambda h, m=m: qkvT[:, 4 * m + h, tok] for m in range(3))
                pe.wait_ge(gtri_ready, c + 1)
                ps = v_bank(("gc", c))
                mm(ps[:, :], ones[:, :], g_tri.rearrange("p h n -> p (h n)"), start=True, stop=True).then_inc(v_filled, 1)
                transposes(("kt", c), [kc_(h) for h in range(4)])
                transposes(("vt", c), [vc_(h) for h in range(4)])
                four(("kk", c), kc_, kc_)
                four(("qk", c), kc_, qc)
                fill(2)
                GD.wait(pe, ("nnt", c))
                transposes(("n", c), [neg_nT[:, h, :] for h in range(4)])
                GD.wait(pe, ("tt0", c))
                for l in range(1, LEVELS):
                    four(("z", c, l), lambda h: neg_nT[:, h, :], lambda h: t_inv[:, h, :])
                    fill(2)
                    GD.wait(pe, ("z", c, l))
                    four(("ut", c, l), lambda h: z_sb[:, h, :], lambda h: t_invT[:, h, :])
                    if l < LEVELS - 1:
                        four(("u", c, l), lambda h: t_invT[:, h, :], lambda h: z_sb[:, h, :])
                    if l < LEVELS - 1:
                        fill(2)
                        GD.wait(pe, ("t", c, l))
                if c > 0:
                    GD.wait(pe, ("state", c - 1))
                    four(("ks", c), kc_, lambda h: state[:, h, :])
                    four(("os", c), qc, lambda h: state[:, h, :], O)
                GD.wait(pe, ("resid", c))
                four(("x2", c), lambda h: t_invT[:, h, :], lambda h: resid[:, h, :])
                GD.wait(pe, ("vnew", c))
                four(("o", c), lambda h: attnT[:, h, :], lambda h: v_new[:, h, :])
                if c < NT - 1:
                    four(("st", c), lambda h: k_tok[:, h, :], lambda h: v_new[:, h, :])

            for a in range(2):
                ps, r = v_bank(f"cl{a}"), 64 * a
                for q in range(NT):
                    for m in range(2):
                        u = 2 * q + m
                        ins = mm(ps[:, u * N_CMP:(u + 1) * N_CMP], qT_c[r:r + 64, m, q * P:(q + 1) * P], kcT[r:r + 64, 0:N_CMP],
                                 start=True, stop=True)
                ins.then_inc(v_filled, 1)

            def unit_logits(u):
                m, q, h = units[u]
                qT, kT = {"A": (qT_a, kT_a[:, h // 2, :]), "sel": (qT_c, kT_sel), "win": (qT_c, kT_win)}[m]
                r, L = 64 * (h % 2), P * (q + 1)
                ps = v_bank(("lg", m, q, h))
                mm(ps[:, 0:L], qT[r:r + 64, h // 2, q * P:(q + 1) * P], kT[r:r + 64, 0:L], start=True, stop=True).then_inc(v_filled, 1)

            unit_logits(0)
            unit_logits(1)
            pe.wait_ge(cexp_ready, 1)
            for q in range(NT):
                ps = s_bank(("cp", q))
                for h in range(4):
                    ins = nc.tensor.transpose(ps[0:N_CMP, h * P:(h + 1) * P], cmp_p[:, (4 * q + h) * N_CMP:(4 * q + h + 1) * N_CMP], ident)
                ins.then_inc(s_filled, 1)
            for n in range(2):
                ps = o_bank(("oc", n))
                pe.wait_ge(s_drained, S.filled(("cp", 2 * n + 1)))
                for u in range(8):
                    ins = mm(ps[:, 64 * u:64 * u + 64], cmp_pT[:, 8 * n + u, :], cmp_v[:, :], start=True, stop=True)
                ins.then_inc(o_filled, 1)

            def unit_out(u):
                m, q, h = units[u]
                ps = O.bank(("o", m, q)) if h else o_bank(("o", m, q))
                pe.wait_ge(s_drained, S.filled(("pT", m, q, h)))
                for k in range(q + 1):
                    v = {"A": v_a[:, k, 64 * h:64 * h + 64], "sel": raw_c1[:, k, 0:64], "win": raw_c1[:, k, 128:192]}[m]
                    ins = mm(ps[:, 64 * h:64 * h + 64], probsT[u % 2][:, k * P:(k + 1) * P], v, start=k == 0, stop=k == q)
                ins.then_inc(pv_done, 1)
                if h == 3:
                    pe.wait_ge(pv_done, u + 1)
                    pe.nop().then_inc(o_filled, 1)

            for u, (m, q, h) in enumerate(units):
                pe.wait_ge(probs_ready, u + 1)
                ps = s_bank(("pT", m, q, h))
                for k in range(q + 1):
                    ins = nc.tensor.transpose(ps[:, k * P:(k + 1) * P], probs[u % 2][:, k * P:(k + 1) * P], ident)
                ins.then_inc(s_filled, 1)
                fill(1)
                if u + 2 < len(units):
                    unit_logits(u + 2)
                if u >= 1:
                    unit_out(u - 1)
                fill(1)
            unit_out(len(units) - 1)

            pe.wait_ge(y_b, NT)
            pe.wait_ge(y_ready, 2 * NT)
            sources = [(raw_a2, 72), (raw_a2, 200)] + [(raw_b, 8 + P * n) for n in range(4)] + [(raw_c1, 204), (raw_c1, 332)]
            for f, (raw, c0) in enumerate(sources):
                transposes(("yT", f), [raw[:, t, c0:c0 + P] for t in range(NT)])
            pe.wait_ge(v_drained, V.filled(("yT", KC - 1)))
            for j in range(KC):
                c, m = (CH_WB0, CH_WB1)[j // 4], j % 4 * P
                for b, rows in enumerate(((0, 2), (2, 6), (6, 8))):
                    ps = v_bank(("br", j, b))
                    for k in range(*rows):
                        if j % 4 == 0:
                            ready_pair(c, k)
                        ins = product(ps[:, :], part(c, k, m, m + P), (yT_parts[:, k, 0, :], yT_parts[:, k, 1, :]),
                                      k == rows[0], k == rows[1] - 1)
                        if j % 4 == 3 and k == 3:
                            ins.then_inc(pair_used, 1)
                    ins.then_inc(v_filled, 1)
                    if j % 4 == 3:
                        release(v_filled, V.filled(("br", j, b)))
            for n in range(2):
                for t in range(NT):
                    ps = v_bank(("wo", n, t))
                    for k in range(KC):
                        if t == 0:
                            ready_pair(CH_WO0 + n, k)
                            if n == 0:
                                pe.wait_ge(merged_ready, k + 1)
                        ins = product(ps[:, :], [merged_parts[:, k, a, t * P:(t + 1) * P] for a in range(2)],
                                      part(CH_WO0 + n, k, 0, 512), k == 0, k == KC - 1)
                        if t == 3 and k % 2 and k < KC - 1:
                            ins.then_inc(pair_used, 1)
                    ins.then_inc(v_filled, 1)
                if n == 0:
                    release(v_filled, V.filled(("wo", 0, NT - 1)))


NAMES = ["x", "norm_g", "w_in", "a_kv_norm", "a_w_ukv", "a_q_norm", "a_k_norm", "b_conv", "b_a_log", "b_dt_bias",
         "b_out_norm", "c_q_norm", "c_k_norm", "c_cmp_pos", "c_phi_w1", "c_phi_w2", "w_branch", "w_out", "rel_bias"]


def kernel(**inputs):
    import concourse.bacc as bacc
    from concourse.bass_utils import run_bass_kernel_spmd

    nc = bacc.Bacc("TRN2", target_bir_lowering=False, num_devices=1)
    floats, masks = shape_constants()
    arrays, args = {}, []
    for name, a in [(n, np.ascontiguousarray(inputs[n])) for n in NAMES] + [("floats", floats), ("masks", masks)]:
        arrays[f"in_{name}"] = a
        args.append(nc.dram_tensor(f"in_{name}", a.shape, mybir.dt.from_np(a.dtype), kind="ExternalInput").ap())
    out = nc.dram_tensor("out_x", (1, T, D), mybir.dt.float32, kind="ExternalOutput").ap()
    rel_rows = nc.dram_tensor("rel_rows", (N_HEADS, P, S_REL), mybir.dt.float32, kind="Internal").ap()
    trunk(nc, *args, out, rel_rows)
    r = run_bass_kernel_spmd(nc, [arrays], core_ids=[0])
    return r.results[0]["out_x"]
```

```python
import math
from contextlib import ExitStack
from itertools import chain

import numpy as np
import concourse.bass as bass
from concourse import mybir

P = 128
T, D = 512, 1024
NT, KC = T // P, D // P
EPS = 1e-6
NEG = -1e30
TAKEN = -3e38

A_HEADS, A_HD = 4, 64
IDX_HEADS = 8
TOPK = min(256, T // 4)
B_HD = 128
C_HEADS, C_HD = 4, 64
CMP_BLOCK, N_CMP = 32, (T - 32) // 16 + 1
PHI = 256
N_BUCKETS, EXACT, MAX_DIST = 32, 16, 128
N_HEADS = A_HEADS + C_HEADS

A_Q, A_QI, A_KI = 0, 384, 896
B_BASE = 1224
B_AB = B_BASE + 1536
C_BASE = B_AB + 8 + 512
C_VSEL = C_BASE + 256 + 192
G_BASE = 4188

CHUNKS = [
    ("w_in", C_BASE, 448), ("w_in", C_VSEL, 460),
    ("w_in", A_Q, 384), ("w_in", A_QI, 512), ("w_in", A_KI, 328),
    ("phi", 0, PHI), ("phi", 1, PHI),
    ("w_in", B_BASE, 512), ("w_in", B_BASE + 512, 512),
    ("w_in", B_AB, 260), ("w_in", B_AB + 260, 260), ("w_in", B_BASE + 1024, 512),
    ("w_in", G_BASE, 512), ("w_in", G_BASE + D, 512), ("w_in", G_BASE + 2 * D, 512),
    ("w_in", G_BASE + 512, 512), ("w_in", G_BASE + D + 512, 512), ("w_in", G_BASE + 2 * D + 512, 512),
    ("w_branch", 0, 512), ("w_branch", 512, 512), ("w_out", 0, 512), ("w_out", 512, 512),
]
W_SCALE, Y_SCALE = 64.0, 1.0 / 16
STAGES, PAIRS = 3, 6
(CH_C0, CH_C1, CH_A0, CH_QI, CH_A2, CH_PK, CH_PV, CH_B0, CH_B1, CH_B3, CH_B4, CH_B2,
 CH_G0, CH_G1, CH_G2, CH_G3, CH_G4, CH_G5, CH_WB0, CH_WB1, CH_WO0, CH_WO1) = range(22)

R_NORM, R_CONV, R_CKV, R_AQ, R_AK, R_CQ, R_CK, R_BOUT, R_POS, N_ROWS = 0, 8, 56, 57, 58, 59, 60, 63, 64, 96
F_IDENT, F_TRI, F_SEEN, F_HOT, N_FLOAT = 0, 128, 256, 260, 260 + 640
LEVELS = 7
FILL_Z, FILL_U, FILL_X, FILL_T = 7, 2, 7, 3
TOPK_A, TOPK_B = 16, 6
Y_EARLY = {20: (2,), 22: (3,), 26: (0,), 28: (1,), 46: (4,), 47: (5,)}
Y_ORDER = (2, 3, 0, 1, 4, 5, 6, 7)
ATTENTION_FILL = (7, 7, 5, 5)
FILL_N = 3 * KC * 3 - (LEVELS - 1) * FILL_Z - (LEVELS - 2) * FILL_U - FILL_X - 2 * FILL_T
S_REL = 640


def shape_constants():
    f = np.zeros((P, N_FLOAT), np.float32)
    i = np.arange(P)
    f[:, F_IDENT:F_IDENT + P] = np.eye(P)
    f[:, F_TRI:F_TRI + P] = i[:, None] <= i[None, :]
    f[:, F_SEEN] = i >= CMP_BLOCK - 1
    f[:, F_SEEN + 1:F_SEEN + 4] = 1.0
    dist = T - 1 - np.arange(S_REL)
    ratio = np.log(np.maximum(dist, 1).astype(np.float32) / EXACT) / math.log(MAX_DIST / EXACT)
    large = np.minimum(EXACT + (ratio * (N_BUCKETS - EXACT)).astype(np.int32), N_BUCKETS - 1)
    bucket = np.where(dist < 0, N_BUCKETS, np.where(dist < EXACT, dist, large))
    f[0:N_BUCKETS + 1, F_HOT:F_HOT + S_REL] = bucket[None, :] == np.arange(N_BUCKETS + 1)[:, None]
    m = np.zeros((P, 2 * LEVELS, P), np.float16)
    for n in range(LEVELS):
        b = 1 << n
        same = i[:, None] // (2 * b) == i[None, :] // (2 * b)
        low = same & (i[:, None] // b % 2 == 1) & (i[None, :] // b % 2 == 0)
        m[:, n] = low
        m[:, LEVELS + n] = low.T
    return f, m


class Uses:

    def __init__(self, banks, names):
        self.banks = banks
        self.at = {n: i for i, n in enumerate(names)}
        assert len(self.at) == len(names)

    def bank(self, name):
        return self.banks[self.at[name] % len(self.banks)]

    def filled(self, name):
        return self.at[name] + 1

    def free(self, name):
        return self.at[name] + 1 - len(self.banks)


class Steps:

    def __init__(self, sem, names):
        self.sem = sem
        self.n = {n: i + 1 for i, n in enumerate(names)}
        assert len(self.n) == len(names)

    def wait(self, eng, name):
        eng.wait_ge(self.sem, self.n[name])


def trunk(nc, x, norm_g, w_in, a_kv_norm, a_w_ukv, a_q_norm, a_k_norm, b_conv, b_a_log, b_dt_bias, b_out_norm,
          c_q_norm, c_k_norm, c_cmp_pos, c_phi_w1, c_phi_w2, w_branch, w_out, rel_bias, floats, masks, out, rel_rows):
    f32 = mybir.dt.float32
    f16 = mybir.dt.float16
    u8 = mybir.dt.uint8
    ALU = mybir.AluOpType
    ACT = mybir.ActivationFunctionType
    AX = mybir.AxisListType
    ctx = ExitStack()
    with ctx:
        def sb(name, shape, dt=f32):
            return ctx.enter_context(nc.sbuf_tensor(name, shape, dt))

        def sem(name):
            return ctx.enter_context(nc.semaphore(name))

        hT_hi = sb("hT_hi", [P, KC, T], f16)
        hT_lo = sb("hT_lo", [P, KC, T], f16)
        stage = sb("stage", [P, STAGES, 1024])
        w_hi = sb("w_hi", [P, PAIRS, 1024], f16)
        w_lo = sb("w_lo", [P, PAIRS, 1024], f16)
        early = sb("early", [P, 6144])
        work = sb("work", [P, 6144])
        late = sb("late", [P, 4608])
        qkvT = sb("qkvT", [P, 12, T + 3])
        strips = sb("strips", [P, N_HEADS, T])
        cmp_strip = sb("cmp_strip", [P, C_HEADS, NT, N_CMP])
        raw_a2 = sb("raw_a2", [P, NT, 328])
        raw_b = sb("raw_b", [P, NT, 520])
        raw_c1 = sb("raw_c1", [P, NT, 460])
        v_a = sb("v_a", [P, NT, 256])
        qT_a = sb("qT_a", [P, 2, T])
        kT_a = sb("kT_a", [P, 2, T])
        qT_c = sb("qT_c", [P, 2, T])
        kT_sel = sb("kT_sel", [P, T])
        kT_win = sb("kT_win", [P, T])
        consts = sb("consts", [P, F_HOT])
        level_masks = sb("level_masks", [P, 2 * LEVELS, P], u8)
        ones = sb("ones", [P, P])
        par = sb("par", [P, N_ROWS])
        small = sb("small", [P, 600])
        kcT = sb("kcT", [P, N_CMP + 1])
        cmp_v = sb("cmp_v", [N_CMP, 64])
        g_scale = sb("g_scale", [P, 16, 12])

        ident = consts[:, F_IDENT:F_IDENT + P]
        tri = consts[:, F_TRI:F_TRI + P]
        seen = consts[:, F_SEEN:F_SEEN + 4]

        x_in = [early[:, D * t:D * t + D] for t in range(NT - 1)] + [raw_c1[:, :, :].rearrange("p t n -> p (t n)")[:, 0:D]]
        rel_row = work[0:N_HEADS, 4608:4608 + S_REL]
        hot = work[:, S_REL:2 * S_REL]
        rel33 = work[0:N_BUCKETS + 1, 1280:1280 + N_HEADS]
        par_rows = work[0:N_ROWS, 1288:1288 + P]
        squares = early[:, 0:2048]
        conv_acc = early[:, 2048:3072].rearrange("p (b n) -> p b n", b=2)
        raw_c0 = early[:, 3072:4864].rearrange("p (t n) -> p t n", t=NT)
        blocks = early[:, 4864:5856].rearrange("p (v c n) -> p v c n", v=2, c=16)
        hidT = early[:, 5856:5980].rearrange("p (v n) -> p v n", v=4)
        gates = early[:, 0:6144].rearrange("p (g n) -> p g n", g=12)
        raw_a0 = work[:, 0:1536].rearrange("p (t n) -> p t n", t=NT)
        qiT = work[:, 1536:3072].rearrange("p (m n) -> p m n", m=4)
        ukv = work[:, 3072:3584]
        ckvT = work[:, 3584:4096]
        kiT = work[:, 4096:4608]
        mask_halves = late[:, 3456:3456 + LEVELS * P].bitcast(f16).rearrange("p (n m) -> p n m", m=P)
        phi2 = work[:, 5632:5888].rearrange("p (k n) -> p k n", k=4)
        k_raw = work[:, 4608:5632].rearrange("p (t n) -> p t n", t=NT)
        merged_parts = work[:, 0:4096].bitcast(f16).rearrange("p (c a n) -> p c a n", c=KC, a=2)
        o_c = work[:, 3584:4608].rearrange("p (t n) -> p t n", t=NT)

        def slot(t, n):
            return t[:, 512 * n:512 * n + 512].rearrange("p (h n) -> p h n", h=4)

        (g_tri, decay, decay_k, neg_nT, t_inv, t_invT, z_sb, v_tok, k_tok, attnT0, resid, v_new) = (
            slot(work, n) for n in range(12))
        state, decay_n, o_state, attnT1, o_tok, o_sq = (slot(late, n) for n in range(6))
        attnT = (attnT0, attnT1)
        scores = [late[:, 0:256], late[:, 3072:3456], early[:, 4608:5120]]
        topk_work = [early[:, 5120:5632], early[:, 5632:6144]]
        relu_buf = [late[:, 640:1152], late[:, 1152:1664]]
        probs = [late[:, 512 * n:512 * n + 512] for n in range(2)]
        probsT = [late[:, 1024 + 512 * n:1536 + 512 * n] for n in range(2)]
        bias_sel = [late[:, 2048 + 512 * n:2560 + 512 * n] for n in range(2)]
        keep_add = [late[:, 3456:3712], late[:, 3712:4096], late[:, 4096:4608]]
        x_again = late[:, 0:4096].rearrange("p (t d) -> p t d", t=NT)
        qkv_flat = qkvT[:, :, :].rearrange("p a b -> p (a b)")
        h_full = qkv_flat[:, 0:4096].rearrange("p (c n) -> p c n", c=KC)
        gates_b = qkv_flat[:, 0:6144].rearrange("p (g n) -> p g n", g=12)
        yT_parts = strips[:, :, :].bitcast(f16).rearrange("p c (a n) -> p c a n", a=2)
        cmp_p = work[:, 0:496]
        cmp_pT = work[0:N_CMP, 512:2560].rearrange("p (u n) -> p u n", u=16)

        col = [0]

        def cols(n):
            col[0] += n
            return small[:, col[0] - n:col[0]]

        banks = [ctx.enter_context(nc.psum_tensor(f"bank{n}", [P, 512], f32)) for n in range(8)]
        s_names = [(c, t) for c in ("C0", "C1", "A0", "QI", "A2", "B0") for t in range(4)]
        s_names += [("idx", q, h) for q in range(1, NT) for h in range(IDX_HEADS)]
        s_names += [(c, t) for c in ("B1", "B3", "B4", "B2") for t in range(4)]
        s_names += [("cp", q) for q in range(4)]
        units = [(m, q, h) for m in "A" for q in range(NT) for h in range(4)]
        units += [(m, q, h) for q in range(NT) for m in ("sel", "win") for h in range(4)]
        groups = [u[:2] for u in units[::4]]
        s_names += [("pT", *u) for u in units]
        S = Uses(banks[0:2], s_names)
        G = Uses(banks[2:4], range(24))
        v_names = ["par"] + [("x", t, a) for t in range(NT) for a in range(2)] + ["rel0", "rel1"]
        v_names += ["cqT0", "cqT1", "kcmp", "vcmp", "ksT", "kwT"]
        v_names += ["ckvT", "qT0", "qT1"] + [("ukv", t) for t in range(NT)] + ["kT0", "kT1", "kiT", "cmpkv", "kcT", "sums"]
        v_names += [(n, 0) for n in ("gc", "kk", "qk", "n")]
        for c in range(NT):
            for l in range(1, LEVELS):
                v_names += [("z", c, l)] + ([("u", c, l)] if l < LEVELS - 1 else []) + [("ut", c, l)]
                v_names += [("ks", c)] if c and l == 1 else []
                v_names += [("kt", 0), ("vt", 0)] if c == 0 and l == 3 else []
                if l == 2:
                    v_names += [("gc", c + 1)] if c < NT - 1 else ["cl0", "cl1"]
            if c < NT - 1:
                v_names += [("kk", c + 1), ("qk", c + 1), ("x2", c), ("n", c + 1), ("o", c), ("st", c), ("kt", c + 1), ("vt", c + 1)]
            else:
                v_names += [("x2", c), ("o", c)]
        for n, u in enumerate(units):
            v_names += [("lg", *u)] + [("yT", f) for f in Y_EARLY.get(n - 2, ())]
        v_names += [("yT", f) for n in range(len(units) - 2, len(units)) for f in Y_EARLY[n]]
        for j in range(KC):
            v_names += [("br", j, 0), ("br", j, 1)] + ([("yT", 6), ("yT", 7)] if j == 0 else []) + [("br", j, 2)]
        v_names += [("wo", n, t) for n in range(2) for t in range(NT)]
        V = Uses(banks[4:6], v_names)
        O = Uses(banks[6:8], [("os", c) for c in range(1, NT)] + [("oc", n) for n in range(2)] + [("o", *g) for g in groups])

        s_filled, s_drained = sem("scalar_banks_filled"), sem("scalar_banks_drained")
        v_filled, v_drained = sem("vector_banks_filled"), sem("vector_banks_drained")
        o_filled, o_drained = sem("out_banks_filled"), sem("out_banks_drained")
        g_filled, g_drained = sem("gate_banks_filled"), sem("gate_banks_drained")
        w_loaded = [sem(f"weights_loaded{n}") for n in range(STAGES)]
        scaled, hi_ready, lo_ready = sem("weights_scaled"), sem("weights_hi_ready"), sem("weights_lo_ready")
        hid_filled, hid_ready = sem("hidden_banks_filled"), sem("hidden_ready")
        pair_used, phi_used = sem("weight_pairs_used"), sem("phi_weights_used")
        x_loaded = [sem(f"x_loaded{t}") for t in range(NT)]
        in_loaded = sem("parameters_loaded")
        ident_loaded, const_loaded, masks_loaded = sem("identity_loaded"), sem("constants_loaded"), sem("masks_loaded")
        ukv_loaded = sem("ukv_loaded")
        fills = sem("fills_done")
        hot_ready = sem("rel_table_ready")
        row_stored, strips_loaded, cmp_strip_ready = sem("rel_rows_stored"), sem("strips_loaded"), sem("cmp_strip_ready")
        x_reloaded, out_stored = sem("x_reloaded"), sem("out_stored")
        v_step, p_step, a_step = sem("vector_step"), sem("pool_step"), sem("scalar_step")
        roots = ["x", "C0", "C1", "A0", "Ak", "kc", "B"] + [("ob", c) for c in range(NT)]
        ROOT_IN = Steps(sem("root_input_ready"), roots)
        ROOT_OUT = Steps(sem("root_ready"), roots)
        SQ = Steps(sem("squares_ready"), ["C0", "C1", "A0", "Ak"] + [("B", m) for m in range(8)] + [("ob", c) for c in range(NT)])
        ssx_ready, h_ready, h_full_ready = sem("x_square_sums_ready"), sem("h_ready"), sem("hT_full_ready")
        h_hi_ready, h_lo_ready = sem("hT_hi_ready"), sem("hT_lo_ready")
        rows_ready = sem("rel_rows_ready")
        conv_ready, conv_done = sem("conv_ready"), sem("conv_silu_done")
        T_IN = Steps(sem("transpose_input_ready"), ["C0q", "C0blk", "C0ks", "C1kw", "A0ckv", "A0q", "Ak", "Aki", "kc"])
        score_ready, diag_ready = sem("score_ready"), sem("diagonal_masked")
        relu_used = sem("relu_used")
        keep_ready = sem("keep_ready")
        GATE_IN = Steps(sem("decay_input_ready"), ["g", "gc2"])
        GATE_OUT = Steps(sem("decay_exp_ready"), ["beta", "expa", "sp", "exps"])
        z_ready, sums_taken, gsum_ready = sem("z_gates_ready"), sem("squares_summed"), sem("log_decay_ready")
        gtri_ready = sem("cumulative_input_ready")
        diff_ready, exp_ready, decays_ready = sem("decay_difference_ready"), sem("decay_ready"), sem("decays_masked")
        g_names = [(n, 0) for n in ("nnt", "attn", "tt0")]
        for c in range(NT):
            for l in range(1, LEVELS):
                g_names += [("z", c, l)] + ([("t", c, l)] if l < LEVELS - 1 else []) + [("tt", c, l)]
                g_names += [("resid", c)] if c and l == 1 else []
                g_names += [("kt", 0)] if c == 0 and l == 3 else []
            if c < NT - 1:
                g_names += [("nnt", c + 1), ("attn", c + 1), ("vnew", c), ("tt0", c + 1), ("oraw", c), ("state", c), ("kt", c + 1)]
            else:
                g_names += [("vnew", c), ("oraw", c)]
        GD = Steps(sem("deltanet_ready"), g_names)
        eye_ready = sem("inverse_reset")
        o_scaled = sem("deltanet_output_scaled")
        y_b = sem("y_b_ready")
        cl_ready, cexp_ready = sem("cmp_logits_ready"), sem("cmp_exp_ready")
        logits_ready, probs_ready, pv_done = sem("logits_ready"), sem("probs_ready"), sem("probsT_used")
        bias_ready = sem("selected_bias_ready")
        o_norm, y_ready = sem("output_normalised"), sem("y_ready")
        sum_ready, merged_ready = sem("branches_added"), sem("merged_ready")
        yT_hi_ready, m_hi_ready = sem("yT_hi_ready"), sem("merged_hi_ready")
        out_ready = sem("out_ready")

        ss_x, ss_a, ss_k = cols(4), cols(20), cols(16)
        ss_c, ss_w, ss_kc, ss_b, ss_o = cols(20), cols(4), cols(1), cols(32), cols(16)
        root = cols(32)
        newton = cols(32)
        max8 = cols(16)
        beta_t, g_t, sp_a, sp_b, neg_exp_a, dt_b = cols(16), cols(16), cols(16), cols(16), cols(4), cols(4)
        rk, nk = cols(16), cols(16)
        sums_sb = cols(64)
        mx, nmx, rsum = cols(48), cols(48), cols(48)
        cmx, crs = cols(16), cols(16)
        fac = cols(4)
        bout_s = cols(1)
        (gc_, gl_, egc, negegc, egl, ekd, kd_s, n_s, a_s, rqs) = (g_scale[:, :, n] for n in range(10))
        assert col[0] <= 600, col[0]

        def bc(ap, n):
            return ap.unsqueeze(2).to_broadcast([ap.shape[0], ap.shape[1], n])

        def heads(ap, c):
            return bc(ap[:, 4 * c:4 * c + 4], P)

        def over_heads(ap):
            return ap.unsqueeze(1).to_broadcast([P, 4, P])

        order = [(c, j) for c in range(CH_A2 + 1) for j in range(4)]
        for v, c in ((CH_PK, CH_B0), (CH_PV, CH_B1)):
            order += [(v, 0), (c, 0), (v, 1), (c, 1), (v, 2), (c, 2), (c, 3), (v, 3)]
        order += [(c, j) for c in range(CH_B3, len(CHUNKS)) for j in range(4)]
        pieces, n_pairs, n_phi = [], 0, 0
        for c, j in order:
            phi_piece = CHUNKS[c][0] == "phi"
            pieces.append((c, j, n_phi if phi_piece else n_pairs))
            n_phi, n_pairs = n_phi + phi_piece, n_pairs + (not phi_piece)
        piece_at = {(c, j): n for n, (c, j, _) in enumerate(pieces)}
        pair_at = {(c, j): k for c, j, k in pieces if CHUNKS[c][0] != "phi"}
        split_chunks = [c for c in range(len(CHUNKS)) if CHUNKS[c][0] != "phi"]
        GATE_CHUNKS = (CH_G0, CH_G1, CH_G2, CH_G3, CH_G4, CH_G5)

        def after(c):
            return split_chunks[split_chunks.index(c) + 1]

        FOLLOW = ((0,), (1,), (2, 3), ())
        WITH_GATE = ((0,), (1,), (), (2, 3))

        def attention_splits(u):
            g = 12 + u // 4
            c = GATE_CHUNKS[g // 4]
            if g % 4 == 3:
                return [(after(c), 2 + u % 4 - 1)] if u % 4 in (1, 2) else []
            return [(after(c), g % 4)] if u % 4 == 3 and g % 4 < 2 else []

        def final_splits(j):
            c = CH_WB0 if j < 4 else CH_WB1
            return [(after(c), k) for k in FOLLOW[j % 4]]

        def gate_tile(j, b):
            return gates[:, 4 * b + j, :] if j < 4 else gates_b[:, 4 * b + j - 4, :]

        def piece_view(t, c, n_rows=2):
            n = CHUNKS[c][2]
            return t[:, 0:n_rows * n].rearrange("p (k n) -> p k n", k=n_rows)

        block = ctx.enter_context(nc.Block())

        @block.sync
        def _(sp):
            for t in range(NT):
                sp.dma_start(x_in[t], x[0, t * P:(t + 1) * P, :]).then_inc(x_loaded[t], 16)

            def load(n):
                c, j, k = pieces[n]
                src, c0, width = CHUNKS[c]
                if n >= STAGES:
                    pc, _, pk = pieces[n - STAGES]
                    sp.wait_ge(phi_used if CHUNKS[pc][0] == "phi" else lo_ready, pk + 1)
                if src == "phi":
                    dst = piece_view(stage[:, n % STAGES, :], c, 4)
                    ap = c_phi_w1[0, c0].rearrange("(k p) n -> p k n", p=P)[:, 4 * j:4 * j + 4, :]
                else:
                    dst = piece_view(stage[:, n % STAGES, :], c)
                    ap = {"w_in": w_in, "w_branch": w_branch, "w_out": w_out}[src][0].rearrange(
                        "(k p) n -> p k n", p=P)[:, 2 * j:2 * j + 2, c0:c0 + width]
                sp.dma_start(dst, ap).then_inc(w_loaded[n % STAGES], 16)

            for n in range(piece_at[CH_WO0, 0]):
                h = n - piece_at[CH_C1, 3]
                if 0 <= h < N_HEADS:
                    sp.wait_ge(rows_ready, 1)
                    sp.dma_start(rel_rows[h], rel_row[h:h + 1, :].unsqueeze(1).to_broadcast([1, P, S_REL])).then_inc(row_stored, 16)
                h -= N_HEADS + 2
                if 0 <= h < N_HEADS:
                    sp.wait_ge(row_stored, 16 * N_HEADS)
                    sp.dma_start(strips[:, h, :], bass.AP(rel_rows.tensor, P * S_REL * h + P - 1, [[S_REL - 1, P], [1, T]])).then_inc(strips_loaded, 16)
                if n == piece_at[CH_A0, 2]:
                    sp.dma_start(mask_halves, masks).then_inc(masks_loaded, 16)
                load(n)
            sp.wait_ge(y_ready, NT * 2)
            sp.dma_start(x_again, x[0].rearrange("(t p) d -> p t d", p=P)).then_inc(x_reloaded, 16)
            for n in range(piece_at[CH_WO0, 0], len(pieces)):
                load(n)
            for n in range(2):
                for t in range(NT):
                    sp.wait_ge(out_ready, NT * n + t + 1)
                    sp.dma_start(out[0, t * P:(t + 1) * P, 512 * n:512 * n + 512],
                                 x_again[:, t, 512 * n:512 * n + 512]).then_inc(out_stored, 16)
            sp.wait_ge(out_stored, 16 * 2 * NT)

        @block.gpsimd
        def _(gp):
            step = [0]

            def hold(ins):
                step[0] += 1
                ins.then_inc(p_step, 1)
                gp.wait_ge(p_step, step[0])

            gp.memset(ones[:, :], 1.0).then_inc(fills, 1)
            gp.memset(cmp_strip[:, :, :, :], NEG).then_inc(fills, 1)
            def lo_split(c, j):
                k = pair_at[c, j]
                gp.wait_ge(hi_ready, k + 1)
                gp.tensor_tensor(piece_view(w_lo[:, k % PAIRS, :], c), piece_view(stage[:, piece_at[c, j] % STAGES, :], c),
                                 piece_view(w_hi[:, k % PAIRS, :], c), ALU.subtract).then_inc(lo_ready, 1)

            def follow(c, t):
                for j in FOLLOW[t]:
                    lo_split(after(c), j)

            gp.wait_ge(fills, 2)
            hold(gp.memset(work[N_BUCKETS:N_BUCKETS + 1, 1280:1280 + N_HEADS], NEG))
            gp.nop().then_inc(hot_ready, 1)
            for j in range(4):
                lo_split(CH_C0, j)
            gp.wait_ge(h_lo_ready, 2 * NT)
            gp.memset(qkvT[:, :, 0:3], 0.0).then_inc(fills, 1)
            for t in range(4):
                follow(CH_C0, t)
            gp.wait_ge(s_drained, S.filled(("C0", 3)))
            sq_c = squares[:, 0:1280].rearrange("p (t g d) -> p t g d", t=NT, d=64)
            gp.tensor_tensor(sq_c[:, :, 0:4, :], raw_c0[:, :, 0:256].rearrange("p t (g d) -> p t g d", d=64),
                             raw_c0[:, :, 0:256].rearrange("p t (g d) -> p t g d", d=64), ALU.mult)
            gp.tensor_tensor(sq_c[:, :, 4, :], raw_c0[:, :, 384:448], raw_c0[:, :, 384:448], ALU.mult).then_inc(SQ.sem, 1)
            for t in range(4):
                follow(CH_C1, t)
            gp.wait_ge(s_drained, S.filled(("C1", 3)))
            sq_w = squares[:, 1280:1536].rearrange("p (t d) -> p t d", t=NT)
            gp.tensor_tensor(sq_w, raw_c1[:, :, 64:128], raw_c1[:, :, 64:128], ALU.mult).then_inc(SQ.sem, 1)
            for t in range(4):
                follow(CH_A0, t)
            gp.wait_ge(s_drained, S.filled(("A0", 3)))
            gp.wait_ge(v_filled, V.filled("kwT"))
            gp.tensor_tensor(squares[:, 0:1536], work[:, 0:1536], work[:, 0:1536], ALU.mult).then_inc(SQ.sem, 1)
            for t in range(4):
                follow(CH_QI, t)
            gp.wait_ge(v_drained, V.filled(("ukv", 3)))
            kf = work[:, 4608:5632]
            gp.tensor_tensor(squares[:, 0:1024], kf, kf, ALU.mult).then_inc(SQ.sem, 1)
            for c in (CH_A2, CH_B0):
                for t in range(4):
                    follow(c, t)
                if c == CH_A2:
                    gp.wait_ge(masks_loaded, 16)
                    hold(gp.tensor_copy(level_masks[:, :, :], mask_halves))
            for q in range(1, NT):
                gp.wait_ge(score_ready, q)
                d = scores[q - 1][:, P * q:P * q + P]
                gp.affine_select(out=d, in_=d, compare_op=ALU.is_ge, fill=NEG, base=0, pattern=[[-1, P]],
                                 channel_multiplier=1).then_inc(diag_ready, 1)
            def cumulative_input(c):
                if c == 0:
                    gp.wait_ge(gsum_ready, 1)
                else:
                    gp.wait_ge(v_filled, V.filled(("gc", c - 1)))
                gp.tensor_tensor(g_tri, over_heads(tri), heads(g_t, c), ALU.mult).then_inc(gtri_ready, 1)

            def reset(t):
                gp.tensor_copy(t, over_heads(ident)).then_inc(eye_ready, 1)

            def masked_decays(c):
                gp.wait_ge(exp_ready, c + 1)
                hold(gp.tensor_tensor(decay_k, decay, over_heads(tri), ALU.mult))
                gp.tensor_tensor(decay_n, decay_k, heads(n_s, c), ALU.mult).then_inc(decays_ready, 1)
                if c > 1:
                    gp.wait_ge(v_filled, V.filled(("o", c - 2)))
                gp.tensor_tensor(attnT[c % 2], decay_k, heads(rk, c), ALU.mult).then_inc(decays_ready, 1)

            def squares_b(m):
                gp.wait_ge(conv_done, m + 1)
                if m >= 4:
                    gp.wait_ge(sums_taken, m - 3)
                gp.tensor_tensor(squares[:, 512 * (m % 4):512 * (m % 4) + 512], qkvT[:, m, 3:T + 3], qkvT[:, m, 3:T + 3],
                                 ALU.mult).then_inc(SQ.sem, 1)

            for c in (CH_B1, CH_B3, CH_B4):
                for t in range(4):
                    follow(c, t)
                if c == CH_B1:
                    for m in range(4):
                        squares_b(m)
            gp.wait_ge(strips_loaded, 16 * N_HEADS)
            for q in range(NT):
                n = min(N_CMP, 7 + 8 * q)
                first = 415 - P * q
                ins = gp.tensor_copy(cmp_strip[:, :, q, 0:n], strips[:, A_HEADS:, first:first + 16 * (n - 1) + 1:16])
            ins.then_inc(cmp_strip_ready, 1)
            for m in range(4, 8):
                squares_b(m)
            cumulative_input(0)
            reset(t_inv)
            reset(t_invT)
            follow(CH_B2, 0)
            masked_decays(0)
            follow(CH_B2, 1)
            follow(CH_B2, 2)
            def scaled_output(c):
                GD.wait(gp, ("oraw", c))
                hold(gp.tensor_tensor(o_tok, o_tok, heads(rqs, c), ALU.mult))
                gp.tensor_tensor(o_sq, o_tok, o_tok, ALU.mult).then_inc(SQ.sem, 1)

            def gated_output(c):
                gp.wait_ge(o_scaled, c + 1)
                gp.wait_ge(z_ready, 1)
                zb = raw_b[:, c, 8:520].rearrange("p (h d) -> p h d", h=4)
                gp.tensor_tensor(zb, zb, o_tok, ALU.mult).then_inc(y_b, 1)

            split_gates = set()

            def gate_splits(g):
                if g not in split_gates:
                    split_gates.add(g)
                    for j in WITH_GATE[g % 4]:
                        lo_split(after(GATE_CHUNKS[g // 4]), j)

            for c in range(NT):
                if c < NT - 1:
                    cumulative_input(c + 1)
                if c == 1:
                    gate_splits(3)
                if c < NT - 1:
                    masked_decays(c + 1)
                if c > 0:
                    gated_output(c - 1)
                gate_splits(3 * c)
                gate_splits(3 * c + 1)
                if c < NT - 1:
                    GD.wait(gp, ("z", c, LEVELS - 1))
                    reset(t_inv)
                    GD.wait(gp, ("tt", c, LEVELS - 1))
                    gp.wait_ge(v_filled, V.filled(("x2", c)))
                    reset(t_invT)
                gate_splits(3 * c + 2)
                scaled_output(c)
            gated_output(NT - 1)
            def join(u):
                m, q, h = units[u]
                if u == 4:
                    gp.wait_ge(y_b, NT)
                elif u >= 6:
                    gp.wait_ge(logits_ready, u - 1)
                L = P * (q + 1)
                gp.tensor_tensor(bias_sel[u % 2][:, 0:L], strips[:, h, T - L:T], keep_add[q - 1], ALU.add).then_inc(bias_ready, 1)

            def gate_z(g):
                m, q = groups[g]
                z = raw_a2[:, q, 72:328] if m == "A" else raw_c1[:, q, 204:460]
                if m != "sel":
                    gp.wait_ge(o_norm, g + 1)
                    gp.tensor_tensor(z, z, o_c[:, q, :], ALU.mult).then_inc(y_ready, 1)

            join(4)
            join(5)
            for u in range(len(units)):
                if u >= 4 and u + 2 < 16:
                    join(u + 2)
                for c, j in attention_splits(u):
                    lo_split(c, j)
                if u % 4 == 3 and u >= 7:
                    gate_z(u // 4 - 1)
            gate_z(len(groups) - 1)
            for j in range(KC):
                for c, k in final_splits(j):
                    lo_split(c, k)
            for t in range(4):
                follow(CH_WO0, t)

        @block.scalar
        def _(act):
            def twice(row):
                return row.unsqueeze(1).to_broadcast([row.shape[0], 2, 64])

            def halves(row, n):
                return par_rows[row:row + n, :].rearrange("r (a d) -> r a d", a=2)

            act.dma_start(consts[:, :], floats[:, 0:F_HOT]).then_inc(ident_loaded, 16)
            for src, dst in (
                (norm_g[0].rearrange("(k p) -> k p", p=P), par_rows[R_NORM:R_NORM + 8, :]),
                (b_conv[0].rearrange("w (m p) -> (w m) p", p=P), par_rows[R_CONV:R_CONV + 48, :]),
                (a_kv_norm, par_rows[R_CKV:R_CKV + 1, :]),
                (twice(a_q_norm), halves(R_AQ, 1)), (twice(a_k_norm), halves(R_AK, 1)), (twice(c_q_norm), halves(R_CQ, 1)),
                (twice(c_k_norm[0]), halves(R_CK, 3)),
                (b_out_norm, par_rows[R_BOUT:R_BOUT + 1, :]),
                (c_cmp_pos[0].rearrange("v (c a) d -> (v c) (a d)", a=2), par_rows[R_POS:R_POS + 32, :]),
            ):
                act.dma_start(dst, src).then_inc(in_loaded, 16)
            for src, dst in (
                (floats[:, F_HOT:N_FLOAT], hot),
                (rel_bias, rel33[0:N_BUCKETS, :]),
                (b_dt_bias.to_broadcast([P, 4]), dt_b), (b_a_log.to_broadcast([P, 4]), neg_exp_a),
                (c_phi_w2[0].rearrange("v (k p) n -> p (v k) n", p=P), phi2),
            ):
                act.dma_start(dst, src).then_inc(const_loaded, 16)
            act.dma_start(ukv, a_w_ukv[0]).then_inc(ukv_loaded, 16)
            step = [0]

            def hold(ins):
                step[0] += 1
                ins.then_inc(a_step, 1)
                act.wait_ge(a_step, step[0])

            def sqrt(name, src, n):
                ROOT_IN.wait(act, name)
                nc.scalar.activation(root[0:src.shape[0], 0:n], src, ACT.Sqrt).then_inc(ROOT_OUT.sem, 1)

            def drain(name, dst, n=512, func=ACT.Copy, rows=P, scale=1.0):
                act.wait_ge(s_filled, S.filled(name))
                nc.scalar.activation(dst, S.bank(name)[0:rows, 0:n], func, scale=scale).then_inc(s_drained, 1)

            def hi_split(c, j):
                n, k = piece_at[c, j], pair_at[c, j]
                act.wait_ge(w_loaded[n % STAGES], 16 * (n // STAGES + 1))
                full = piece_view(stage[:, n % STAGES, :], c)
                nc.scalar.activation(full, full, ACT.Copy, scale=W_SCALE).then_inc(scaled, 1)
                act.wait_ge(scaled, k + 1)
                if k >= PAIRS:
                    act.wait_ge(pair_used, k - PAIRS + 1)
                    act.wait_ge(lo_ready, k - PAIRS + 1)
                nc.scalar.activation(piece_view(w_hi[:, k % PAIRS, :], c), full, ACT.Copy).then_inc(hi_ready, 1)

            def follow(c, t):
                for j in FOLLOW[t]:
                    hi_split(after(c), j)

            def drain_chunk(c, name, dst, n=512, between=None):
                for t in range(4):
                    drain((name, t), dst(t), n, scale=1.0 / W_SCALE)
                    follow(c, t)
                    if between:
                        between(t)

            def drain_gate(g, func=ACT.Sigmoid, scale=1.0 / W_SCALE):
                act.wait_ge(g_filled, G.filled(g))
                b, j = g // 4 % 3, g % 4 + 4 * (g // 12)
                nc.scalar.activation(gate_tile(j, b), G.bank(g)[:, :], func, scale=scale).then_inc(g_drained, 1)

            sqrt("x", ss_x, NT)
            def h_hi(t):
                for a in range(2):
                    if t < 2:
                        hi_split(CH_C0, 2 * t + a)
                    act.wait_ge(h_full_ready, 2 * t + a + 1)
                    nc.scalar.activation(hT_hi[:, 4 * a:4 * a + 4, t * P:(t + 1) * P], h_full[:, 4 * a:4 * a + 4, t * P:(t + 1) * P],
                                         ACT.Copy).then_inc(h_hi_ready, 1)

            for t in range(3):
                h_hi(t)
            for t in range(4):
                drain(("C0", t), raw_c0[:, t, :], 448, scale=1.0 / W_SCALE)
                follow(CH_C0, t)
                if t == 0:
                    h_hi(3)
            drain_chunk(CH_C1, "C1", lambda t: raw_c1[:, t, :], 460)
            sqrt("C0", ss_c, 20)
            sqrt("C1", ss_w, 4)
            drain_chunk(CH_A0, "A0", lambda t: raw_a0[:, t, :], 384)
            sqrt("A0", ss_a, 20)
            drain_chunk(CH_QI, "QI", lambda t: qiT[:, t, :], 384)
            drain_chunk(CH_A2, "A2", lambda t: raw_a2[:, t, :], 328)
            sqrt("Ak", ss_k, 16)
            act.wait_ge(fills, 3)
            drain_chunk(CH_B0, "B0", lambda t: qkvT[:, t, 3:T + 3])
            act.wait_ge(hid_filled, 1)
            for h in range(2):
                ins = nc.scalar.activation(hidT[:, h::2, :], banks[2 + h][:, 0:2 * N_CMP].rearrange("p (v n) -> p v n", v=2), ACT.Silu)
            ins.then_inc(hid_ready, 1)
            n = 0
            for q in range(1, NT):
                for h in range(IDX_HEADS):
                    if n >= 2:
                        act.wait_ge(relu_used, n - 1)
                    L = P * (q + 1)
                    drain(("idx", q, h), relu_buf[n % 2][:, 0:L], L, ACT.Relu)
                    n += 1
            sqrt("kc", ss_kc[0:N_CMP, :], 1)

            def silu_conv(m):
                act.wait_ge(conv_ready, m + 1)
                nc.scalar.activation(qkvT[:, m, 3:T + 3], conv_acc[:, m % 2, :], ACT.Silu).then_inc(conv_done, 1)

            def silus(t, at):
                for m in at.get(t, ()):
                    silu_conv(m)

            drain_chunk(CH_B1, "B1", lambda t: qkvT[:, 4 + t, 3:T + 3], between=lambda t: silus(t, {0: (0, 1), 1: (2, 3)}))
            drain_chunk(CH_B3, "B3", lambda t: raw_b[:, t, 0:260], 260)
            act.wait_ge(s_drained, S.filled(("B3", 3)))
            nc.scalar.activation(raw_c1[:, :, 192:204], raw_c1[:, :, 192:204], ACT.Sigmoid)
            nc.scalar.activation(beta_t.rearrange("p (c h) -> p c h", c=NT), raw_b[:, :, 4:8], ACT.Sigmoid).then_inc(GATE_OUT.sem, 1)
            drain_chunk(CH_B4, "B4", lambda t: raw_b[:, t, 260:520], 260, between=lambda t: silus(t, {0: (4, 5), 2: (6, 7)}))
            act.wait_ge(const_loaded, 16 * 5)
            nc.scalar.activation(neg_exp_a, neg_exp_a, ACT.Exp).then_inc(GATE_OUT.sem, 1)
            GATE_IN.wait(act, "g")
            hold(nc.scalar.activation(sp_b, sp_b, ACT.Exp, scale=-1.0))
            nc.scalar.activation(sp_b, sp_b, ACT.Ln, bias=1.0).then_inc(GATE_OUT.sem, 1)

            def decays_b(t):
                if t == 0:
                    sqrt("B", ss_b, 32)
                    GATE_IN.wait(act, "gc2")
                    nc.scalar.activation(egc, gc_, ACT.Exp)
                    nc.scalar.activation(egl, gl_, ACT.Exp)
                    nc.scalar.activation(ekd, kd_s, ACT.Exp).then_inc(GATE_OUT.sem, 1)
                    decay_exp(0)
                silus(t, {1: (8, 9), 3: (10, 11)})

            def decay_exp(c):
                act.wait_ge(diff_ready, c + 1)
                hold(nc.scalar.activation(decay, decay, ACT.Relu, scale=-1.0))
                nc.scalar.activation(decay, decay, ACT.Exp, scale=-1.0).then_inc(exp_ready, 1)

            drain_chunk(CH_B2, "B2", lambda t: qkvT[:, 8 + t, 3:T + 3], between=decays_b)
            split_gates = set()

            def gate_splits(g):
                if g not in split_gates:
                    split_gates.add(g)
                    for j in WITH_GATE[g % 4]:
                        hi_split(after(GATE_CHUNKS[g // 4]), j)

            for z in (raw_a2[:, :, 72:328], raw_c1[:, :, 204:460], raw_b[:, :, 8:520]):
                ins = nc.scalar.activation(z, z, ACT.Silu)
            ins.then_inc(z_ready, 1)
            for c in range(NT):
                if c > 0:
                    act.wait_ge(o_filled, O.filled(("os", c)))
                    if c > 1:
                        GD.wait(act, ("oraw", c - 1))
                    for h in range(4):
                        ins = nc.scalar.activation(o_state[:, h, :], O.bank(("os", c))[:, h * P:(h + 1) * P], ACT.Copy,
                                                   scale=egc[:, 4 * c + h:4 * c + h + 1])
                    ins.then_inc(o_drained, 1)
                    sqrt(("ob", c - 1), ss_o[:, 4 * c - 4:4 * c], 4)
                if c == 1:
                    gate_splits(3)
                if c < NT - 1:
                    decay_exp(c + 1)
                else:
                    act.wait_ge(cl_ready, 1)
                    nc.scalar.activation(cmp_p, cmp_p, ACT.Exp).then_inc(cexp_ready, 1)
                for g in range(3 * c, 3 * c + 3):
                    if g == 9:
                        act.wait_ge(keep_ready, NT - 1)
                    gate_splits(g)
                    drain_gate(g)
            for q in range(NT):
                drain(("cp", q), cmp_pT[:, 4 * q:4 * q + 4, :].rearrange("p a b -> p (a b)"), rows=N_CMP)
            sqrt(("ob", NT - 1), ss_o[:, 4 * NT - 4:4 * NT], 4)

            def exps(u):
                m, q, h = units[u]
                L = P * (q + 1)
                act.wait_ge(logits_ready, u + 1)
                nc.scalar.activation(probs[u % 2][:, 0:L], probs[u % 2][:, 0:L], ACT.Exp, bias=nmx[:, u:u + 1],
                                     accum_out=rsum[:, u:u + 1]).then_inc(probs_ready, 1)

            hold(nc.scalar.activation(bout_s, par[:, R_BOUT:R_BOUT + 1], ACT.Copy, scale=Y_SCALE))

            def y_hi(f):
                act.wait_ge(v_filled, V.filled(("yT", f)))
                nc.scalar.activation(yT_parts[:, f, 0, :], V.bank(("yT", f))[:, :], ACT.Copy,
                                     scale=bout_s if 2 <= f < 6 else Y_SCALE).then_inc(yT_hi_ready, 1)

            exps(0)
            for u, (m, q, h) in enumerate(units):
                if u + 1 < len(units):
                    exps(u + 1)
                L = P * (q + 1)
                if u >= 2:
                    act.wait_ge(pv_done, u - 1)
                drain(("pT", m, q, h), probsT[u % 2][:, 0:L], L)
                for c, j in attention_splits(u):
                    hi_split(c, j)
                if u % 4 == 3:
                    drain_gate(12 + u // 4, ACT.Exp, -1.0 / W_SCALE)
                for f in Y_EARLY.get(u, ()):
                    y_hi(f)
            y_hi(6)
            y_hi(7)
            for j in range(KC):
                act.wait_ge(sum_ready, j + 1)
                nc.scalar.activation(merged_parts[:, j, 0, :], gate_tile(j, 0), ACT.Copy, scale=Y_SCALE).then_inc(m_hi_ready, 1)
                for c, k in final_splits(j):
                    hi_split(c, k)
            for t in range(4):
                follow(CH_WO0, t)

        @block.vector
        def _(ve):
            step = [0]

            def hold(ins):
                step[0] += 1
                ins.then_inc(v_step, 1)
                ve.wait_ge(v_step, step[0])

            def filled(name):
                ve.wait_ge(v_filled, V.filled(name))
                return V.bank(name)

            def inv_root(name, ss, n, inv_n):
                ve.tensor_scalar(ss, ss, inv_n, EPS, ALU.mult, ALU.add).then_inc(ROOT_IN.sem, 1)
                return newton_root(name, ss, n)

            def newton_root(name, ss, n):
                rows = ss.shape[0]
                ROOT_OUT.wait(ve, name)
                y, w = root[0:rows, 0:n], newton[0:rows, 0:n]
                hold(ve.reciprocal(y, y))
                hold(ve.tensor_tensor(w, y, y, ALU.mult))
                hold(ve.tensor_tensor(w, w, ss, ALU.mult))
                hold(ve.tensor_scalar(w, w, -0.5, 1.5, ALU.mult, ALU.add))
                return y, w

            for t in range(NT):
                ve.wait_ge(x_loaded[t], 16)
                ve.tensor_tensor_reduce(out=late[:, D * t:D * t + D], in0=x_in[t], in1=x_in[t], scale=1.0, scalar=0.0,
                                        op0=ALU.mult, op1=ALU.add, accum_out=ss_x[:, t:t + 1]).then_inc(ssx_ready, 1)
            ve.wait_ge(ssx_ready, NT)
            y, w = inv_root("x", ss_x, NT, 1.0 / D)
            hold(ve.tensor_tensor(ss_x, y, w, ALU.mult))

            ve.tensor_copy(par[:, :], filled("par")[:, 0:N_ROWS]).then_inc(v_drained, 1)
            ve.wait_ge(v_drained, 1)

            def normalise(t):
                ve.tensor_scalar(x_in[t], x_in[t], ss_x[:, t:t + 1], None, ALU.mult).then_inc(h_ready, 1)

            def h_lo(n):
                part = (slice(0, P), slice(4 * (n % 2), 4 * (n % 2) + 4), slice(n // 2 * P, n // 2 * P + P))
                ve.wait_ge(h_hi_ready, n + 1)
                ve.tensor_tensor(hT_lo[part], h_full[part], hT_hi[part], ALU.subtract).then_inc(h_lo_ready, 1)

            normalise(0)
            for t in range(NT):
                if t < NT - 1:
                    normalise(t + 1)
                for a in range(2):
                    ps = filled(("x", t, a))[:, :].rearrange("p (k n) -> p k n", k=4)
                    ve.tensor_tensor(h_full[:, 4 * a:4 * a + 4, t * P:(t + 1) * P], ps,
                                     bc(par[:, R_NORM + 4 * a:R_NORM + 4 * a + 4], P), ALU.mult).then_inc(v_drained, 1)
                    ve.wait_ge(v_drained, V.filled(("x", t, a)))
                    ve.nop().then_inc(h_full_ready, 1)
                h_lo(2 * t)
                h_lo(2 * t + 1)
            for n in range(2):
                ps = filled(f"rel{n}")
                ve.tensor_copy(rel_row[:, 320 * n:320 * n + 320], ps[0:N_HEADS, 0:320]).then_inc(v_drained, 1)
            ve.wait_ge(v_drained, V.filled("rel1"))
            ve.nop().then_inc(rows_ready, 1)

            SQ.wait(ve, "C0")
            hold(ve.tensor_reduce(ss_c, squares[:, 0:1280].rearrange("p (g d) -> p g d", d=64), AX.X, ALU.add))
            y, w = inv_root("C0", ss_c, 20, 1.0 / 64)
            hold(ve.tensor_tensor(ss_c, y, w, ALU.mult))
            ssc = ss_c.rearrange("p (t g) -> p t g", t=NT)
            for g in range(4):
                q_g = raw_c0[:, :, 64 * g:64 * g + 64]
                ins = ve.tensor_tensor(q_g, q_g, bc(ssc[:, :, g], 64), ALU.mult)
            ins.then_inc(T_IN.sem, 1)
            dup = squares[:, 0:2048].rearrange("p (s t a d) -> p s t a d", s=4, t=NT, a=2)
            T_IN.wait(ve, "C0q")
            SQ.wait(ve, "C1")
            hold(ve.tensor_reduce(ss_w, squares[:, 1280:1536].rearrange("p (t d) -> p t d", t=NT), AX.X, ALU.add))
            y, w = inv_root("C1", ss_w, 4, 1.0 / 64)
            hold(ve.tensor_tensor(ss_w, y, w, ALU.mult))
            for s in range(2):
                for a in range(2):
                    ins = ve.tensor_copy(dup[:, s, :, a, :], raw_c0[:, :, 256 + 64 * s:320 + 64 * s])
            ins.then_inc(T_IN.sem, 1)
            for a in range(2):
                ins = ve.tensor_tensor(dup[:, 2, :, a, :], raw_c0[:, :, 384:448], bc(ssc[:, :, 4], 64), ALU.mult)
            ins.then_inc(T_IN.sem, 1)
            for a in range(2):
                ins = ve.tensor_tensor(dup[:, 3, :, a, :], raw_c1[:, :, 64:128], bc(ss_w, 64), ALU.mult)
            ins.then_inc(T_IN.sem, 1)
            for m in range(2):
                ve.tensor_scalar(qT_c[:, m, :], filled(f"cqT{m}")[:, :], par[:, R_CQ:R_CQ + 1], C_HD ** -0.5,
                                 ALU.mult, ALU.mult).then_inc(v_drained, 1)
            for v, name in enumerate(("kcmp", "vcmp")):
                ps = filled(name)[:, :].rearrange("p (m q) -> p m q", q=16)
                for a in range(2):
                    for half in range(2):
                        src = ps[64 * a:64 * a + 64, half:half + N_CMP, a:16:2].rearrange("p m q -> p q m")
                        pos = par[64 * a:64 * a + 64, R_POS + 16 * v + 8 * half:R_POS + 16 * v + 8 * half + 8]
                        ins = ve.tensor_tensor(blocks[64 * a:64 * a + 64, v, 8 * half:8 * half + 8, :], src,
                                               bc(pos, N_CMP), ALU.add)
                ins.then_inc(v_drained, 1)
            ve.tensor_scalar(kT_sel[:, :], filled("ksT")[:, :], par[:, R_CK + 1:R_CK + 2], None, ALU.mult).then_inc(v_drained, 1)
            ve.tensor_scalar(kT_win[:, :], filled("kwT")[:, :], par[:, R_CK + 2:R_CK + 3], None, ALU.mult).then_inc(v_drained, 1)

            SQ.wait(ve, "A0")
            sq = squares[:, 0:1536].rearrange("p (t n) -> p t n", t=NT)
            ssq = ss_a.rearrange("p (t g) -> p t g", t=NT)
            ve.tensor_reduce(ssq[:, :, 0:4], sq[:, :, 0:256].rearrange("p t (g d) -> p t g d", d=64), AX.X, ALU.add)
            hold(ve.tensor_reduce(ssq[:, :, 4], sq[:, :, 256:384], AX.X, ALU.add))
            hold(ve.tensor_scalar(ssq[:, :, 4], ssq[:, :, 4], 0.5, None, ALU.mult))
            y, w = inv_root("A0", ss_a, 20, 1.0 / 64)
            hold(ve.tensor_tensor(ss_a, y, w, ALU.mult))
            ckv = raw_a0[:, :, 256:384]
            ve.tensor_tensor(ckv, ckv, bc(ssq[:, :, 4], P), ALU.mult).then_inc(T_IN.sem, 1)
            for g in range(4):
                q_g = raw_a0[:, :, 64 * g:64 * g + 64]
                ins = ve.tensor_tensor(q_g, q_g, bc(ssq[:, :, g], 64), ALU.mult)
            ins.then_inc(T_IN.sem, 1)
            ve.tensor_scalar(ckvT, filled("ckvT")[:, :], par[:, R_CKV:R_CKV + 1], None, ALU.mult).then_inc(v_drained, 1)
            for m in range(2):
                ve.tensor_scalar(qT_a[:, m, :], filled(f"qT{m}")[:, :], par[:, R_AQ:R_AQ + 1], A_HD ** -0.5,
                                 ALU.mult, ALU.mult).then_inc(v_drained, 1)
            ve.wait_ge(row_stored, 16 * N_HEADS)
            for t in range(NT):
                ps = filled(("ukv", t))
                ve.tensor_copy(k_raw[:, t, :], ps[:, 0:256])
                ve.tensor_copy(v_a[:, t, :], ps[:, 256:512]).then_inc(v_drained, 1)
            SQ.wait(ve, "Ak")
            hold(ve.tensor_reduce(ss_k, squares[:, 0:1024].rearrange("p (g d) -> p g d", d=64), AX.X, ALU.add))
            y, w = inv_root("Ak", ss_k, 16, 1.0 / 64)
            hold(ve.tensor_tensor(ss_k, y, w, ALU.mult))
            kf = work[:, 4608:5632].rearrange("p (g d) -> p g d", d=64)
            ve.tensor_tensor(kf, kf, bc(ss_k, 64), ALU.mult).then_inc(T_IN.sem, 1)
            ve.wait_ge(s_drained, S.filled(("A2", 3)))
            ki2 = squares[:, 1024:1536].rearrange("p (t a d) -> p t a d", t=NT, a=2)
            for a in range(2):
                ins = ve.tensor_copy(ki2[:, :, a, :], raw_a2[:, :, 0:64])
            ins.then_inc(T_IN.sem, 1)
            hold(ve.tensor_scalar(raw_a2[:, :, 64:72], raw_a2[:, :, 64:72], IDX_HEADS ** -0.5, 64 ** -0.5, ALU.mult, ALU.mult))
            for m in range(2):
                ve.tensor_scalar(kT_a[:, m, :], filled(f"kT{m}")[:, :], par[:, R_AK:R_AK + 1], None, ALU.mult).then_inc(v_drained, 1)
            ve.tensor_copy(kiT, filled("kiT")[:, :]).then_inc(v_drained, 1)
            ve.wait_ge(v_drained, V.filled("kiT"))
            n = 0
            for q in range(1, NT):
                L = P * (q + 1)
                for h in range(IDX_HEADS):
                    ve.wait_ge(s_drained, S.filled(("idx", q, h)))
                    r, wi = relu_buf[n % 2][:, 0:L], raw_a2[:, q, 64 + h:65 + h]
                    if h == 0:
                        ins = ve.tensor_scalar(scores[q - 1], r, wi, None, ALU.mult)
                    else:
                        ins = ve.scalar_tensor_tensor(scores[q - 1], r, wi, scores[q - 1], ALU.mult, ALU.add)
                    n += 1
                    ins.then_inc(relu_used, 1)
                    ve.wait_ge(relu_used, n)
                ve.nop().then_inc(score_ready, 1)

            def conv(m):
                name = (("B0", "B1", "B2")[m // 4], m % 4)
                ve.wait_ge(s_drained, S.filled(name))
                if m >= 2:
                    ve.wait_ge(conv_done, m - 1)
                acc = conv_acc[:, m % 2, :]
                tap = [par[:, R_CONV + 12 * w + m:R_CONV + 12 * w + m + 1] for w in range(4)]
                hold(ve.tensor_scalar(acc, qkvT[:, m, 0:T], tap[0], None, ALU.mult))
                for w in range(1, 4):
                    ins = ve.scalar_tensor_tensor(acc, qkvT[:, m, w:w + T], tap[w], acc, ALU.mult, ALU.add)
                    if w < 3:
                        hold(ins)
                ins.then_inc(conv_ready, 1)

            ps = filled("cmpkv")
            kc, vc, kc2 = raw_c0[0:N_CMP, 1, 0:64], cmp_v[:, :], raw_c0[0:N_CMP, 1, 64:128]
            ve.tensor_copy(kc, ps[0:N_CMP, 0:64])
            ve.tensor_copy(vc, ps[0:N_CMP, 64:128]).then_inc(v_drained, 1)
            ve.wait_ge(v_drained, V.filled("cmpkv"))
            hold(ve.tensor_tensor(kc2, kc, kc, ALU.mult))
            s = ss_kc[0:N_CMP, :]
            hold(ve.tensor_reduce(s, kc2, AX.X, ALU.add))
            y, w = inv_root("kc", s, 1, 1.0 / 64)
            hold(ve.tensor_tensor(s, y, w, ALU.mult))
            kdup = raw_c0[0:N_CMP, 0, 0:128]
            for a in range(2):
                ins = ve.tensor_scalar(kdup[:, 64 * a:64 * a + 64], kc, s, None, ALU.mult)
            ins.then_inc(T_IN.sem, 1)
            def topk(q):
                ve.wait_ge(diag_ready, q)
                src = scores[q - 1]
                for r in range(TOPK // 8):
                    m8 = max8[:, 8 * (r % 2):8 * (r % 2) + 8]
                    hold(ve.max(m8, src))
                    yield
                    dst = topk_work[r % 2][:, 0:P * (q + 1)]
                    hold(ve.match_replace(dst, m8, src, TAKEN))
                    src = dst
                    if r < TOPK // 8 - 1:
                        yield
                hold(ve.tensor_scalar(src, src, TAKEN, -NEG, ALU.is_equal, ALU.mult))
                ve.tensor_scalar(keep_add[q - 1], src, NEG, None, ALU.add).then_inc(keep_ready, 1)
                yield

            for m in range(4):
                conv(m)
            for _ in topk(1):
                pass
            ve.tensor_scalar(kcT[:, 0:N_CMP], filled("kcT")[:, 0:N_CMP], par[:, R_CK:R_CK + 1], None, ALU.mult).then_inc(v_drained, 1)
            for m in range(4, 8):
                conv(m)

            def topk_later():
                yield from topk(2)
                yield from topk(3)

            topk_last = topk_later()

            ve.wait_ge(const_loaded, 16 * 5)
            sa = sp_a.rearrange("p (c h) -> p c h", c=NT)
            hold(ve.tensor_tensor(sa, raw_b[:, :, 0:4], dt_b.unsqueeze(1).to_broadcast([P, NT, 4]), ALU.add))
            hold(ve.scalar_tensor_tensor(sp_b, sp_a, -1.0, sp_a, ALU.mult, ALU.max))
            hold(ve.tensor_scalar(sp_a, sp_a, 0.0, None, ALU.max))
            ve.nop().then_inc(GATE_IN.sem, 1)
            for _ in range(TOPK_A):
                next(topk_last)
            GATE_OUT.wait(ve, "sp")
            hold(ve.tensor_tensor(sp_a, sp_a, sp_b, ALU.add))
            gt = g_t.rearrange("p (c h) -> p c h", c=NT)
            hold(ve.tensor_tensor(gt, sa, neg_exp_a.unsqueeze(1).to_broadcast([P, NT, 4]), ALU.mult))
            hold(ve.tensor_scalar(g_t, g_t, -1.0, None, ALU.mult))
            ve.nop().then_inc(gsum_ready, 1)
            for _ in range(TOPK_B):
                next(topk_last)
            ps = filled("sums")
            ve.tensor_copy(sums_sb, ps[:, 0:64]).then_inc(v_drained, 1)
            ve.wait_ge(v_drained, V.filled("sums"))
            ve.tensor_copy(ss_b, sums_sb[:, 32:64])
            ve.tensor_copy(gc_, sums_sb[:, 0:16])
            ve.tensor_copy(gl_, sums_sb[:, 16:32])
            hold(ve.tensor_tensor(kd_s, sums_sb[:, 16:32], sums_sb[:, 0:16], ALU.subtract))
            y, w = inv_root("B", ss_b, 32, 1.0)
            hold(ve.tensor_tensor(y, y, w, ALU.mult))
            hold(ve.tensor_scalar(rqs, y[:, 0:16], B_HD ** -0.5, None, ALU.mult))
            hold(ve.tensor_copy(rk, y[:, 16:32]))
            hold(ve.tensor_tensor(nk, ss_b[:, 16:32], rk, ALU.mult))
            hold(ve.tensor_tensor(a_s, beta_t, rk, ALU.mult))
            hold(ve.tensor_tensor(n_s, a_s, rk, ALU.mult))
            hold(ve.tensor_scalar(n_s, n_s, -1.0, None, ALU.mult))
            ve.nop().then_inc(GATE_IN.sem, 1)
            GATE_OUT.wait(ve, "exps")
            hold(ve.tensor_scalar(negegc, egc, -1.0, None, ALU.mult))
            hold(ve.tensor_tensor(kd_s, ekd, rk, ALU.mult))

            def bank4(name):
                return filled(name)[:, :].rearrange("p (h n) -> p h n", h=4)

            def done(name):
                ve.wait_ge(v_drained, V.filled(name))
                ve.nop().then_inc(GD.sem, 1)

            def difference(c):
                ps = bank4(("gc", c))
                if c > 0:
                    ve.wait_ge(decays_ready, 2 * c)
                ve.tensor_tensor(decay, ps, heads(gc_, c), ALU.subtract).then_inc(v_drained, 1)
                ve.wait_ge(v_drained, V.filled(("gc", c)))
                ve.nop().then_inc(diff_ready, 1)

            def token_major(c):
                ve.tensor_tensor(k_tok, bank4(("kt", c)), heads(kd_s, c), ALU.mult).then_inc(v_drained, 1)
                ve.tensor_tensor(v_tok, bank4(("vt", c)), heads(nk, c), ALU.mult).then_inc(v_drained, 1)
                done(("vt", c))

            def decayed_products(c):
                ve.wait_ge(decays_ready, 2 * c + 2)
                ve.tensor_tensor(neg_nT, bank4(("kk", c)), decay_n, ALU.mult).then_inc(v_drained, 1)
                done(("kk", c))
                ve.tensor_tensor(attnT[c % 2], bank4(("qk", c)), attnT[c % 2], ALU.mult).then_inc(v_drained, 1)
                done(("qk", c))

            def put(dst, n, src):
                return ve.copy_predicated(dst, level_masks[:, n, :].unsqueeze(1).to_broadcast([P, 4, P]), src)

            def level_zero(c):
                ve.wait_ge(eye_ready, 2 * c + 1)
                put(t_inv, 0, bank4(("n", c))).then_inc(v_drained, 1)
                ve.wait_ge(eye_ready, 2 * c + 2)
                hold(put(t_invT, LEVELS, neg_nT))
                done(("n", c))

            def output_norm(c):
                SQ.wait(ve, ("ob", c))
                so = ss_o[:, 4 * c:4 * c + 4]
                hold(ve.tensor_reduce(so, o_sq, AX.X, ALU.add))
                ve.tensor_scalar(so, so, 1.0 / B_HD, EPS, ALU.mult, ALU.add).then_inc(ROOT_IN.sem, 1)
                yield
                y, w = newton_root(("ob", c), so, 4)
                yield
                hold(ve.tensor_tensor(so, y, w, ALU.mult))
                ve.tensor_tensor(o_tok, o_tok, bc(so, P), ALU.mult).then_inc(o_scaled, 1)
                yield

            cpg = cmp_p.rearrange("p (g n) -> p g n", g=16)
            gate = raw_c1[:, :, 192:204].rearrange("p t (h k) -> p t h k", k=3)

            def compressed_softmax():
                cpv = cmp_p.rearrange("p (q h n) -> p q h n", q=NT, h=C_HEADS)
                ve.wait_ge(cmp_strip_ready, 1)
                for a in range(2):
                    ps = filled(f"cl{a}")[:, 0:248].rearrange("p (q h n) -> p q h n", q=NT, h=2)
                    ve.tensor_tensor(cpv[:, :, a::2, :], ps, cmp_strip[:, a::2, :, :].rearrange("p h q n -> p q h n"),
                                     ALU.add).then_inc(v_drained, 1)
                ve.wait_ge(v_drained, V.filled("cl1"))
                hold(ve.tensor_reduce(cmx, cpg, AX.X, ALU.max))
                ve.tensor_tensor(cpg, cpg, bc(cmx, N_CMP), ALU.subtract).then_inc(cl_ready, 1)
                yield
                ve.wait_ge(cexp_ready, 1)
                hold(ve.tensor_reduce(crs, cpg, AX.X, ALU.add))
                hold(ve.reciprocal(crs, crs))
                yield
                crq = crs.rearrange("p (q h) -> p q h", q=NT)
                hold(ve.tensor_scalar(crq[:, 0, :], crq[:, 0, :], seen[:, 0:1], None, ALU.mult))
                hold(ve.tensor_tensor(crq, crq, gate[:, :, :, 0], ALU.mult))
                yield

            difference(0)
            conv(8)
            conv(9)
            decayed_products(0)
            conv(10)
            level_zero(0)
            conv(11)
            for c in range(NT):
                norm = output_norm(c - 1) if c else iter(())
                softmax = compressed_softmax() if c == NT - 1 else iter(())
                extras = chain(norm, softmax)

                def between_steps(l, late_in_level=False):
                    if l < 3 or next(extras, "end") == "end":
                        next(topk_last, None)
                        if not late_in_level:
                            next(topk_last, None)

                for l in range(1, LEVELS):
                    ve.tensor_copy(z_sb, bank4(("z", c, l))).then_inc(v_drained, 1)
                    done(("z", c, l))
                    between_steps(l)
                    if l < LEVELS - 1:
                        put(t_inv, l, bank4(("u", c, l))).then_inc(v_drained, 1)
                        done(("u", c, l))
                    put(t_invT, LEVELS + l, bank4(("ut", c, l))).then_inc(v_drained, 1)
                    done(("ut", c, l))
                    if l == 1 and c:
                        ps = bank4(("ks", c))
                        for h in range(4):
                            ins = ve.scalar_tensor_tensor(resid[:, h, :], ps[:, h, :], negegc[:, 4 * c + h:4 * c + h + 1],
                                                          v_tok[:, h, :], ALU.mult, ALU.add)
                        ins.then_inc(v_drained, 1)
                        done(("ks", c))
                        next(norm)
                    if l == 2:
                        if c < NT - 1:
                            difference(c + 1)
                        else:
                            next(softmax)
                    if l == 3 and c == 0:
                        token_major(0)
                    if l < LEVELS - 1:
                        between_steps(l, late_in_level=True)
                if c < NT - 1:
                    decayed_products(c + 1)
                else:
                    for _ in topk_last:
                        pass
                ve.tensor_tensor(v_new, bank4(("x2", c)), heads(a_s, c), ALU.mult).then_inc(v_drained, 1)
                done(("x2", c))
                if c < NT - 1:
                    level_zero(c + 1)
                ps = bank4(("o", c))
                if c == 0:
                    ve.tensor_copy(o_tok, ps).then_inc(v_drained, 1)
                else:
                    ve.wait_ge(o_drained, O.filled(("os", c)))
                    ve.wait_ge(y_b, c)
                    ve.tensor_tensor(o_tok, ps, o_state, ALU.add).then_inc(v_drained, 1)
                done(("o", c))
                if c < NT - 1:
                    ps = bank4(("st", c))
                    if c == 0:
                        ve.tensor_copy(state, ps).then_inc(v_drained, 1)
                    else:
                        for h in range(4):
                            ins = ve.scalar_tensor_tensor(state[:, h, :], state[:, h, :], egl[:, 4 * c + h:4 * c + h + 1],
                                                          ps[:, h, :], ALU.mult, ALU.add)
                        ins.then_inc(v_drained, 1)
                    done(("st", c))
                    token_major(c + 1)

            def cmp_out():
                for n in range(2):
                    ve.wait_ge(o_filled, O.filled(("oc", n)))
                    ps = O.bank(("oc", n))[:, :].rearrange("p (g d) -> p g d", d=64)
                    ve.tensor_tensor(o_cg[:, 8 * n:8 * n + 8, :], ps, bc(crs[:, 8 * n:8 * n + 8], 64), ALU.mult).then_inc(o_drained, 1)

            o_cg = work[:, 2560:3584].rearrange("p (g d) -> p g d", d=64)

            def logits(u):
                m, q, h = units[u]
                L = P * (q + 1)
                ps = filled(("lg", m, q, h))
                if u >= 2:
                    ve.wait_ge(s_filled, S.filled(("pT", *units[u - 2])))
                if m == "A":
                    if q:
                        ve.wait_ge(bias_ready, u - 3)
                    b = bias_sel[u % 2][:, 0:L] if q else strips[:, h, T - L:T]
                else:
                    b = strips[:, A_HEADS + h, T - L:T]
                ve.tensor_tensor_reduce(out=probs[u % 2][:, 0:L], in0=ps[:, 0:L], in1=b, scale=1.0, scalar=-3e38,
                                        op0=ALU.add, op1=ALU.max, accum_out=mx[:, u:u + 1]).then_inc(v_drained, 1)
                ve.wait_ge(v_drained, V.filled(("lg", m, q, h)))
                ve.tensor_scalar(nmx[:, u:u + 1], mx[:, u:u + 1], -1.0, None, ALU.mult).then_inc(logits_ready, 1)

            def finish(g):
                m, q = groups[g]
                ve.wait_ge(probs_ready, 4 * g + 4)
                hold(ve.reciprocal(fac, rsum[:, 4 * g:4 * g + 4]))
                if m != "A":
                    hold(ve.tensor_tensor(fac, fac, gate[:, q, :, 1 if m == "sel" else 2], ALU.mult))
                ve.wait_ge(o_filled, O.filled(("o", m, q)))
                ps = O.bank(("o", m, q))[:, 0:256].rearrange("p (h d) -> p h d", h=4)
                oc = o_c[:, q, :].rearrange("p (h d) -> p h d", h=4)
                if m == "A":
                    ve.tensor_tensor(oc, ps, bc(fac, 64), ALU.mult).then_inc(o_drained, 1)
                    ve.wait_ge(o_drained, O.filled(("o", m, q)))
                elif m == "sel":
                    ve.wait_ge(y_ready, q + 1)
                    hold(ve.tensor_copy(oc, o_cg[:, 4 * q:4 * q + 4, :]))
                if m != "A":
                    tmp = cmp_p[:, 0:256].rearrange("p (h d) -> p h d", h=4)
                    ve.tensor_tensor(tmp, ps, bc(fac, 64), ALU.mult).then_inc(o_drained, 1)
                    ve.wait_ge(o_drained, O.filled(("o", m, q)))
                    hold(ve.tensor_tensor(oc, oc, tmp, ALU.add))
                ve.nop().then_inc(o_norm, 1)

            def y_lo(f):
                ps = filled(("yT", f))
                ve.wait_ge(yT_hi_ready, Y_ORDER.index(f) + 1)
                ve.scalar_tensor_tensor(yT_parts[:, f, 1, :], ps[:, :], bout_s if 2 <= f < 6 else Y_SCALE,
                                        yT_parts[:, f, 0, :], ALU.mult, ALU.subtract).then_inc(v_drained, 1)

            def sigmoid_rest(g, quarter):
                t = gate_tile(g % 4 + 4, g // 4 % 3)[:, P * quarter:P * quarter + P]
                ve.wait_ge(g_drained, g + 1)
                hold(ve.tensor_scalar(t, t, 1.0, None, ALU.add))
                hold(ve.reciprocal(t, t))

            logits(0)
            logits(1)
            for _ in output_norm(NT - 1):
                pass
            cmp_out()
            for u in range(len(units)):
                if u + 2 < len(units):
                    logits(u + 2)
                for f in Y_EARLY.get(u, ()):
                    y_lo(f)
                if u >= 4:
                    sigmoid_rest(12 + u // 4 - 1, u % 4)
                if u % 4 == 3 and u >= 7:
                    finish(u // 4 - 1)
            finish(len(groups) - 1)

            def merged_lo(j):
                ve.wait_ge(m_hi_ready, j + 1)
                ve.scalar_tensor_tensor(merged_parts[:, j, 1, :], gate_tile(j, 0), Y_SCALE, merged_parts[:, j, 0, :],
                                        ALU.mult, ALU.subtract).then_inc(merged_ready, 1)

            for j in range(KC):
                for b in range(3):
                    g = gate_tile(j, b)
                    ins = ve.scalar_tensor_tensor(g, filled(("br", j, b))[:, :], 1.0 / (W_SCALE * Y_SCALE), g, ALU.mult, ALU.mult)
                    ins.then_inc(v_drained, 1)
                    if j == 0 and b == 1:
                        y_lo(6)
                        y_lo(7)
                    if b == 1:
                        ve.wait_ge(v_drained, V.filled(("br", j, 1)))
                        hold(ve.tensor_tensor(gate_tile(j, 0), gate_tile(j, 0), gate_tile(j, 1), ALU.add))
                ve.wait_ge(v_drained, V.filled(("br", j, 2)))
                ve.tensor_tensor(gate_tile(j, 0), gate_tile(j, 0), gate_tile(j, 2), ALU.add).then_inc(sum_ready, 1)
                if 0 < j <= 4:
                    sigmoid_rest(23, j - 1)
                if j:
                    merged_lo(j - 1)
            merged_lo(KC - 1)
            ve.wait_ge(x_reloaded, 16)
            for n in range(2):
                for t in range(NT):
                    xr = x_again[:, t, 512 * n:512 * n + 512]
                    ve.scalar_tensor_tensor(xr, filled(("wo", n, t))[:, :], 1.0 / (W_SCALE * Y_SCALE), xr, ALU.mult,
                                            ALU.add).then_inc(v_drained, 1)
                    ve.wait_ge(v_drained, V.filled(("wo", n, t)))
                    ve.nop().then_inc(out_ready, 1)

        @block.tensor
        def _(pe):
            mm = nc.tensor.matmul

            def v_bank(name):
                if V.free(name) > 0:
                    pe.wait_ge(v_drained, V.free(name))
                return V.bank(name)

            def s_bank(name):
                if S.free(name) > 0:
                    pe.wait_ge(s_drained, S.free(name))
                return S.bank(name)

            def o_bank(name):
                if O.free(name) > 0:
                    pe.wait_ge(o_drained, O.free(name))
                return O.bank(name)

            def part(c, k, m0, m1):
                slot_ = pair_at[c, k // 2] % PAIRS
                return tuple(piece_view(w[:, slot_, :], c)[:, k % 2, m0:m1] for w in (w_hi, w_lo))

            def ready_pair(c, k):
                if k % 2 == 0:
                    pe.wait_ge(lo_ready, pair_at[c, k // 2] + 1)

            def product(ps, lhs, rhs, start, stop):
                mm(ps, lhs[0], rhs[0], start=start, stop=False)
                mm(ps, lhs[0], rhs[1], start=False, stop=False)
                return mm(ps, lhs[1], rhs[0], start=False, stop=stop)

            def project(c, name, token_major, first=0, between=None, within=None):
                n = CHUNKS[c][2]
                for t in range(4):
                    ps = s_bank((name, t))
                    for k in range(KC):
                        if t == 0:
                            ready_pair(c, k)
                        if token_major:
                            ins = product(ps[:, 0:n], [h[:, k, t * P:(t + 1) * P] for h in (hT_hi, hT_lo)],
                                          part(c, k, 0, n), k == 0, k == KC - 1)
                        else:
                            ins = product(ps[:, 0:T - first], part(c, k, t * P, (t + 1) * P),
                                          [h[:, k, first:T] for h in (hT_hi, hT_lo)], k == 0, k == KC - 1)
                        if t == 3 and k % 2 and k < KC - 1:
                            ins.then_inc(pair_used, 1)
                        if within and k < KC - 1:
                            within(t, k)
                    ins.then_inc(s_filled, 1)
                    if t == 3:
                        release(s_filled, S.filled((name, 3)))
                    if between:
                        between(t)

            def release(filled, n):
                pe.wait_ge(filled, n)
                pe.nop().then_inc(pair_used, 1)

            def transposes(name, sources, rows=P, cols_=P):
                ps = v_bank(name)
                for n, src in enumerate(sources):
                    ins = nc.tensor.transpose(ps[0:cols_, n * rows:n * rows + rows], src, ident[0:rows, 0:rows])
                ins.then_inc(v_filled, 1)

            pe.wait_ge(ident_loaded, 16)
            pe.wait_ge(in_loaded, 16 * 9)
            transposes("par", [par_rows], N_ROWS)
            def x_transposes(t):
                pe.wait_ge(h_ready, t + 1)
                for a in range(2):
                    transposes(("x", t, a), [x_in[t][:, (4 * a + k) * P:(4 * a + k + 1) * P] for k in range(4)])

            def between_c0(t):
                if t < 2:
                    x_transposes(t + 2)
                if t == 2:
                    pe.wait_ge(hot_ready, 1)
                    pe.wait_ge(const_loaded, 16 * 5)
                    for n in range(2):
                        ps = v_bank(f"rel{n}")
                        mm(ps[0:N_HEADS, 0:320], rel33, hot[0:N_BUCKETS + 1, 320 * n:320 * n + 320], start=True, stop=True).then_inc(v_filled, 1)
                if t < 3:
                    pe.wait_ge(h_lo_ready, 2 * t + 4)

            x_transposes(0)
            x_transposes(1)
            pe.wait_ge(h_lo_ready, 2)
            hid = banks[2:4]

            def phi(v, j):
                n = piece_at[CH_PK + v, j]
                if j == 0:
                    pe.wait_ge(v_drained, V.filled(("kcmp", "vcmp")[v]))
                pe.wait_ge(w_loaded[n % STAGES], 16 * (n // STAGES + 1))
                w = piece_view(stage[:, n % STAGES, :], CH_PK, 4)
                for h in range(2):
                    for k in range(4):
                        ins = mm(hid[h][:, v * N_CMP:(v + 1) * N_CMP], w[:, k, h * P:(h + 1) * P], blocks[:, v, 4 * j + k, :],
                                 start=j + k == 0, stop=4 * j + k == 15)
                ins.then_inc(phi_used, 1)

            project(CH_C0, "C0", True, between=between_c0)
            project(CH_C1, "C1", True)
            project(CH_A0, "A0", True)
            T_IN.wait(pe, "C0q")
            for m in range(2):
                transposes(f"cqT{m}", [raw_c0[:, t, m * P:(m + 1) * P] for t in range(NT)])
            for n, (name, inp) in enumerate((("kcmp", "C0blk"), ("vcmp", "C0blk"), ("ksT", "C0ks"), ("kwT", "C1kw"))):
                T_IN.wait(pe, inp)
                transposes(name, [squares[:, 512 * n + P * t:512 * n + P * t + P] for t in range(NT)])

            def between_qi(t):
                if t == 2:
                    T_IN.wait(pe, "A0ckv")
                    transposes("ckvT", [raw_a0[:, i, 256:384] for i in range(NT)])
                    T_IN.wait(pe, "A0q")
                    transposes("qT0", [raw_a0[:, i, 0:P] for i in range(NT)])
                if t == 3:
                    transposes("qT1", [raw_a0[:, i, P:2 * P] for i in range(NT)])

            project(CH_QI, "QI", False, P, between=between_qi)
            pe.wait_ge(v_drained, V.filled("ckvT"))
            pe.wait_ge(ukv_loaded, 16)
            for t in range(NT):
                ps = v_bank(("ukv", t))
                mm(ps[:, :], ckvT[:, t * P:(t + 1) * P], ukv, start=True, stop=True).then_inc(v_filled, 1)
            project(CH_A2, "A2", True, between=lambda t: phi(0, t))

            def between_b0(t):
                phi(1, t)
                if t == 0:
                    T_IN.wait(pe, "Ak")
                    for m in range(2):
                        transposes(f"kT{m}", [k_raw[:, i, m * P:(m + 1) * P] for i in range(NT)])
                    T_IN.wait(pe, "Aki")
                    transposes("kiT", [squares[:, 1024 + P * i:1152 + P * i] for i in range(NT)])

            project(CH_B0, "B0", False, between=between_b0)
            pe.wait_ge(phi_used, 8)
            pe.nop().then_inc(hid_filled, 1)
            pe.wait_ge(v_drained, V.filled("kiT"))
            for q in range(1, NT):
                for h in range(IDX_HEADS):
                    L, r = P * (q + 1), 64 * (h % 2)
                    ps = s_bank(("idx", q, h))
                    mm(ps[:, 0:L], qiT[r:r + 64, h // 2, (q - 1) * P:q * P], kiT[r:r + 64, 0:L], start=True, stop=True).then_inc(s_filled, 1)
            pe.wait_ge(hid_ready, 1)
            ps = v_bank("cmpkv")
            for v in range(2):
                for h in range(2):
                    ins = mm(ps[0:N_CMP, 64 * v:64 * v + 64], hidT[:, 2 * v + h, :], phi2[:, 2 * v + h, :], start=h == 0, stop=h == 1)
            ins.then_inc(v_filled, 1)
            project(CH_B1, "B1", False)
            T_IN.wait(pe, "kc")
            transposes("kcT", [raw_c0[0:N_CMP, 0, 0:128]], N_CMP)
            project(CH_B3, "B3", True)

            def four(name, lhs, rhs, ring_=None):
                ps = v_bank(name) if ring_ is None else o_bank(name)
                for h in range(4):
                    ins = mm(ps[:, h * P:(h + 1) * P], lhs(h), rhs(h), start=True, stop=True)
                ins.then_inc(v_filled if ring_ is None else o_filled, 1)

            def features(c):
                tok = slice(3 + c * P, 3 + (c + 1) * P)
                return tuple(lambda h, m=m: qkvT[:, 4 * m + h, tok] for m in range(3))

            def cumulative(c):
                pe.wait_ge(gtri_ready, c + 1)
                ps = v_bank(("gc", c))
                mm(ps[:, :], ones[:, :], g_tri.rearrange("p h n -> p (h n)"), start=True, stop=True).then_inc(v_filled, 1)

            def token_major_inputs(c, n=0):
                qc, kc_, vc_ = features(c)
                fill(n)
                transposes(("kt", c), [kc_(h) for h in range(4)])
                fill(n)
                transposes(("vt", c), [vc_(h) for h in range(4)])

            def key_products(c):
                qc, kc_, vc_ = features(c)
                four(("kk", c), kc_, kc_)
                four(("qk", c), kc_, qc)

            def square_sums(ms):
                ps = V.bank("sums")
                for m in ms:
                    SQ.wait(pe, ("B", m))
                    for t in range(NT):
                        c0 = 32 + 16 * (m // 4) + 4 * t + m % 4
                        ins = mm(ps[:, c0:c0 + 1], squares[:, 512 * (m % 4) + t * P:512 * (m % 4) + (t + 1) * P], ones[:, 0:1],
                                 start=True, stop=True)
                    ins.then_inc(sums_taken, 1)

            def between_b4(t):
                if t == 0:
                    v_bank("sums")
                    square_sums(range(4))

            def between_b2(t):
                if t == 1:
                    pe.wait_ge(gsum_ready, 1)
                    ps = V.bank("sums")
                    mm(ps[:, 0:16], tri, g_t, start=True, stop=True)
                    mm(ps[:, 16:32], ones[:, :], g_t, start=True, stop=True).then_inc(v_filled, 1)
                    cumulative(0)
                if t == 2:
                    key_products(0)

            def within_b2(t, k):
                if t == 1 and k % 2 == 0:
                    square_sums([4 + k // 2])

            project(CH_B4, "B4", True, between=between_b4)
            project(CH_B2, "B2", False, between=between_b2, within=within_b2)

            def gate_products():
                for g in range(24):
                    c, m = GATE_CHUNKS[g // 4], g % 4 * P
                    if G.free(g) > 0:
                        pe.wait_ge(g_drained, G.free(g))
                    for k in range(KC):
                        if g % 4 == 0:
                            ready_pair(c, k)
                        w, h = part(c, k, m, m + P), (hT_hi[:, k, :], hT_lo[:, k, :])
                        mm(G.bank(g)[:, :], w[0], h[0], start=k == 0, stop=False)
                        yield
                        mm(G.bank(g)[:, :], w[0], h[1], start=False, stop=False)
                        yield
                        ins = mm(G.bank(g)[:, :], w[1], h[0], start=False, stop=k == KC - 1)
                        if k == KC - 1:
                            ins.then_inc(g_filled, 1)
                            if g % 4 == 3:
                                release(g_filled, g + 1)
                        elif g % 4 == 3 and k % 2:
                            ins.then_inc(pair_used, 1)
                        yield

            gate_steps = gate_products()

            def fill(n):
                for _ in range(n):
                    next(gate_steps)

            def compressed_logits():
                for a in range(2):
                    ps, r = v_bank(f"cl{a}"), 64 * a
                    for q in range(NT):
                        for m in range(2):
                            u = 2 * q + m
                            ins = mm(ps[:, u * N_CMP:(u + 1) * N_CMP], qT_c[r:r + 64, m, q * P:(q + 1) * P], kcT[r:r + 64, 0:N_CMP],
                                     start=True, stop=True)
                    ins.then_inc(v_filled, 1)

            fill(2 * FILL_T)
            GD.wait(pe, ("nnt", 0))
            transposes(("n", 0), [neg_nT[:, h, :] for h in range(4)])
            for c in range(NT):
                qc, kc_, vc_ = features(c)
                GD.wait(pe, ("tt0", c))
                for l in range(1, LEVELS):
                    four(("z", c, l), lambda h: neg_nT[:, h, :], lambda h: t_inv[:, h, :])
                    fill(FILL_Z)
                    GD.wait(pe, ("z", c, l))
                    if l > 1:
                        GD.wait(pe, ("tt", c, l - 1))
                    if l < LEVELS - 1:
                        four(("u", c, l), lambda h: t_invT[:, h, :], lambda h: z_sb[:, h, :])
                    four(("ut", c, l), lambda h: z_sb[:, h, :], lambda h: t_invT[:, h, :])
                    if l == 1 and c:
                        GD.wait(pe, ("state", c - 1))
                        four(("ks", c), kc_, lambda h: state[:, h, :])
                        four(("os", c), qc, lambda h: state[:, h, :], O)
                    if l == 2:
                        if c < NT - 1:
                            cumulative(c + 1)
                        else:
                            compressed_logits()
                    if l == 3 and c == 0:
                        pe.wait_ge(conv_done, 12)
                        token_major_inputs(0)
                    if l < LEVELS - 1:
                        fill(FILL_U)
                        GD.wait(pe, ("t", c, l))
                if c < NT - 1:
                    key_products(c + 1)
                else:
                    fill(FILL_N + 2 * FILL_T)
                GD.wait(pe, ("tt", c, LEVELS - 1))
                four(("x2", c), lambda h: t_invT[:, h, :], (lambda h: resid[:, h, :]) if c else (lambda h: v_tok[:, h, :]))
                fill(FILL_X)
                if c < NT - 1:
                    GD.wait(pe, ("nnt", c + 1))
                    transposes(("n", c + 1), [neg_nT[:, h, :] for h in range(4)])
                    fill(FILL_N)
                else:
                    pe.wait_ge(cexp_ready, 1)
                    for q in range(NT):
                        ps = s_bank(("cp", q))
                        for h in range(4):
                            ins = nc.tensor.transpose(ps[0:N_CMP, h * P:(h + 1) * P],
                                                      cmp_p[:, (4 * q + h) * N_CMP:(4 * q + h + 1) * N_CMP], ident)
                        ins.then_inc(s_filled, 1)
                GD.wait(pe, ("vnew", c))
                four(("o", c), lambda h: attnT[c % 2][:, h, :], lambda h: v_new[:, h, :])
                if c < NT - 1:
                    four(("st", c), lambda h: k_tok[:, h, :], lambda h: v_new[:, h, :])
                    token_major_inputs(c + 1, FILL_T if c else 0)

            def unit_logits(u):
                m, q, h = units[u]
                qT, kT = {"A": (qT_a, kT_a[:, h // 2, :]), "sel": (qT_c, kT_sel), "win": (qT_c, kT_win)}[m]
                r, L = 64 * (h % 2), P * (q + 1)
                ps = v_bank(("lg", m, q, h))
                mm(ps[:, 0:L], qT[r:r + 64, h // 2, q * P:(q + 1) * P], kT[r:r + 64, 0:L], start=True, stop=True).then_inc(v_filled, 1)

            unit_logits(0)
            unit_logits(1)
            for n in range(2):
                ps = o_bank(("oc", n))
                pe.wait_ge(s_drained, S.filled(("cp", 2 * n + 1)))
                for u in range(8):
                    ins = mm(ps[:, 64 * u:64 * u + 64], cmp_pT[:, 8 * n + u, :], cmp_v[:, :], start=True, stop=True)
                ins.then_inc(o_filled, 1)

            def unit_out(u):
                m, q, h = units[u]
                ps = O.bank(("o", m, q)) if h else o_bank(("o", m, q))
                pe.wait_ge(s_drained, S.filled(("pT", m, q, h)))
                for k in range(q + 1):
                    v = {"A": v_a[:, k, 64 * h:64 * h + 64], "sel": raw_c1[:, k, 0:64], "win": raw_c1[:, k, 128:192]}[m]
                    ins = mm(ps[:, 64 * h:64 * h + 64], probsT[u % 2][:, k * P:(k + 1) * P], v, start=k == 0, stop=k == q)
                ins.then_inc(pv_done, 1)
                if h == 3:
                    pe.wait_ge(pv_done, u + 1)
                    pe.nop().then_inc(o_filled, 1)

            def y_transposes(f):
                if 2 <= f < 6:
                    pe.wait_ge(y_b, NT)
                else:
                    pe.wait_ge(y_ready, NT if f < 2 else 2 * NT)
                raw, c0 = {0: (raw_a2, 72), 1: (raw_a2, 200), 6: (raw_c1, 204), 7: (raw_c1, 332)}.get(f, (raw_b, 8 + P * (f - 2)))
                transposes(("yT", f), [raw[:, t, c0:c0 + P] for t in range(NT)])

            for u, (m, q, h) in enumerate(units):
                pe.wait_ge(probs_ready, u + 1)
                ps = s_bank(("pT", m, q, h))
                for k in range(q + 1):
                    ins = nc.tensor.transpose(ps[:, k * P:(k + 1) * P], probs[u % 2][:, k * P:(k + 1) * P], ident)
                ins.then_inc(s_filled, 1)
                fill(ATTENTION_FILL[q] // 2)
                if u + 2 < len(units):
                    unit_logits(u + 2)
                if u >= 1:
                    unit_out(u - 1)
                for f in Y_EARLY.get(u, ()):
                    y_transposes(f)
                fill(ATTENTION_FILL[q] - ATTENTION_FILL[q] // 2)
            unit_out(len(units) - 1)

            for j in range(KC):
                c, m = (CH_WB0, CH_WB1)[j // 4], j % 4 * P
                for b, rows in enumerate(((0, 2), (2, 6), (6, 8))):
                    if j == 0:
                        if b == 2:
                            y_transposes(6)
                            y_transposes(7)
                        pe.wait_ge(v_drained, V.filled(("yT", (1, 5, 7)[b])))
                    ps = v_bank(("br", j, b))
                    for k in range(*rows):
                        if j % 4 == 0:
                            ready_pair(c, k)
                        ins = product(ps[:, :], part(c, k, m, m + P), (yT_parts[:, k, 0, :], yT_parts[:, k, 1, :]),
                                      k == rows[0], k == rows[1] - 1)
                        if j % 4 == 3 and k == 3:
                            ins.then_inc(pair_used, 1)
                    ins.then_inc(v_filled, 1)
                    if j % 4 == 3:
                        release(v_filled, V.filled(("br", j, b)))
            def out_products(n, t, ks):
                ps = V.bank(("wo", n, t)) if ks[0] else v_bank(("wo", n, t))
                for k in ks:
                    if t == 0:
                        ready_pair(CH_WO0 + n, k)
                        if n == 0:
                            pe.wait_ge(merged_ready, k + 1)
                    ins = product(ps[:, :], [merged_parts[:, k, a, t * P:(t + 1) * P] for a in range(2)],
                                  part(CH_WO0 + n, k, 0, 512), k == 0, k == KC - 1)
                    if t == 3 and k % 2 and k < KC - 1:
                        ins.then_inc(pair_used, 1)
                if k == KC - 1:
                    ins.then_inc(v_filled, 1)

            for n in range(2):
                for t, ks in [(0, range(6)), (1, range(6)), (0, range(6, KC)), (1, range(6, KC))] if n == 0 else [(0, range(KC)), (1, range(KC))]:
                    out_products(n, t, ks)
                for t in range(2, NT):
                    out_products(n, t, range(KC))
                if n == 0:
                    release(v_filled, V.filled(("wo", 0, NT - 1)))


NAMES = ["x", "norm_g", "w_in", "a_kv_norm", "a_w_ukv", "a_q_norm", "a_k_norm", "b_conv", "b_a_log", "b_dt_bias",
         "b_out_norm", "c_q_norm", "c_k_norm", "c_cmp_pos", "c_phi_w1", "c_phi_w2", "w_branch", "w_out", "rel_bias"]


def kernel(**inputs):
    import concourse.bacc as bacc
    from concourse.bass_utils import run_bass_kernel_spmd

    nc = bacc.Bacc("TRN2", target_bir_lowering=False, num_devices=1)
    floats, masks = shape_constants()
    arrays, args = {}, []
    for name, a in [(n, np.ascontiguousarray(inputs[n])) for n in NAMES] + [("floats", floats), ("masks", masks)]:
        arrays[f"in_{name}"] = a
        args.append(nc.dram_tensor(f"in_{name}", a.shape, mybir.dt.from_np(a.dtype), kind="ExternalInput").ap())
    out = nc.dram_tensor("out_x", (1, T, D), mybir.dt.float32, kind="ExternalOutput").ap()
    rel_rows = nc.dram_tensor("rel_rows", (N_HEADS, P, S_REL), mybir.dt.float32, kind="Internal").ap()
    trunk(nc, *args, out, rel_rows)
    r = run_bass_kernel_spmd(nc, [arrays], core_ids=[0])
    return r.results[0]["out_x"]
```
